# Optimizing a Trainium2 kernel written in Bass

```python
import math
import jax
import jax.numpy as jnp
from jax import lax
import numpy as np
import jax, jax.numpy as jnp

D_MODEL = 1024
BATCH = 1
SEQ = 256
DEPTH = 2

CHUNK = 64
Q_BLOCK = 128
ROPE_THETA = 500000.0
HEAD_DIM = 64

MLA_HEADS = 8
DIFF_HEADS = 4
FOX_HEADS = 4
D_MIX = (MLA_HEADS + DIFF_HEADS + FOX_HEADS) * HEAD_DIM

MLA_Q_RANK = 384
MLA_KV_RANK = 256
MLA_NOPE = 64
MLA_ROPE = 32
MLA_V = HEAD_DIM

DIFF_QK = HEAD_DIM // 2
DIFF_V = HEAD_DIM
DIFF_ROT = DIFF_QK // 4
DIFF_W = DIFF_HEADS * HEAD_DIM

FOX_W = FOX_HEADS * HEAD_DIM

IN_SPLITS = (MLA_Q_RANK, MLA_KV_RANK, MLA_ROPE,
             DIFF_W, DIFF_W, DIFF_W,
             FOX_W, FOX_W, FOX_W, FOX_HEADS)
IN_COLS = MLA_Q_RANK + MLA_KV_RANK + MLA_ROPE + 3 * DIFF_W + 3 * FOX_W + FOX_HEADS

N_EXPERTS = 16
N_GROUPS = 4
GROUP_SIZE = N_EXPERTS // N_GROUPS
TOP_K = 2
D_EXPERT = 512

DEEPNORM_ALPHA = (2 * DEPTH) ** 0.25
DEEPNORM_BETA = (8 * DEPTH) ** -0.25

LN_EPS = 1e-5
RMS_EPS = 1e-6
NEG_INF = -1e30
F32 = jnp.float32


def layer_norm(x, g, b):
    xf = x.astype(F32)
    mu = jnp.mean(xf, axis=-1, keepdims=True)
    var = jnp.mean(jnp.square(xf - mu), axis=-1, keepdims=True)
    return ((xf - mu) * lax.rsqrt(var + LN_EPS) * g.astype(F32) + b.astype(F32)).astype(x.dtype)

def rms_norm(x, g):
    xf = x.astype(F32)
    return (xf * lax.rsqrt(jnp.mean(xf * xf, axis=-1, keepdims=True) + RMS_EPS) * g.astype(F32)).astype(x.dtype)

def rope_tables(positions, rot_dim):
    inv_freq = ROPE_THETA ** (-jnp.arange(0, rot_dim, 2, dtype=F32) / rot_dim)
    ang = positions.astype(F32)[..., None] * inv_freq
    return jnp.cos(ang), jnp.sin(ang)

def apply_rope(x, cos, sin):
    xf = x.astype(F32)
    x1, x2 = jnp.split(xf, 2, axis=-1)
    c = cos[:, :, None, :]
    s = sin[:, :, None, :]
    return jnp.concatenate([x1 * c - x2 * s, x2 * c + x1 * s], axis=-1).astype(x.dtype)

def partial_rope(x, cos, sin, rot_dim):
    return jnp.concatenate([apply_rope(x[..., :rot_dim], cos, sin), x[..., rot_dim:]], axis=-1)

def q_block(a, i, axis=1):
    return lax.dynamic_slice_in_dim(a, i * Q_BLOCK, Q_BLOCK, axis)

def chunk_causal_mask(i, seq):
    q_idx = i * Q_BLOCK + jnp.arange(Q_BLOCK)
    k_idx = jnp.arange(seq)
    return (k_idx[None, :] // CHUNK) <= (q_idx[:, None] // CHUNK)

def frame_causal_mask(i, seq):
    q_idx = i * Q_BLOCK + jnp.arange(Q_BLOCK)
    k_idx = jnp.arange(seq)
    return k_idx[None, :] <= q_idx[:, None]

def sweep_query_blocks(block_fn, seq):
    out = lax.map(block_fn, jnp.arange(seq // Q_BLOCK))
    out = jnp.moveaxis(out, 0, 1)
    return out.reshape(out.shape[0], seq, out.shape[3], out.shape[4])

def mla_attention(c_q, c_kv, k_rope_raw, q_norm_g, kv_norm_g, w_uq, w_ukv, cos, sin):
    b, seq, _ = c_q.shape
    q = (rms_norm(c_q, q_norm_g) @ w_uq).reshape(b, seq, MLA_HEADS, MLA_NOPE + MLA_ROPE)
    q_nope = q[..., :MLA_NOPE]
    q_rope = apply_rope(q[..., MLA_NOPE:], cos, sin)
    kv = (rms_norm(c_kv, kv_norm_g) @ w_ukv).reshape(b, seq, MLA_HEADS, MLA_NOPE + MLA_V)
    k_nope = kv[..., :MLA_NOPE]
    v = kv[..., MLA_NOPE:]
    k_rope = apply_rope(k_rope_raw[:, :, None, :], cos, sin)[:, :, 0, :]
    scale = (MLA_NOPE + MLA_ROPE) ** -0.5

    def block(i):
        sc = (jnp.einsum('bqhd,bkhd->bhqk', q_block(q_nope, i), k_nope, preferred_element_type=F32)
              + jnp.einsum('bqhr,bkr->bhqk', q_block(q_rope, i), k_rope, preferred_element_type=F32)) * scale
        sc = jnp.where(chunk_causal_mask(i, seq), sc, NEG_INF)
        p = jax.nn.softmax(sc, axis=-1).astype(v.dtype)
        return jnp.einsum('bhqk,bkhd->bqhd', p, v)

    return sweep_query_blocks(block, seq)

def diff_attention(q, k, v, lam_q1, lam_k1, lam_q2, lam_k2, subln_g, lam_init, cos, sin):
    b, seq, _ = q.shape
    q = partial_rope(q.reshape(b, seq, 2 * DIFF_HEADS, DIFF_QK), cos, sin, DIFF_ROT)
    k = partial_rope(k.reshape(b, seq, 2 * DIFF_HEADS, DIFF_QK), cos, sin, DIFF_ROT)
    q1, q2 = q[:, :, 0::2], q[:, :, 1::2]
    k1, k2 = k[:, :, 0::2], k[:, :, 1::2]
    v = v.reshape(b, seq, DIFF_HEADS, DIFF_V)
    lam = (jnp.exp(jnp.sum(lam_q1.astype(F32) * lam_k1.astype(F32)))
           - jnp.exp(jnp.sum(lam_q2.astype(F32) * lam_k2.astype(F32))) + lam_init)
    scale = DIFF_QK ** -0.5

    def block(i):
        mask = chunk_causal_mask(i, seq)
        s1 = jnp.einsum('bqhd,bkhd->bhqk', q_block(q1, i), k1, preferred_element_type=F32) * scale
        s2 = jnp.einsum('bqhd,bkhd->bhqk', q_block(q2, i), k2, preferred_element_type=F32) * scale
        p = (jax.nn.softmax(jnp.where(mask, s1, NEG_INF), axis=-1)
             - lam * jax.nn.softmax(jnp.where(mask, s2, NEG_INF), axis=-1)).astype(v.dtype)
        return jnp.einsum('bhqk,bkhd->bqhd', p, v)

    o = sweep_query_blocks(block, seq)
    return rms_norm(o, subln_g) * (1.0 - lam_init)

def forgetting_attention(q, k, v, f_logit, f_bias):
    b, seq, _ = q.shape
    q = q.reshape(b, seq, FOX_HEADS, HEAD_DIM)
    k = k.reshape(b, seq, FOX_HEADS, HEAD_DIM)
    v = v.reshape(b, seq, FOX_HEADS, HEAD_DIM)
    log_f = jax.nn.log_sigmoid(f_logit.astype(F32) + f_bias.astype(F32))
    cum = jnp.cumsum(log_f, axis=1).transpose(0, 2, 1)
    scale = HEAD_DIM ** -0.5

    def block(i):
        sc = jnp.einsum('bqhd,bkhd->bhqk', q_block(q, i), k, preferred_element_type=F32) * scale
        sc = sc + q_block(cum, i, axis=2)[..., :, None] - cum[..., None, :]
        sc = jnp.where(frame_causal_mask(i, seq), sc, NEG_INF)
        p = jax.nn.softmax(sc, axis=-1).astype(v.dtype)
        return jnp.einsum('bhqk,bkhd->bqhd', p, v)

    return sweep_query_blocks(block, seq)

def mixer_sublayer(h, cos_m, sin_m, cos_d, sin_d, w_in, mla_q_norm_g, mla_kv_norm_g, mla_w_uq, mla_w_ukv,
                   diff_lam_q1, diff_lam_k1, diff_lam_q2, diff_lam_k2, diff_subln_g, lam_init, fox_f_bias, w_out):
    b, seq, _ = h.shape
    proj = h @ w_in
    parts = []
    start = 0
    for width in IN_SPLITS:
        parts.append(proj[..., start:start + width])
        start += width
    c_q, c_kv, k_rope, dq, dk, dv, fq, fk, fv, ff = parts
    o_mla = mla_attention(c_q, c_kv, k_rope, mla_q_norm_g, mla_kv_norm_g, mla_w_uq, mla_w_ukv, cos_m, sin_m)
    o_diff = diff_attention(dq, dk, dv, diff_lam_q1, diff_lam_k1, diff_lam_q2, diff_lam_k2,
                            diff_subln_g, lam_init, cos_d, sin_d)
    o_fox = forgetting_attention(fq, fk, fv, ff, fox_f_bias)
    o = jnp.concatenate([o_mla.reshape(b, seq, -1), o_diff.reshape(b, seq, -1),
                         o_fox.reshape(b, seq, -1)], axis=-1)
    return o @ w_out

def grouped_moe(h, router_w, router_bias, w_gate, w_up, w_down):
    n = h.shape[0]
    scores = jax.nn.sigmoid(jnp.einsum('nd,de->ne', h, router_w, preferred_element_type=F32))
    biased = (scores + router_bias.astype(F32)).reshape(n, N_GROUPS, GROUP_SIZE)
    group_score = jnp.sum(lax.top_k(biased, TOP_K)[0], axis=-1)
    group_sel = jnp.argmax(group_score, axis=-1)
    in_group = group_sel[:, None] == jnp.arange(N_GROUPS)[None, :]
    cand = jnp.where(in_group[:, :, None], biased, NEG_INF).reshape(n, N_EXPERTS)
    _, idx = lax.top_k(cand, TOP_K)
    sel = jnp.take_along_axis(scores, idx, axis=-1)
    gates = sel / jnp.sum(sel, axis=-1, keepdims=True)
    dense_gates = jnp.einsum('nk,nke->ne', gates, jax.nn.one_hot(idx, N_EXPERTS, dtype=F32)).astype(h.dtype)
    y = jnp.zeros_like(h)
    for e in range(N_EXPERTS):
        a = jax.nn.silu(h @ w_gate[e]) * (h @ w_up[e])
        y = y + dense_gates[:, e:e + 1] * (a @ w_down[e])
    return y

def first_inputs(seed: int = 0) -> dict:
    key = jax.random.key(seed)
    ks = jax.random.split(key, 24)

    def nrm(k, shape, scale):
        return jax.random.normal(k, shape, F32) * scale

    def gain(k, shape):
        return 1.0 + nrm(k, shape, 0.02)

    x = nrm(ks[0], (BATCH, SEQ, D_MODEL), 1.0)
    offsets = jax.random.randint(ks[1], (BATCH, 1), 0, 64, dtype=jnp.int32) * CHUNK
    positions = offsets + jnp.arange(SEQ, dtype=jnp.int32)[None, :]
    return {
        "x": x,
        "positions": positions,
        "ln_in_g": gain(ks[2], (D_MODEL,)),
        "ln_in_b": nrm(ks[3], (D_MODEL,), 0.02),
        "w_in": nrm(ks[4], (DEPTH, D_MODEL, IN_COLS), D_MODEL ** -0.5),
        "mla_q_norm_g": gain(ks[5], (DEPTH, MLA_Q_RANK)),
        "mla_kv_norm_g": gain(ks[6], (DEPTH, MLA_KV_RANK)),
        "mla_w_uq": nrm(ks[7], (DEPTH, MLA_Q_RANK, MLA_HEADS * (MLA_NOPE + MLA_ROPE)), MLA_Q_RANK ** -0.5),
        "mla_w_ukv": nrm(ks[8], (DEPTH, MLA_KV_RANK, MLA_HEADS * (MLA_NOPE + MLA_V)), MLA_KV_RANK ** -0.5),
        "diff_lam_q1": nrm(ks[9], (DEPTH, DIFF_QK), 0.1),
        "diff_lam_k1": nrm(ks[10], (DEPTH, DIFF_QK), 0.1),
        "diff_lam_q2": nrm(ks[11], (DEPTH, DIFF_QK), 0.1),
        "diff_lam_k2": nrm(ks[12], (DEPTH, DIFF_QK), 0.1),
        "diff_subln_g": gain(ks[13], (DEPTH, DIFF_V)),
        "fox_f_bias": jax.random.uniform(ks[14], (DEPTH, FOX_HEADS), F32, 1.0, 4.0),
        "w_out": nrm(ks[15], (DEPTH, D_MIX, D_MODEL), D_MIX ** -0.5 * DEEPNORM_BETA),
        "ln1_g": gain(ks[16], (DEPTH, D_MODEL)),
        "ln1_b": nrm(ks[17], (DEPTH, D_MODEL), 0.02),
        "router_w": nrm(ks[18], (D_MODEL, N_EXPERTS), D_MODEL ** -0.5),
        "router_bias": nrm(ks[19], (N_EXPERTS,), 0.01),
        "exp_w_gate": nrm(ks[20], (DEPTH, N_EXPERTS, D_MODEL, D_EXPERT), D_MODEL ** -0.5),
        "exp_w_up": nrm(ks[21], (DEPTH, N_EXPERTS, D_MODEL, D_EXPERT), D_MODEL ** -0.5),
        "exp_w_down": nrm(ks[22], (DEPTH, N_EXPERTS, D_EXPERT, D_MODEL), D_EXPERT ** -0.5 * DEEPNORM_BETA),
        "ln2_g": gain(ks[23], (DEPTH, D_MODEL)),
        "ln2_b": nrm(jax.random.fold_in(ks[23], 1), (DEPTH, D_MODEL), 0.02),
    }

def first_block(x, positions, ln_in_g, ln_in_b, w_in, mla_q_norm_g, mla_kv_norm_g, mla_w_uq, mla_w_ukv,
              diff_lam_q1, diff_lam_k1, diff_lam_q2, diff_lam_k2, diff_subln_g, fox_f_bias, w_out,
              ln1_g, ln1_b, router_w, router_bias, exp_w_gate, exp_w_up, exp_w_down, ln2_g, ln2_b):
    b, seq, d = x.shape
    cos_m, sin_m = rope_tables(positions, MLA_ROPE)
    cos_d, sin_d = rope_tables(positions, DIFF_ROT)
    h = layer_norm(x, ln_in_g, ln_in_b)
    for l in range(DEPTH):
        lam_init = 0.8 - 0.6 * math.exp(-0.3 * l)
        mix = mixer_sublayer(h, cos_m, sin_m, cos_d, sin_d, w_in[l], mla_q_norm_g[l], mla_kv_norm_g[l],
                             mla_w_uq[l], mla_w_ukv[l], diff_lam_q1[l], diff_lam_k1[l], diff_lam_q2[l],
                             diff_lam_k2[l], diff_subln_g[l], lam_init, fox_f_bias[l], w_out[l])
        h = layer_norm(DEEPNORM_ALPHA * h + mix, ln1_g[l], ln1_b[l])
        ffn = grouped_moe(h.reshape(b * seq, d), router_w, router_bias,
                          exp_w_gate[l], exp_w_up[l], exp_w_down[l]).reshape(b, seq, d)
        h = layer_norm(DEEPNORM_ALPHA * h + ffn, ln2_g[l], ln2_b[l])
    return h


DEPTH_2 = 1

QBLK = 128
EPS = 1e-6

REC_HEADS = 4
REC_DK = 128
REC_DV = 128
REC_W = REC_HEADS * REC_DV
ATT_HEADS = 8
ATT_DH = 64
ATT_W = ATT_HEADS * ATT_DH
IDX_HEADS = 8
IDX_DIM = 64
TOPK_MAX = 256
NUM_BUCKETS = 32
MAX_DISTANCE = 128
EXPERTS_PER_GROUP = 4
N_EXPERTS_2 = N_GROUPS * EXPERTS_PER_GROUP
TOP_K_EXPERTS = 2

MIX_W = REC_W + ATT_W
IN_SIZES = (REC_HEADS * REC_DK,
            REC_HEADS * REC_DK,
            REC_W,
            REC_W,
            ATT_W, ATT_W, ATT_W,
            IDX_HEADS * IDX_DIM,
            IDX_DIM,
            IDX_HEADS)
D_IN = int(sum(IN_SIZES))
IN_OFFSETS = tuple(int(o) for o in np.cumsum(IN_SIZES)[:-1])


def _rms(x, g):
    xf = x.astype(jnp.float32)
    y = xf * lax.rsqrt(jnp.mean(xf * xf, axis=-1, keepdims=True) + EPS)
    return (y * g.astype(jnp.float32)).astype(x.dtype)

def _layernorm(x, g, b):
    xf = x.astype(jnp.float32)
    mu = jnp.mean(xf, axis=-1, keepdims=True)
    var = jnp.mean(jnp.square(xf - mu), axis=-1, keepdims=True)
    y = (xf - mu) * lax.rsqrt(var + EPS)
    return (y * g.astype(jnp.float32) + b.astype(jnp.float32)).astype(x.dtype)

def _t5_bucket(rel):
    nb = NUM_BUCKETS // 2
    max_exact = nb // 2
    ret = jnp.where(rel > 0, nb, 0)
    n = jnp.abs(rel)
    nf = jnp.maximum(n, 1).astype(jnp.float32)
    large = max_exact + (jnp.log(nf / max_exact) / np.log(MAX_DISTANCE / max_exact)
                         * (nb - max_exact)).astype(jnp.int32)
    large = jnp.minimum(large, nb - 1)
    return ret + jnp.where(n < max_exact, n, large)

def _hgrn2(q_raw, f_raw, i_raw, g_raw, lb, out_g):
    B, S, _ = q_raw.shape
    nc = S // CHUNK
    f32 = jnp.float32
    q = jax.nn.silu(q_raw.astype(f32))
    f = lb + (1.0 - lb) * jax.nn.sigmoid(f_raw.astype(f32))
    k = 1.0 - f
    lf = jnp.log(f)
    v = i_raw.astype(f32)

    def to_chunks(a, d):
        return a.reshape(B, nc, CHUNK, REC_HEADS, d).transpose(1, 0, 3, 2, 4)

    tril = jnp.tril(jnp.ones((CHUNK, CHUNK), bool))[:, :, None]

    def step(state, inp):
        qc, kc, vc, lfc = inp
        b = jnp.cumsum(lfc, axis=2)
        diff = b[:, :, :, None, :] - b[:, :, None, :, :]
        decay = jnp.where(tril, jnp.exp(jnp.where(tril, diff, 0.0)), 0.0)
        attn = jnp.einsum('bhtk,bhsk,bhtsk->bhts', qc, kc, decay)
        o = (jnp.einsum('bhts,bhsv->bhtv', attn, vc)
             + jnp.einsum('bhtk,bhkv->bhtv', qc * jnp.exp(b), state))
        b_end = b[:, :, -1:, :]
        state = (jnp.exp(b_end[:, :, 0, :])[..., None] * state
                 + jnp.einsum('bhsk,bhsv->bhkv', kc * jnp.exp(b_end - b), vc))
        return state, o

    s0 = jnp.zeros((B, REC_HEADS, REC_DK, REC_DV), f32)
    _, o = lax.scan(step, s0, (to_chunks(q, REC_DK), to_chunks(k, REC_DK),
                               to_chunks(v, REC_DV), to_chunks(lf, REC_DK)))
    o = o.transpose(1, 0, 3, 2, 4).reshape(B, S, REC_HEADS, REC_DV)
    o = _rms(o, out_g.reshape(REC_HEADS, REC_DV))
    gate = jax.nn.silu(g_raw.astype(f32)).reshape(B, S, REC_HEADS, REC_DV)
    return (o * gate).reshape(B, S, REC_W).astype(q_raw.dtype)

def _dsa_attention(q, k, v, iq, ik, iw, rel_bias):
    B, S = q.shape[0], q.shape[1]
    nb = S // QBLK
    k_sel = min(TOPK_MAX, S // 4)
    key_chunk = jnp.arange(S) // CHUNK
    ikf = ik.astype(jnp.float32)

    def blocks(a):
        return a.reshape((B, nb, QBLK) + a.shape[2:]).swapaxes(0, 1)

    def one_block(args):
        bi, qb, iqb, iwb = args
        t = bi * QBLK + jnp.arange(QBLK)
        t_chunk = t // CHUNK
        sc = jnp.einsum('bqhd,bsd->bqhs', iqb.astype(jnp.float32), ikf) * IDX_DIM ** -0.5
        score = jnp.einsum('bqhs,bqh->bqs', jax.nn.relu(sc), iwb.astype(jnp.float32))
        adm = key_chunk[None, :] <= t_chunk[:, None]
        score = jnp.where(adm[None], score, -jnp.inf)
        _, idx = lax.top_k(score, k_sel)
        valid = (idx // CHUNK) <= t_chunk[None, :, None]
        kg = jax.vmap(lambda a, j: a[j])(k, idx)
        vg = jax.vmap(lambda a, j: a[j])(v, idx)
        logits = jnp.einsum('bqhd,bqkhd->bqhk', qb, kg).astype(jnp.float32) * ATT_DH ** -0.5
        bias = rel_bias[_t5_bucket(idx - t[None, :, None])]
        logits = logits + jnp.swapaxes(bias, 2, 3).astype(jnp.float32)
        logits = jnp.where(valid[:, :, None, :], logits, -jnp.inf)
        p = jax.nn.softmax(logits, axis=-1).astype(vg.dtype)
        return jnp.einsum('bqhk,bqkhd->bqhd', p, vg)

    out = lax.map(one_block, (jnp.arange(nb), blocks(q), blocks(iq), blocks(iw)))
    return out.swapaxes(0, 1).reshape(B, S, ATT_HEADS, ATT_DH)

def _hier_moe(h, w_rg, b_rg, w_re, b_re, w1, w3, w2):
    B, S, D = h.shape
    hf = h.reshape(B * S, D)
    g_logits = (hf @ w_rg + b_rg).astype(jnp.float32)
    p_group = jax.nn.softmax(g_logits, axis=-1)
    g_top = jnp.argmax(g_logits, axis=-1)
    gate_g = jnp.take_along_axis(p_group, g_top[:, None], axis=-1)
    e_logits = (hf @ w_re + b_re).astype(jnp.float32).reshape(-1, N_GROUPS, EXPERTS_PER_GROUP)
    e_in = jnp.take_along_axis(e_logits, g_top[:, None, None], axis=1)[:, 0]
    top_v, top_j = lax.top_k(e_in, TOP_K_EXPERTS)
    w_sel = jax.nn.softmax(top_v, axis=-1) * gate_g
    e_id = g_top[:, None] * EXPERTS_PER_GROUP + top_j
    combine = jnp.einsum('nk,nke->ne', w_sel,
                         jax.nn.one_hot(e_id, N_EXPERTS_2, dtype=jnp.float32)).astype(h.dtype)
    y = jnp.zeros_like(hf)
    for e in range(N_EXPERTS_2):
        he = jax.nn.silu(hf @ w1[e]) * (hf @ w3[e])
        y = y + combine[:, e:e + 1] * (he @ w2[e])
    return y.reshape(B, S, D)

def second_inputs(seed: int = 0) -> dict:
    key = jax.random.key(seed)
    ks = jax.random.split(key, 24)
    f32 = jnp.float32

    def nrm(k, shape, s):
        return jax.random.normal(k, shape, f32) * s

    D = D_MODEL
    return {
        'x': nrm(ks[0], (BATCH, SEQ, D), 1.0),
        'c': nrm(ks[1], (BATCH, D), 1.0),
        'w_ada': nrm(ks[2], (DEPTH_2, D, 6 * D), 0.5 * D ** -0.5),
        'b_ada': nrm(ks[3], (DEPTH_2, 6 * D), 0.02),
        'norm1_g': 1.0 + nrm(ks[4], (DEPTH_2, D), 0.02),
        'norm2_g': 1.0 + nrm(ks[5], (DEPTH_2, D), 0.02),
        'w_in': nrm(ks[6], (DEPTH_2, D, D_IN), D ** -0.5),
        'lb_logits': nrm(ks[7], (DEPTH_2 + 1, REC_HEADS * REC_DK), 0.5),
        'rec_out_g': 1.0 + nrm(ks[8], (DEPTH_2, REC_W), 0.02),
        'q_norm_g': 1.0 + nrm(ks[9], (DEPTH_2, ATT_DH), 0.02),
        'k_norm_g': 1.0 + nrm(ks[10], (DEPTH_2, ATT_DH), 0.02),
        'idx_k_norm_g': 1.0 + nrm(ks[11], (DEPTH_2, IDX_DIM), 0.02),
        'idx_k_norm_b': nrm(ks[12], (DEPTH_2, IDX_DIM), 0.02),
        'attn_out_g': 1.0 + nrm(ks[13], (DEPTH_2, ATT_W), 0.02),
        'rel_bias': nrm(ks[14], (NUM_BUCKETS, ATT_HEADS), 0.5),
        'w_out': nrm(ks[15], (DEPTH_2, MIX_W, D), MIX_W ** -0.5),
        'w_rg': nrm(ks[16], (DEPTH_2, D, N_GROUPS), D ** -0.5),
        'b_rg': nrm(ks[17], (DEPTH_2, N_GROUPS), 0.01),
        'w_re': nrm(ks[18], (DEPTH_2, D, N_EXPERTS_2), D ** -0.5),
        'b_re': nrm(ks[19], (DEPTH_2, N_EXPERTS_2), 0.01),
        'w1': nrm(ks[20], (DEPTH_2, N_EXPERTS_2, D, D_EXPERT), D ** -0.5),
        'w3': nrm(ks[21], (DEPTH_2, N_EXPERTS_2, D, D_EXPERT), D ** -0.5),
        'w2': nrm(ks[22], (DEPTH_2, N_EXPERTS_2, D_EXPERT, D), D_EXPERT ** -0.5),
    }

def second_block(x, c, w_ada, b_ada, norm1_g, norm2_g, w_in, lb_logits, rec_out_g,
              q_norm_g, k_norm_g, idx_k_norm_g, idx_k_norm_b, attn_out_g, rel_bias,
              w_out, w_rg, b_rg, w_re, b_re, w1, w3, w2):
    B, S, D = x.shape
    lb_all = jnp.cumsum(jax.nn.softmax(lb_logits.astype(jnp.float32), axis=0), axis=0)
    for l in range(DEPTH_2):
        mod = jax.nn.silu(c) @ w_ada[l] + b_ada[l]
        sh1, sc1, g1, sh2, sc2, g2 = jnp.split(mod, 6, axis=-1)

        h = _rms(x, norm1_g[l]) * (1.0 + sc1[:, None, :]) + sh1[:, None, :]
        z = h @ w_in[l]
        rq, rf, ri, rg, aq, ak, av, iq, ik, iw = jnp.split(z, IN_OFFSETS, axis=-1)

        rec = _hgrn2(rq, rf, ri, rg, lb_all[l], rec_out_g[l])

        aq = _rms(aq.reshape(B, S, ATT_HEADS, ATT_DH), q_norm_g[l])
        ak = _rms(ak.reshape(B, S, ATT_HEADS, ATT_DH), k_norm_g[l])
        av = av.reshape(B, S, ATT_HEADS, ATT_DH)
        iq = iq.reshape(B, S, IDX_HEADS, IDX_DIM)
        ik = _layernorm(ik, idx_k_norm_g[l], idx_k_norm_b[l])
        iw = iw * IDX_HEADS ** -0.5
        att = _dsa_attention(aq, ak, av, iq, ik, iw, rel_bias)
        att = _rms(att, attn_out_g[l].reshape(ATT_HEADS, ATT_DH)).reshape(B, S, ATT_W)

        mix = jnp.concatenate([rec, att.astype(rec.dtype)], axis=-1) @ w_out[l]
        x = x + g1[:, None, :] * mix

        h2 = _rms(x, norm2_g[l]) * (1.0 + sc2[:, None, :]) + sh2[:, None, :]
        x = x + g2[:, None, :] * _hier_moe(h2, w_rg[l], b_rg[l], w_re[l], b_re[l],
                                           w1[l], w3[l], w2[l])
    return x


def setup_inputs(seed=0):
    out = dict(first_inputs(seed))
    for name, value in second_inputs(seed + 1).items():
        if name != "x":
            out[name + "_2"] = value
    return out


def reference(
    x, positions, ln_in_g, ln_in_b, w_in, mla_q_norm_g, mla_kv_norm_g, mla_w_uq, mla_w_ukv,
    diff_lam_q1, diff_lam_k1, diff_lam_q2, diff_lam_k2, diff_subln_g, fox_f_bias, w_out, ln1_g,
    ln1_b, router_w, router_bias, exp_w_gate, exp_w_up, exp_w_down, ln2_g, ln2_b, c_2, w_ada_2,
    b_ada_2, norm1_g_2, norm2_g_2, w_in_2, lb_logits_2, rec_out_g_2, q_norm_g_2, k_norm_g_2,
    idx_k_norm_g_2, idx_k_norm_b_2, attn_out_g_2, rel_bias_2, w_out_2, w_rg_2, b_rg_2, w_re_2,
    b_re_2, w1_2, w3_2, w2_2,
):
    x = first_block(
        x, positions, ln_in_g, ln_in_b, w_in, mla_q_norm_g, mla_kv_norm_g, mla_w_uq, mla_w_ukv,
        diff_lam_q1, diff_lam_k1, diff_lam_q2, diff_lam_k2, diff_subln_g, fox_f_bias, w_out,
        ln1_g, ln1_b, router_w, router_bias, exp_w_gate, exp_w_up, exp_w_down, ln2_g, ln2_b,
    )
    return second_block(
        x, c_2, w_ada_2, b_ada_2, norm1_g_2, norm2_g_2, w_in_2, lb_logits_2, rec_out_g_2,
        q_norm_g_2, k_norm_g_2, idx_k_norm_g_2, idx_k_norm_b_2, attn_out_g_2, rel_bias_2,
        w_out_2, w_rg_2, b_rg_2, w_re_2, b_re_2, w1_2, w3_2, w2_2,
    )


_drawn_inputs = setup_inputs


def setup_inputs(seed=0):
    import zlib

    import numpy as np

    out = dict(_drawn_inputs(seed))
    spreads = {}
    factors = {'mla_q_norm_g': 8.0,
     'mla_kv_norm_g': 3.451,
     'diff_lam_k1': 3.684,
     'diff_subln_g': 2.792,
     'norm1_g_2': 3.137,
     'norm2_g_2': 5.682,
     'lb_logits_2': 6.311,
     'rec_out_g_2': 8.0,
     'q_norm_g_2': 8.0,
     'k_norm_g_2': 8.0,
     'idx_k_norm_g_2': 3.944,
     'idx_k_norm_b_2': 5.08,
     'attn_out_g_2': 8.0,
     'b_rg_2': 6.687,
     'b_re_2': 8.0}
    for name, (base, spread) in spreads.items():
        noise = np.random.default_rng([zlib.crc32(name.encode()), seed]).standard_normal(out[name].shape)
        drawn = base * np.exp(spread * noise) if base else spread * noise
        out[name] = jnp.asarray(drawn.astype(out[name].dtype))
    for name, factor in factors.items():
        out[name] = (out[name] * factor).astype(out[name].dtype)
    return out
```

```python
from contextlib import ExitStack, contextmanager
import math

import numpy as np

import concourse.bass as bass
from concourse import mybir

F32 = mybir.dt.float32
I32 = mybir.dt.int32
U32 = mybir.dt.uint32
ALU = mybir.AluOpType
ACT = mybir.ActivationFunctionType
AX = mybir.AxisListType.X

P = 128
SEQ = 256
TILES = SEQ // P
D = 1024
DC = D // P
DEPTH = 2
HEADS = 8
CHUNK = 64
NEG = -1e30

MLA_Q, MLA_KV, MLA_ROPE, MLA_NOPE = 384, 256, 32, 64
MLA_QK = MLA_NOPE + MLA_ROPE
DIFF_QK, DIFF_ROT, DIFF_HEADS = 32, 8, 4
FOX_HEADS = 4
HD = 64
IN1 = 2212
IN2 = 4168
THETA = 500000.0
ALPHA = (2 * DEPTH) ** 0.25

REC_HEADS, REC_D = 4, 128
TOPK = 64
BUCKETS = 32
LEVELS = 8

N_EXPERTS, N_GROUPS, D_EXPERT = 16, 4, 512
EC = D_EXPERT // P

SLOT = 4096
SLOTS = 6
BANKS, BANK = 8, 512

TAB = {}
_at = 0
for _name, _n in (("ident", P), ("upto", P), ("before", P), ("ones", P), ("chunk_mask", TILES * SEQ),
                  ("causal_mask", TILES * SEQ), ("spans", LEVELS * P), ("last_span", P),
                  ("level_mask", LEVELS * P), ("freq_mla", MLA_ROPE // 2), ("freq_diff", DIFF_ROT // 2),
                  ("iota", N_EXPERTS)):
    TAB[_name] = (_at, _n)
    _at += _n
TAB_N = _at


def tables():
    tab = np.zeros((P, TAB_N), np.float32)

    def put(name, value):
        a, n = TAB[name]
        tab[:, a:a + n] = np.asarray(value, np.float32).reshape(P, n)

    p = np.arange(P)
    put("ident", np.eye(P))
    put("upto", p[:, None] <= p[None, :])
    put("before", p[:, None] < p[None, :])
    put("ones", np.ones((P, P)))
    k = np.arange(SEQ)
    q = p[:, None, None] + P * np.arange(TILES)[None, :, None]
    put("chunk_mask", np.where(k[None, None] // CHUNK <= q // CHUNK, 0.0, NEG))
    put("causal_mask", np.where(k[None, None] <= q, 0.0, NEG))
    u, x = p[:, None, None], p[None, None, :]
    size = (2 ** np.arange(LEVELS))[None, :, None]
    mid = (x // (2 * size)) * (2 * size) + size
    right = x >= mid
    put("spans", np.where(right, (mid <= u) & (u <= x), (x < u) & (u < mid)))
    put("last_span", p[:, None] <= p[None, :])
    s, t = p[:, None, None], p[None, None, :]
    size = (2 ** np.arange(LEVELS - 1))[None, :, None]
    pair = (s // (2 * size) == t // (2 * size)) & (s // size % 2 == 0) & (t // size % 2 == 1)
    put("level_mask", np.concatenate([pair, (s == t)], axis=1))
    f = lambda n: np.float32(THETA) ** (-np.arange(0, n, 2, dtype=np.float32) / np.float32(n))
    put("freq_mla", np.broadcast_to(f(MLA_ROPE), (P, MLA_ROPE // 2)))
    put("freq_diff", np.broadcast_to(f(DIFF_ROT), (P, DIFF_ROT // 2)))
    put("iota", np.broadcast_to(np.arange(N_EXPERTS), (P, N_EXPERTS)))
    return tab


SCRATCH = {"mod": (4 * D,), "bias_rows": (HEADS * P * 2 * SEQ + 2 * SEQ,)}


def bucket_table():
    rel = np.arange(-(SEQ - 1), SEQ)
    half, exact, far = BUCKETS // 2, BUCKETS // 4, 128
    n = np.abs(rel)
    nf = np.maximum(n, 1).astype(np.float32)
    large = exact + (np.log(nf / np.float32(exact)) / np.float32(np.log(far / exact))
                     * np.float32(half - exact)).astype(np.int32)
    b = np.where(rel > 0, half, 0) + np.where(n < exact, n, np.minimum(large, half - 1))
    out = np.zeros((BUCKETS, 2 * SEQ), np.float32)
    out[b, np.arange(rel.size)] = 1.0
    return out


class Ring:

    def __init__(self, tensor, landed, unit_used, sources):
        self.tensor, self.landed, self.unit_used, self.sources = tensor, landed, unit_used, sources
        self.sent = 0
        self.used = 0

    def view(self, n, c):
        w = self.sources[n].shape[2]
        return self.tensor[:, n % SLOTS, 0:c * w].rearrange("p (c w) -> p c w", c=c)

    def landings(self, n):
        return 16 * sum(s is not None for s in self.sources[n % SLOTS:n + 1:SLOTS])

    def after(self, n):
        n += 1
        while n < len(self.sources) and self.sources[n] is None:
            n += 1
        return n

    def feed(self, sp, consumed):
        while self.sent < min(len(self.sources), consumed + SLOTS):
            n = self.sent
            source = self.sources[n]
            if source is not None:
                if n >= SLOTS:
                    sp.wait_ge(self.unit_used, n - SLOTS + 1)
                sp.dma_start(self.view(n, source.shape[1]), source).then_inc(self.landed[n % SLOTS], 16)
            self.sent += 1


def build(nc, a, scratch, outs, stop=None):
    ctx = ExitStack()
    with ctx:
        def sb(name, shape, dt=F32):
            return ctx.enter_context(nc.sbuf_tensor(name, shape, dt))

        ring_mem = sb("ring", [P, SLOTS, SLOT])
        tab = sb("tab", [P, TAB_N])
        h = sb("h", [P, TILES, D])
        hT = sb("hT", [P, DC, SEQ])
        par = sb("par", [P, 5120])
        ARENA = 15000
        arena = sb("arena", [P, ARENA])
        trig = sb("trig", [P, TILES, 2, 20])
        positions_i = sb("positions_i", [P, TILES], I32)
        small = sb("small", [P, 512])
        index = sb("index", [P, 16], U32)
        ps = ctx.enter_context(nc.psum_tensor("ps", [P, BANKS, BANK], F32))

        def table(name):
            at, n = TAB[name]
            return tab[:, at:at + n]

        ident, upto, before, ones = (table(x) for x in ("ident", "upto", "before", "ones"))

        def region(at, *dims):
            n = int(np.prod(dims))
            assert at + n <= ARENA, (at, dims)
            v = arena[:, at:at + n]
            if len(dims) == 1:
                return v
            names = "abcd"[:len(dims)]
            return v.rearrange(f"p ({' '.join(names)}) -> p {' '.join(names)}",
                               **{x: d for x, d in zip(names, dims)})

        mixed = hT[:, :, :].rearrange("p c t -> p (c t)").rearrange("p (t n) -> p t n", t=TILES)

        sources = []

        def unit(w, chunks, lo, hi):
            sources.append(w.rearrange("(c p) n -> p c n", p=P)[:, :, lo:hi])
            return len(sources) - 1

        def cut(w, chunks, cols, width):
            return [unit(w, chunks, x, min(x + width, cols)) for x in range(0, cols, width)]

        def expert_units(gate, up, down):
            while len(sources) % SLOTS:
                sources.append(None)
            first = len(sources)
            for e in range(N_EXPERTS):
                unit(gate[e], DC, 0, D_EXPERT)
                unit(up[e], DC, 0, D_EXPERT)
                unit(down[e], EC, 0, D)
            return first

        plan = []
        for l in range(DEPTH):
            plan.append({
                "in": cut(a["w_in"][l], DC, IN1, 512),
                "uq": cut(a["mla_w_uq"][l], 3, 768, 768),
                "ukv": cut(a["mla_w_ukv"][l], 2, 1024, 1024),
                "out": cut(a["w_out"][l], DC, D, 512),
                "experts": expert_units(a["exp_w_gate"][l], a["exp_w_up"][l], a["exp_w_down"][l]),
            })
        plan.append({
            "ada": cut(a["w_ada_2"][0], DC, 6 * D, 512),
            "in": cut(a["w_in_2"][0], DC, IN2, 512),
            "out": cut(a["w_out_2"][0], DC, D, 512),
            "experts": expert_units(a["w1_2"][0], a["w3_2"][0], a["w2_2"][0]),
        })
        landed = [ctx.enter_context(nc.semaphore(f"landed{i}")) for i in range(SLOTS)]
        unit_used = ctx.enter_context(nc.semaphore("unit_used"))
        ring = Ring(ring_mem, landed, unit_used, sources)

        @contextmanager
        def stage(*names):
            with ExitStack() as s:
                sems = [s.enter_context(nc.semaphore(x)) for x in names]
                with nc.Block(no_gpsimd_drain=True) as block:
                    yield sems, block
                for x in sems:
                    nc.sync.sem_clear(x)

        class Chain:

            def __init__(self, eng, sem):
                self.eng, self.sem, self.n = eng, sem, 0

            def __call__(self, ins):
                ins.then_inc(self.sem, 1)
                self.n += 1
                self.eng.wait_ge(self.sem, self.n)

        V, S, G, T = nc.vector, nc.scalar, nc.gpsimd, nc.tensor

        def bc(x, dims, at):
            return x.unsqueeze(at).broadcast_to(tuple(dims))


        def load_stage(pairs):
            with stage("loaded") as ((loaded,), block):
                @block.scalar
                def _(act):
                    with nc.allow_non_contiguous_dma("small vectors, once"):
                        for dst, src in pairs:
                            act.dma_start(dst, src).then_inc(loaded, 16)
                    act.wait_ge(loaded, 16 * len(pairs))

        def every(x, n):
            return x.rearrange("(o n) -> o n", o=1).broadcast_to((P, n))

        def turn_stage(src, n, rows, dst):
            banks = (n + 1) // 2
            with stage("turned", "act_copied", "dve_copied") as ((turned, act_copied, dve_copied), block):
                @block.tensor
                def _(pe):
                    for b in range(banks):
                        if b >= BANKS:
                            pe.wait_ge((act_copied, dve_copied)[b % 2], (b - BANKS) // 2 + 1)
                        for i in range(2 * b, min(2 * b + 2, n)):
                            for t in range(TILES):
                                at = (i % 2) * SEQ + t * P
                                last = T.transpose(ps[0:rows, b % BANKS, at:at + P], src(t, i), ident)
                        last.then_inc(turned, 1)

                def copy(eng, b, sem, op):
                    i, m = 2 * b, min(2, n - 2 * b)
                    eng.wait_ge(turned, b + 1)
                    op(dst[0:rows, i:i + m, :], ps[0:rows, b % BANKS, 0:m * SEQ]
                       .rearrange("p (i t) -> p i t", i=m)).then_inc(sem, 1)

                @block.scalar
                def _(act):
                    for b in range(0, banks, 2):
                        copy(act, b, act_copied, lambda o, i: S.activation(o, i, ACT.Copy))

                @block.vector
                def _(dve):
                    for b in range(1, banks, 2):
                        copy(dve, b, dve_copied, V.tensor_copy)

        def project_stage(xT, chunks, jobs):
            last_job = {u: i for i, (u, *_) in enumerate(jobs)}
            with stage("group_done", "act_copied", "dve_copied") as ((group_done, act_copied, dve_copied), block):
                copied = (act_copied, dve_copied)

                @block.sync
                def _(sp):
                    ring.feed(sp, ring.after(jobs[-1][0]))

                @block.tensor
                def _(pe):
                    for i, (u, lo, width, _) in enumerate(jobs):
                        w = ring.view(u, chunks)
                        pe.wait_ge(ring.landed[u % SLOTS], ring.landings(u))
                        for t in range(TILES):
                            if i >= BANKS // 2:
                                pe.wait_ge(copied[t], i - BANKS // 2 + 1)
                            for c in range(chunks):
                                last = T.matmul(ps[:, (TILES * i + t) % BANKS, 0:width],
                                                xT[:, c, t * P:(t + 1) * P], w[:, c, lo:lo + width],
                                                start=c == 0, stop=c == chunks - 1)
                            last.then_inc(group_done, 1)
                        if last_job[u] == i:
                            pe.wait_ge(group_done, TILES * (i + 1))
                            pe.sem_inc(ring.unit_used, ring.after(u) - ring.used)
                            ring.used = ring.after(u)

                def copy(eng, t, op):
                    for i, (_, _, width, dst) in enumerate(jobs):
                        eng.wait_ge(group_done, TILES * i + t + 1)
                        op(dst(t), ps[:, (TILES * i + t) % BANKS, 0:width]).then_inc(copied[t], 1)

                @block.scalar
                def _(act):
                    copy(act, 0, lambda o, i: S.activation(o, i, ACT.Copy))

                @block.vector
                def _(dve):
                    copy(dve, 1, V.tensor_copy)

        def layer_norm_stage(eps, gain, bias, mix=None):
            with stage("chain", "rooted", "moment") as ((chain, rooted, moment), block):
                stats, mv = small[:, 0:24].rearrange("p (t s) -> p t s", t=TILES), small[:, 24:28]

                @block.vector
                def _(dve):
                    link = Chain(dve, chain)
                    for t in range(TILES):
                        if mix is not None:
                            link(V.scalar_tensor_tensor(h[:, t, :], h[:, t, :], ALPHA, mix[:, t, :],
                                                        ALU.mult, ALU.add))
                        for j in range(2):
                            link(V.bn_stats(stats[:, t, 6 * j:6 * j + 6], h[:, t, 512 * j:512 * j + 512]))
                        link(V.bn_aggr(mv[:, 2 * t:2 * t + 2], stats[:, t, :]))
                    V.tensor_scalar(small[:, 28:30], mv[:, 1:4:2], eps, None, ALU.add).then_inc(moment, 1)
                    dve.wait_ge(rooted, 1)
                    link(V.reciprocal(small[:, 32:34], small[:, 30:32]))
                    for t in range(TILES):
                        link(V.tensor_scalar(h[:, t, :], h[:, t, :], mv[:, 2 * t:2 * t + 1],
                                             small[:, 32 + t:33 + t], ALU.subtract, ALU.mult))
                        link(V.tensor_tensor(h[:, t, :], h[:, t, :], gain, ALU.mult))
                        link(V.tensor_tensor(h[:, t, :], h[:, t, :], bias, ALU.add))

                @block.scalar
                def _(act):
                    act.wait_ge(moment, 1)
                    S.activation(small[:, 30:32], small[:, 28:30], ACT.Sqrt).then_inc(rooted, 1)

        def rms_stage(jobs, squares):
            with stage("chain", "rooted", "moment") as ((chain, rooted, moment), block):
                @block.vector
                def _(dve):
                    link = Chain(dve, chain)
                    for i, (x, out, eps, factors) in enumerate(jobs):
                        g, w = x.shape[1], x.shape[2]
                        sq = squares[:, 0:g * w].rearrange("p (g w) -> p g w", g=g)
                        link(V.tensor_tensor(sq, x, x, ALU.mult))
                        link(V.tensor_reduce(small[:, 0:g], sq, AX, ALU.add))
                        V.tensor_scalar(small[:, 32:32 + g], small[:, 0:g], 1.0 / w, eps, ALU.mult, ALU.add)\
                            .then_inc(moment, 1)
                        dve.wait_ge(rooted, i + 1)
                        link(V.reciprocal(small[:, 96:96 + g], small[:, 64:64 + g]))
                        link(V.tensor_tensor(out, x, bc(small[:, 96:96 + g], (P, g, w), 2), ALU.mult))
                        for f in factors:
                            link(V.tensor_tensor(out, out, f, ALU.mult))

                @block.scalar
                def _(act):
                    for i, (x, *_) in enumerate(jobs):
                        g = x.shape[1]
                        act.wait_ge(moment, i + 1)
                        S.activation(small[:, 64:64 + g], small[:, 32:32 + g], ACT.Sqrt).then_inc(rooted, 1)

        def attend_stage(heads, dh, qT, kT, value, scale, bias, out, prob, probT, combine=None):
            mx, total = small[:, 0:heads], small[:, 8:8 + heads]
            names = ("scored", "chain", "ready", "weighed", "turned", "copied", "mixed_v", "written")
            with stage(*names) as ((scored, chain, ready, weighed, turned, copied, mixed_v, written), block):
                def scores(t):
                    return ps[:, 4 * t:4 * t + heads // 2, :].rearrange("p b (j k) -> p (b j) k", j=2)

                def turned_p(t):
                    return ps[:, 4 * t:4 * t + (t + 1) * heads // 4, :].rearrange(
                        "p b (h q) -> p (b h) q", q=P)

                def result(t):
                    return ps[:, 2 + t, 0:heads * HD].rearrange("p (h d) -> p h d", h=heads)

                @block.tensor
                def _(pe):
                    for t in range(TILES):
                        keys = (t + 1) * P
                        for i in range(heads):
                            last = T.matmul(scores(t)[:, i, 0:keys], qT[0:dh, i, t * P:(t + 1) * P],
                                            kT[0:dh, i, 0:keys], start=True, stop=True)
                        last.then_inc(scored, 1)
                    for t in range(TILES):
                        pe.wait_ge(weighed, t + 1)
                        for j in range(t + 1):
                            for i in range(heads):
                                last = T.transpose(turned_p(t)[:, j * heads + i, :],
                                                   prob[:, i, j * P:(j + 1) * P], ident)
                        last.then_inc(turned, 1)
                        pe.wait_ge(copied, t + 1)
                        for i in range(heads):
                            for j in range(t + 1):
                                last = T.matmul(result(t)[:, i, :], probT[:, j * heads + i, :], value(j, i),
                                                start=j == 0, stop=j == t)
                        last.then_inc(mixed_v, 1)

                @block.scalar
                def _(act):
                    for t in range(TILES):
                        keys = (t + 1) * P
                        act.wait_ge(ready, t + 1)
                        S.activation(prob[:, 0:heads, 0:keys], prob[:, 0:heads, 0:keys], ACT.Exp)\
                            .then_inc(weighed, 1)
                        act.wait_ge(turned, t + 1)
                        if t:
                            act.wait_ge(mixed_v, t)
                        n = (t + 1) * heads
                        S.activation(probT[:, 0:n, :], turned_p(t), ACT.Copy).then_inc(copied, 1)

                @block.vector
                def _(dve):
                    link = Chain(dve, chain)
                    for t in range(TILES):
                        keys = (t + 1) * P
                        s = prob[:, 0:heads, 0:keys]
                        dve.wait_ge(scored, t + 1)
                        if t:
                            dve.wait_ge(turned, t)
                        link(V.scalar_tensor_tensor(s, scores(t)[:, :, 0:keys], scale, bias(t, keys),
                                                    ALU.mult, ALU.add))
                        link(V.tensor_reduce(mx, s, AX, ALU.max))
                        V.tensor_tensor(s, s, bc(mx, (P, heads, keys), 2), ALU.subtract).then_inc(ready, 1)
                        dve.wait_ge(weighed, t + 1)
                        link(V.tensor_reduce(total, s, AX, ALU.add))
                        link(V.reciprocal(total, total))
                        dve.wait_ge(mixed_v, t + 1)
                        if combine is None:
                            link(V.tensor_tensor(out(t), result(t), bc(total, (P, heads, HD), 2), ALU.mult))
                        else:
                            combine(link, t, result(t), total)


        def vector_stage(program):
            with stage("chain") as ((chain,), block):
                @block.vector
                def _(dve):
                    program(Chain(dve, chain))

        ang = small[:, 16:96].rearrange("p (t c f) -> p t c f", t=TILES, c=2)

        def trig_program(link):
            pos = small[:, 0:TILES]
            link(V.tensor_copy(pos, positions_i[:, :]))
            turns = small[:, 96:176].rearrange("p (t c f) -> p t c f", t=TILES, c=2)
            a0, n0 = TAB["freq_mla"][0], (MLA_ROPE + DIFF_ROT) // 2
            for t in range(TILES):
                link(V.tensor_scalar(ang[:, t, 1, :], tab[:, a0:a0 + n0], pos[:, t:t + 1], None, ALU.mult))
            magic = 1.5 * 2.0 ** 23
            two_pi = 2 * math.pi
            c1 = 6.28125
            c2 = float(np.float32(np.floor((two_pi - c1) * 2 ** 22) / 2 ** 22))
            c3 = two_pi - c1 - c2
            for t in range(TILES):
                x, y = ang[:, t, 1, :], turns[:, t, 1, :]
                link(V.tensor_scalar(y, x, 1 / two_pi, None, ALU.mult))
                link(V.tensor_scalar(y, y, magic, None, ALU.add))
                link(V.tensor_scalar(y, y, -magic, None, ALU.add))
                for c in (c1, c2, c3):
                    link(V.scalar_tensor_tensor(x, y, -c, x, ALU.mult, ALU.add))
                z = ang[:, t, 0, :]
                link(V.tensor_scalar(z, x, math.pi / 2, None, ALU.add))
                link(V.tensor_scalar(y, z, math.pi, -two_pi, ALU.is_gt, ALU.mult))
                link(V.tensor_tensor(z, z, y, ALU.add))
                link(V.tensor_scalar(ang[:, t, :, :], ang[:, t, :, :], 3.1415925, -3.1415925, ALU.min, ALU.max))

        def rope(link, x, heads, width, t, first, n, tmp):
            cos = bc(trig[:, t, 0, first:first + n], (P, heads, n), 1)
            sin = bc(trig[:, t, 1, first:first + n], (P, heads, n), 1)
            x1, x2 = x[:, :, 0:n], x[:, :, n:2 * n]
            y = tmp[:, 0:4 * heads * n].rearrange("p (i h n) -> p i h n", i=4, h=heads)
            link(V.tensor_tensor(y[:, 0], x1, cos, ALU.mult))
            link(V.tensor_tensor(y[:, 1], x2, sin, ALU.mult))
            link(V.tensor_tensor(y[:, 2], x2, cos, ALU.mult))
            link(V.tensor_tensor(y[:, 3], x1, sin, ALU.mult))
            link(V.tensor_tensor(x1, y[:, 0], y[:, 1], ALU.subtract))
            link(V.tensor_tensor(x2, y[:, 2], y[:, 3], ALU.add))

        PAR1 = {"q_g": (0, 384), "kv_g": (384, 256), "sub_g": (640, 64), "ln1_g": (704, 1024),
                "ln1_b": (1728, 1024), "ln2_g": (2752, 1024), "ln2_b": (3776, 1024), "fox_b": (4800, 4),
                "lam": (4804, 128), "router_b": (4932, 16)}

        def par_at(names, name):
            at, n = names[name]
            return par[:, at:at + n]

        with stage("start") as ((start,), block):
            @block.sync
            def _(sp):
                sp.dma_start(h[:, :, :], a["x"][0].rearrange("(t p) n -> p t n", p=P)).then_inc(start, 16)
                ring.feed(sp, 0)
                sp.wait_ge(start, 48)

            @block.scalar
            def _(act):
                act.dma_start(tab[:, :], a["tab"]).then_inc(start, 16)
                with nc.allow_non_contiguous_dma("256 positions"):
                    act.dma_start(positions_i[:, :], a["positions"].rearrange("o (t p) -> p (o t)", p=P))\
                        .then_inc(start, 16)
        load_stage([(par[:, 0:D], every(a["ln_in_g"], D)), (par[:, D:2 * D], every(a["ln_in_b"], D))])
        layer_norm_stage(1e-5, par[:, 0:D], par[:, D:2 * D])
        vector_stage(trig_program)
        with stage("sines") as ((sines,), block):
            @block.scalar
            def _(act):
                S.activation(trig[:, :, :, :], ang, ACT.Sin).then_inc(sines, 1)

        def finish_here():
            with stage("store") as ((store,), block):
                @block.sync
                def _(sp):
                    sp.dma_start(outs[0].rearrange("(t p) n -> p t n", p=P), h[:, :, :]).then_inc(store, 16)
                    sp.wait_ge(store, 16)

        gates = small[:, 448:448 + TILES * N_EXPERTS].rearrange("p (t e) -> p t e", t=TILES)

        def router_stage(w, n):
            with stage("done") as ((done,), block):
                @block.tensor
                def _(pe):
                    for t in range(TILES):
                        for c in range(DC):
                            last = T.matmul(ps[:, t, 0:n], hT[:, c, t * P:(t + 1) * P], w[:, c, :],
                                            start=c == 0, stop=c == DC - 1)
                    last.then_inc(done, 1)
                    pe.wait_ge(done, 1)

        def top2(link, x, t_room):
            vals, hot = t_room[:, 0:8], t_room[:, 8:40].rearrange("p (j e) -> p j e", j=2)
            link(V.max(vals, x))
            link(V.max_index(index[:, 0:8], vals, x))
            link(V.tensor_copy(t_room[:, 40:48], index[:, 0:8]))
            for j in range(2):
                link(V.tensor_scalar(hot[:, j, :], table("iota"), t_room[:, 40 + j:41 + j], None, ALU.is_equal))
            return vals, hot

        def first_of_groups(link, x4, room):
            pad, vals = room[:, 0:8], room[:, 8:16]
            link(V.memset(pad[:, 4:8], -3e38))
            link(V.tensor_copy(pad[:, 0:4], x4))
            link(V.max(vals, pad))
            link(V.max_index(index[:, 0:8], vals, pad))
            link(V.tensor_copy(room[:, 16:17], index[:, 0:1]))
            link(V.tensor_scalar(room[:, 20:24], table("iota")[:, 0:4], room[:, 16:17], None, ALU.is_equal))
            return room[:, 20:24], vals

        def keep_group(link, out, x, group, room):
            full = room[:, 0:16].rearrange("p (g e) -> p g e", g=4)
            off = room[:, 16:20]
            link(V.tensor_scalar(off, group, -NEG, NEG, ALU.mult, ALU.add))
            link(V.tensor_tensor(full, x.rearrange("p (g e) -> p g e", g=4), bc(group, (P, 4, 4), 2), ALU.mult))
            link(V.tensor_tensor(out.rearrange("p (g e) -> p g e", g=4), full, bc(off, (P, 4, 4), 2), ALU.add))

        def route1(link):
            router_b = par_at(PAR1, "router_b")
            for t in range(TILES):
                score, biased = small[:, 16 * t:16 * t + 16], small[:, 32:48]
                link(V.tensor_tensor(biased, score, router_b, ALU.add))
                b4 = biased.rearrange("p (g e) -> p g e", g=4)
                even, odd = b4[:, :, 0:4:2], b4[:, :, 1:4:2]
                hi = small[:, 48:56].rearrange("p (g e) -> p g e", g=4)
                lo = small[:, 56:64].rearrange("p (g e) -> p g e", g=4)
                link(V.tensor_tensor(hi, even, odd, ALU.max))
                link(V.tensor_tensor(lo, even, odd, ALU.min))
                link(V.tensor_reduce(small[:, 64:68], hi, AX, ALU.max))
                link(V.tensor_reduce(small[:, 68:72], hi, AX, ALU.min))
                link(V.tensor_reduce(small[:, 72:76], lo, AX, ALU.max))
                link(V.tensor_tensor(small[:, 68:72], small[:, 68:72], small[:, 72:76], ALU.max))
                link(V.tensor_tensor(small[:, 64:68], small[:, 64:68], small[:, 68:72], ALU.add))
                group, _ = first_of_groups(link, small[:, 64:68], small[:, 80:112])
                keep_group(link, small[:, 112:128], biased, group, small[:, 128:160])
                _, hot = top2(link, small[:, 112:128], small[:, 160:224])
                g = gates[:, t, :]
                link(V.tensor_tensor(small[:, 224:240], hot[:, 0, :], hot[:, 1, :], ALU.add))
                link(V.tensor_tensor(small[:, 240:256], small[:, 224:240], score, ALU.mult))
                link(V.tensor_reduce(small[:, 256:257], small[:, 240:256], AX, ALU.add))
                link(V.reciprocal(small[:, 257:258], small[:, 256:257]))
                link(V.tensor_scalar(g, small[:, 240:256], small[:, 257:258], None, ALU.mult))

        def experts_stage(first):
            y = arena[:, 0:TILES * D].rearrange("p (t n) -> p t n", t=TILES)
            at = TILES * D
            sig, act_rows = region(at, 2, 512), region(at + 1024, 2, 512)
            actT = region(at + 2048, 2, EC, P)
            names = ("gu_done", "sig_done", "rows_done", "turned", "copied", "down_done", "cleared")
            base = first
            with stage(*names) as ((gu_done, sig_done, rows_done, turned, copied, down_done, cleared), block):
                pairs = N_EXPERTS // 2
                here = [ring.landings(first + j) for j in range(SLOTS)]
                assert ring.used == first
                ring.used = first + 3 * N_EXPERTS

                @block.sync
                def _(sp):
                    ring.feed(sp, first)
                    assert ring.sent == first + SLOTS
                    with sp.Fori(1, pairs) as i:
                        for j in range(SLOTS):
                            mat = (sources_of[first][j % 3])
                            e = j // 3
                            sp.wait_ge(unit_used, i * SLOTS + (first - SLOTS + j + 1))
                            w = mat[bass.ds(2 * i + e, 1)].rearrange("o (c p) n -> p (o c) n", p=P)
                            c = w.shape[1]
                            dst = ring_mem[:, j, :].rearrange("p (c w) -> p c w", c=c)
                            sp.dma_start(dst, w).then_inc(landed[j], 16)
                    ring.sent = first + 3 * N_EXPERTS
                    ring.feed(sp, first + 3 * N_EXPERTS)

                @block.tensor
                def _(pe):
                    pe.wait_ge(cleared, 1)
                    for b in range(4):
                        T.matmul(ps[:, b, :], sig[:, 0, 0:P], sig[:, 0, :], start=True, stop=True)
                    with pe.Fori(0, pairs) as i:
                        for e in range(2):
                            for t in range(TILES):
                                n = 2 * e + t
                                for m in range(2):
                                    slot = 3 * e + m
                                    w = ring_mem[:, slot, :].rearrange("p (c w) -> p c w", c=DC)
                                    if t == 0:
                                        pe.wait_ge(landed[slot], i * 16 + here[slot])
                                    if m == 0 and n >= 1:
                                        pe.wait_ge(rows_done, i * 4 + n)
                                    elif m == 0:
                                        pe.wait_ge(rows_done, i * 4)
                                    for c in range(DC):
                                        last = T.matmul(ps[:, 4 + m, :], hT[:, c, t * P:(t + 1) * P], w[:, c, :],
                                                        start=c == 0, stop=c == DC - 1)
                                    if m == 0 or t == 0:
                                        last.then_inc(gu_done, 1)
                                    else:
                                        last.then_inc(gu_done, 1)
                                pe.wait_ge(rows_done, i * 4 + (n + 1))
                                for k in range(EC):
                                    last = T.transpose(ps[:, 6, k * P:(k + 1) * P],
                                                       act_rows[:, 0, k * P:(k + 1) * P], ident)
                                last.then_inc(turned, 1)
                                slot = 3 * e + 2
                                w = ring_mem[:, slot, :].rearrange("p (c w) -> p c w", c=EC)
                                if t == 0:
                                    pe.wait_ge(landed[slot], i * 16 + here[slot])
                                pe.wait_ge(copied, i * 4 + (n + 1))
                                for k in range(EC):
                                    for x in range(2):
                                        last = T.matmul(ps[:, 2 * t + x, :], actT[:, 0, k, :],
                                                        w[:, k, x * 512:(x + 1) * 512],
                                                        start=False, stop=True, skip_group_check=True)
                                last.then_inc(down_done, 1)
                            pe.wait_ge(down_done, i * 4 + (2 * e + 2))
                            pe.sem_inc(unit_used, 3)

                @block.scalar
                def _(act):
                    with act.Fori(0, pairs) as i:
                        for n in range(4):
                            act.wait_ge(gu_done, i * 8 + (2 * n + 1))
                            if n:
                                act.wait_ge(rows_done, i * 4 + n)
                            S.activation(sig[:, 0, :], ps[:, 4, :], ACT.Silu).then_inc(sig_done, 1)
                            act.wait_ge(turned, i * 4 + (n + 1))
                            act.wait_ge(down_done, i * 4 + n)
                            S.activation(actT[:, 0, :, :].rearrange("p k t -> p (k t)"), ps[:, 6, :], ACT.Copy)\
                                .then_inc(copied, 1)

                @block.vector
                def _(dve):
                    V.memset(sig[:, 0, :], 0.0).then_inc(cleared, 1)
                    with dve.Fori(0, pairs) as i:
                        for n in range(4):
                            e, t = n // 2, n % 2
                            dve.wait_ge(gu_done, i * 8 + (2 * n + 2))
                            dve.wait_ge(sig_done, i * 4 + (n + 1))
                            dve.wait_ge(turned, i * 4 + n)
                            V.scalar_tensor_tensor(act_rows[:, 0, :], sig[:, 0, :],
                                                   gates[:, t, bass.ds(2 * i + e, 1)], ps[:, 5, :],
                                                   ALU.mult, ALU.mult).then_inc(rows_done, 1)
                    dve.wait_ge(down_done, 2 * N_EXPERTS)
                    V.tensor_copy(y, ps[:, 0:4, :].rearrange("p (t x) n -> p t (x n)", t=TILES)).then_inc(cleared, 1)
            return y

        sources_of = {plan[l]["experts"]: (a["exp_w_gate"][l], a["exp_w_up"][l], a["exp_w_down"][l])
                      for l in range(DEPTH)}
        sources_of[plan[DEPTH]["experts"]] = (a["w1_2"][0], a["w3_2"][0], a["w2_2"][0])

        def turn_h():
            turn_stage(lambda t, c: h[:, t, c * P:(c + 1) * P], DC, P, hT)

        def output_stage(units):
            oT = region(TILES * D, DC, SEQ)
            turn_stage(lambda t, c: mixed[:, t, c * P:(c + 1) * P], DC, P, oT)
            mix = region(0, TILES, D)
            project_stage(oT, DC, [(u, 0, 512, lambda t, i=i: mix[:, t, i * 512:(i + 1) * 512])
                                   for i, u in enumerate(units)])
            return mix

        for l in range(DEPTH):
            lam_init = 0.8 - 0.6 * math.exp(-0.3 * l)
            p1 = lambda name: par_at(PAR1, name)
            load_stage([(p1("q_g"), every(a["mla_q_norm_g"][l], 384)), (p1("kv_g"), every(a["mla_kv_norm_g"][l], 256)),
                        (p1("sub_g"), every(a["diff_subln_g"][l], 64)), (p1("ln1_g"), every(a["ln1_g"][l], D)),
                        (p1("ln1_b"), every(a["ln1_b"][l], D)), (p1("ln2_g"), every(a["ln2_g"][l], D)),
                        (p1("ln2_b"), every(a["ln2_b"][l], D)), (p1("fox_b"), every(a["fox_f_bias"][l], 4)),
                        (p1("router_b"), every(a["router_bias"], 16))] +
                       [(p1("lam")[:, 32 * i:32 * i + 32], every(a["diff_lam_" + x][l], 32))
                        for i, x in enumerate(("q1", "k1", "q2", "k2"))])
            turn_h()
            z = region(0, TILES, IN1)
            project_stage(hT, DC, [(u, 0, min(512, IN1 - 512 * i),
                                    lambda t, i=i: z[:, t, 512 * i:min(512 * i + 512, IN1)])
                                   for i, u in enumerate(plan[l]["in"])])
            base = TILES * IN1
            kv = region(base, TILES, HEADS, 128)
            qT, kT = region(base + 2048, HEADS, SEQ), region(base + 4096, HEADS, SEQ)
            prob, probT = region(base + 6144, HEADS, SEQ), region(base + 8192, TILES * HEADS, P)
            rms_stage([(z[:, t, o:o + w].unsqueeze(1), z[:, t, o:o + w].unsqueeze(1), 1e-6,
                        [p1(g).unsqueeze(1)])
                       for t in range(TILES) for o, w, g in ((0, MLA_Q, "q_g"), (MLA_Q, MLA_KV, "kv_g"))],
                      region(base + 6144, 2048))
            cT = region(base + 2048, 5, SEQ)
            turn_stage(lambda t, c: z[:, t, c * P:(c + 1) * P], 5, P, cT)
            q96 = region(base + 6144, TILES, HEADS, MLA_QK)
            q_flat = q96.rearrange("p t h d -> p t (h d)")
            kv_flat = kv.rearrange("p t h d -> p t (h d)")
            uq, ukv = plan[l]["uq"][0], plan[l]["ukv"][0]
            project_stage(cT[:, 0:3, :], 3, [(uq, o, w, lambda t, o=o, w=w: q_flat[:, t, o:o + w])
                                             for o, w in ((0, 512), (512, 256))])
            project_stage(cT[:, 3:5, :], 2, [(ukv, o, 512, lambda t, o=o: kv_flat[:, t, o:o + 512])
                                             for o in (0, 512)])
            k96 = region(base + 8192, TILES, HEADS, MLA_QK)
            tmp = region(base + 2048, 2048)

            def rope_program(link):
                r0 = MLA_Q + MLA_KV
                for t in range(TILES):
                    rope(link, q96[:, t, :, MLA_NOPE:], HEADS, MLA_QK, t, 0, MLA_ROPE // 2, tmp)
                    rope(link, z[:, t, r0:r0 + MLA_ROPE].unsqueeze(1), 1, MLA_ROPE, t, 0, MLA_ROPE // 2, tmp)
                    link(V.tensor_copy(k96[:, t, :, 0:MLA_NOPE], kv[:, t, :, 0:MLA_NOPE]))
                    link(V.tensor_copy(k96[:, t, :, MLA_NOPE:],
                                       bc(z[:, t, r0:r0 + MLA_ROPE], (P, HEADS, MLA_ROPE), 1)))
                    d0 = r0 + MLA_ROPE
                    for o in (d0, d0 + 256):
                        rope(link, z[:, t, o:o + 256].rearrange("p (h d) -> p h d", h=8), 8, DIFF_QK, t,
                             MLA_ROPE // 2, DIFF_ROT // 2, tmp)

            vector_stage(rope_program)
            turn_stage(lambda t, i: q96[:, t, i, :], HEADS, MLA_QK, qT)
            turn_stage(lambda t, i: k96[:, t, i, :], HEADS, MLA_QK, kT)
            out8 = mixed.rearrange("p t (h d) -> p t h d", d=HD)
            masks = {n: table(n).rearrange("p (t k) -> p t k", t=TILES) for n in ("chunk_mask", "causal_mask")}

            def chunk_bias(t, keys):
                return bc(masks["chunk_mask"][:, t, 0:keys], (P, HEADS, keys), 1)

            attend_stage(HEADS, MLA_QK, qT, kT, lambda j, i: kv[:, j, i, MLA_NOPE:], MLA_QK ** -0.5, chunk_bias,
                         lambda t: out8[:, t, 0:8, :], prob, probT)
            d0 = MLA_Q + MLA_KV + MLA_ROPE
            turn_stage(lambda t, i: z[:, t, d0 + 32 * i:d0 + 32 * i + 32], HEADS, DIFF_QK, qT)
            turn_stage(lambda t, i: z[:, t, d0 + 256 + 32 * i:d0 + 256 + 32 * i + 32], HEADS, DIFF_QK, kT)
            lam = small[:, 500:501]

            with stage("chain", "asked", "answered") as ((chain, asked, answered), block):
                w = small[:, 128:192].rearrange("p (j d) -> p j d", j=2)
                lams = p1("lam").rearrange("p (j i d) -> p j i d", j=2, i=2)

                @block.vector
                def _(dve):
                    link = Chain(dve, chain)
                    link(V.tensor_tensor(w, lams[:, :, 0, :], lams[:, :, 1, :], ALU.mult))
                    V.tensor_reduce(small[:, 192:194], w, AX, ALU.add).then_inc(asked, 1)
                    dve.wait_ge(answered, 1)
                    link(V.tensor_tensor(small[:, 196:197], small[:, 194:195], small[:, 195:196], ALU.subtract))
                    link(V.tensor_scalar(lam, small[:, 196:197], lam_init, None, ALU.add))

                @block.scalar
                def _(act):
                    act.wait_ge(asked, 1)
                    S.activation(small[:, 194:196], small[:, 192:194], ACT.Exp).then_inc(answered, 1)

            def diff_combine(link, t, res, total):
                both = region(base, HEADS, HD)
                link(V.tensor_tensor(both, res, bc(total, (P, HEADS, HD), 2), ALU.mult))
                pair = both.rearrange("p (h j) d -> p h j d", j=2)
                odd = region(base + 512, DIFF_HEADS, HD)
                link(V.tensor_scalar(odd, pair[:, :, 1, :], lam, None, ALU.mult))
                link(V.tensor_tensor(out8[:, t, 8:12, :], pair[:, :, 0, :], odd, ALU.subtract))

            attend_stage(HEADS, DIFF_QK, qT, kT,
                         lambda j, i: z[:, j, d0 + 512 + (i // 2) * HD:d0 + 512 + (i // 2 + 1) * HD],
                         DIFF_QK ** -0.5, chunk_bias, None, prob, probT, diff_combine)
            rms_stage([(out8[:, t, 8:12, :], out8[:, t, 8:12, :], 1e-6, [bc(p1("sub_g"), (P, 4, HD), 1)])
                       for t in range(TILES)], region(base, 2048))
            f0 = d0 + 768
            turn_stage(lambda t, i: z[:, t, f0 + HD * i:f0 + HD * i + HD], FOX_HEADS, HD, qT)
            turn_stage(lambda t, i: z[:, t, f0 + 256 + HD * i:f0 + 256 + HD * i + HD], FOX_HEADS, HD, kT)
            log_f = small[:, 256:264].rearrange("p (t h) -> p t h", t=TILES)
            cum = small[:, 264:272].rearrange("p (t h) -> p t h", t=TILES)
            fox = region(base, TILES, FOX_HEADS, SEQ)

            with stage("chain", "asked", "answered") as ((chain, asked, answered), block):
                x, n, e, m = (small[:, 128 + 8 * i:136 + 8 * i] for i in range(4))

                @block.vector
                def _(dve):
                    link = Chain(dve, chain)
                    link(V.tensor_tensor(x.rearrange("p (t h) -> p t h", t=TILES), z[:, :, f0 + 768:f0 + 772],
                                         bc(p1("fox_b"), (P, TILES, 4), 1), ALU.add))
                    link(V.tensor_scalar(n, x, -1.0, None, ALU.mult))
                    V.tensor_tensor(n, n, x, ALU.min).then_inc(asked, 1)
                    link(V.tensor_scalar(m, x, 0.0, None, ALU.min))
                    for t in range(TILES):
                        link(V.tensor_scalar(out8[:, t, 8:12, :], out8[:, t, 8:12, :], 1.0 - lam_init, None,
                                             ALU.mult))
                    dve.wait_ge(answered, 2)
                    link(V.tensor_tensor(small[:, 256:264], m, e, ALU.subtract))

                @block.scalar
                def _(act):
                    act.wait_ge(asked, 1)
                    S.activation(e, n, ACT.Exp).then_inc(answered, 1)
                    act.wait_ge(answered, 1)
                    S.activation(e, e, ACT.Ln, bias=1.0).then_inc(answered, 1)

            with stage("summed", "chain") as ((summed, chain), block):
                @block.tensor
                def _(pe):
                    T.matmul(ps[:, 0, 0:4], upto, log_f[:, 0, :], start=True, stop=True)
                    T.matmul(ps[:, 1, 0:4], ones, log_f[:, 0, :], start=True, stop=False)
                    T.matmul(ps[:, 1, 0:4], upto, log_f[:, 1, :], start=False, stop=True).then_inc(summed, 1)
                    for i in range(FOX_HEADS):
                        f = [log_f[:, t, i:i + 1].broadcast_to((P, P)) for t in range(TILES)]
                        row = ps[:, 2 + i, :]
                        T.matmul(row[:, 0:P], f[0], upto, start=True, stop=True)
                        T.matmul(row[:, P:SEQ], f[0], ones, start=True, stop=False)
                        T.matmul(row[:, P:SEQ], f[1], upto, start=False, stop=True).then_inc(summed, 1)

                @block.vector
                def _(dve):
                    link = Chain(dve, chain)
                    dve.wait_ge(summed, 1)
                    link(V.tensor_copy(cum, ps[:, 0:2, 0:4]))
                    for i in range(FOX_HEADS):
                        dve.wait_ge(summed, i + 2)
                        for t in range(TILES):
                            link(V.tensor_scalar(fox[:, t, i, :], ps[:, 2 + i, 0:SEQ], -1.0, cum[:, t, i:i + 1],
                                                 ALU.mult, ALU.add))
                            link(V.tensor_tensor(fox[:, t, i, :], fox[:, t, i, :], masks["causal_mask"][:, t, :],
                                                 ALU.add))
            attend_stage(FOX_HEADS, HD, qT, kT, lambda j, i: z[:, j, f0 + 512 + HD * i:f0 + 512 + HD * (i + 1)],
                         HD ** -0.5, lambda t, keys: fox[:, t, :, 0:keys],
                         lambda t: out8[:, t, 12:16, :], prob, probT)
            mix = output_stage(plan[l]["out"])
            layer_norm_stage(1e-5, p1("ln1_g"), p1("ln1_b"), mix)
            if stop == f"ln1_{l}":
                finish_here()
                return
            turn_h()
            rw = region(0, DC, N_EXPERTS)
            load_stage([(rw, a["router_w"].rearrange("(c p) e -> p c e", p=P))])
            router_stage(rw, N_EXPERTS)
            with stage("scores") as ((scores,), block):
                @block.scalar
                def _(act):
                    S.activation(small[:, 0:32].rearrange("p (t e) -> p t e", t=TILES), ps[:, 0:2, 0:16],
                                 ACT.Sigmoid).then_inc(scores, 1)
            vector_stage(route1)
            y = experts_stage(plan[l]["experts"])
            layer_norm_stage(1e-5, p1("ln2_g"), p1("ln2_b"), y)
            if stop == f"ln2_{l}":
                finish_here()
                return
        plan2 = plan[DEPTH]
        PAR2 = {"norm_g": (0, D), "mod_a": (1024, D), "rec_g": (2048, 512), "att_g": (2560, 512), "q_g": (3072, 64),
                "k_g": (3136, 64), "idx_g": (3200, 64), "idx_b": (3264, 64), "route_b": (3328, 20),
                "room": (3400, 1720)}
        p2 = lambda name: par_at(PAR2, name)
        room = p2("room")
        z_n = TILES * IN2
        mod = region(0, 6 * D)
        cond = small[:, 0:DC]
        load_stage([(p2("norm_g"), every(a["norm1_g_2"][0], D)), (p2("rec_g"), every(a["rec_out_g_2"][0], 512)),
                    (p2("att_g"), every(a["attn_out_g_2"][0], 512)), (p2("q_g"), every(a["q_norm_g_2"][0], 64)),
                    (p2("k_g"), every(a["k_norm_g_2"][0], 64)), (p2("idx_g"), every(a["idx_k_norm_g_2"][0], 64)),
                    (p2("idx_b"), every(a["idx_k_norm_b_2"][0], 64)),
                    (p2("route_b")[:, 0:4], every(a["b_rg_2"][0], 4)),
                    (p2("route_b")[:, 4:20], every(a["b_re_2"][0], 16)),
                    (cond, a["c_2"].rearrange("o (c p) -> p (o c)", p=P)),
                    (mod, every(a["b_ada_2"][0], 6 * D))])
        with stage("cond_done", "group_done", "added") as ((cond_done, group_done, added), block):
            units = plan2["ada"]

            @block.scalar
            def _(act):
                S.activation(small[:, 8:16], cond, ACT.Silu).then_inc(cond_done, 1)

            @block.sync
            def _(sp):
                ring.feed(sp, ring.after(units[-1]))

            @block.tensor
            def _(pe):
                pe.wait_ge(cond_done, 1)
                for i, u in enumerate(units):
                    w = ring.view(u, DC)
                    pe.wait_ge(landed[u % SLOTS], ring.landings(u))
                    if i >= BANKS:
                        pe.wait_ge(added, i - BANKS + 1)
                    for c in range(DC):
                        last = T.matmul(ps[:, i % BANKS, :], small[:, 8 + c:9 + c].broadcast_to((P, P)), w[:, c, :],
                                        start=c == 0, stop=c == DC - 1)
                    last.then_inc(group_done, 1)
                    pe.wait_ge(group_done, i + 1)
                    pe.sem_inc(unit_used, ring.after(u) - ring.used)
                    ring.used = ring.after(u)

            @block.vector
            def _(dve):
                for i in range(len(units)):
                    dve.wait_ge(group_done, i + 1)
                    part = mod[:, 512 * i:512 * i + 512]
                    V.tensor_tensor(part, part, ps[:, i % BANKS, :], ALU.add).then_inc(added, 1)

        def modulated_stage(gain, scale, shift, out, squares):
            rms_stage([(h[:, t, :].unsqueeze(1), out[:, t, :].unsqueeze(1), 1e-6, [gain.unsqueeze(1)])
                       for t in range(TILES)], squares)

            def modulate(link):
                for t in range(TILES):
                    link(V.scalar_tensor_tensor(squares[:, 0:D], scale, 1.0, out[:, t, :], ALU.add, ALU.mult))
                    link(V.tensor_tensor(out[:, t, :], squares[:, 0:D], shift, ALU.add))

            vector_stage(modulate)

        u_rows = region(6 * D, TILES, D)
        with stage("kept") as ((kept,), block):
            @block.sync
            def _(sp):
                sp.dma_start(scratch["mod"].rearrange("(o n) -> o n", o=1), mod[0:1, 2 * D:6 * D]).then_inc(kept, 16)
                sp.wait_ge(kept, 16)
        modulated_stage(p2("norm_g"), mod[:, D:2 * D], mod[:, 0:D], u_rows, region(8 * D, TILES * D))
        turn_stage(lambda t, c: u_rows[:, t, c * P:(c + 1) * P], DC, P, hT)
        z = region(0, TILES, IN2)
        project_stage(hT, DC, [(u, 0, min(512, IN2 - 512 * i), lambda t, i=i: z[:, t, 512 * i:min(512 * i + 512, IN2)])
                               for i, u in enumerate(plan2["in"])])

        k_rows = region(z_n, TILES, 512)
        recT = region(z_n + 2048, 2, REC_HEADS, SEQ)
        spread, q_spread = region(z_n, TILES, LEVELS, P), region(z_n + 4096, TILES, LEVELS, P)
        attnT = region(z_n + 6144, 3, P)
        logits = region(z_n + 4096, 2, 512)
        lb, rest = region(z_n + 5120, 512), region(z_n + 5632, 512)
        load_stage([(logits[:, i, :], every(a["lb_logits_2"][i], 512)) for i in range(2)])
        with stage("chain", "asked", "answered") as ((chain, asked, answered), block):
            @block.scalar
            def _(act):
                S.activation(k_rows, z[:, :, 512:1024], ACT.Sigmoid).then_inc(answered, 1)
                act.wait_ge(asked, 1)
                S.activation(logits, logits, ACT.Exp).then_inc(answered, 1)
                S.activation(z[:, :, 0:512], z[:, :, 0:512], ACT.Silu).then_inc(answered, 1)
                act.wait_ge(asked, 3)
                S.activation(z[:, :, 512:1024], z[:, :, 512:1024], ACT.Ln).then_inc(answered, 1)

            @block.vector
            def _(dve):
                link = Chain(dve, chain)
                link(V.tensor_tensor(lb, logits[:, 0, :], logits[:, 1, :], ALU.max))
                V.tensor_tensor(logits, logits, bc(lb, (P, 2, 512), 1), ALU.subtract).then_inc(asked, 1)
                dve.wait_ge(answered, 2)
                link(V.tensor_tensor(rest, logits[:, 0, :], logits[:, 1, :], ALU.add))
                link(V.reciprocal(rest, rest))
                link(V.tensor_tensor(lb, logits[:, 0, :], rest, ALU.mult))
                link(V.tensor_scalar(rest, lb, -1.0, 1.0, ALU.mult, ALU.add))
                link(V.tensor_tensor(k_rows, k_rows, bc(rest, (P, TILES, 512), 1), ALU.mult))
                V.tensor_tensor(z[:, :, 512:1024], k_rows, bc(lb, (P, TILES, 512), 1), ALU.add).then_inc(asked, 1)
                dve.wait_ge(asked, 2)
                V.tensor_scalar(k_rows, z[:, :, 512:1024], -1.0, 1.0, ALU.mult, ALU.add).then_inc(asked, 1)
        turn_stage(lambda t, i: z[:, t, i * P:(i + 1) * P], REC_HEADS, P, recT[:, 0])
        turn_stage(lambda t, i: k_rows[:, t, i * P:(i + 1) * P], REC_HEADS, P, recT[:, 1])
        spans, last_span, level_mask = (table(x) for x in ("spans", "last_span", "level_mask"))
        for i in range(REC_HEADS):
            names = ("spanned", "grown", "spread_done", "paired", "chain", "masked", "summed")
            with stage(*names) as ((spanned, grown, spread_done, paired, chain, masked, summed), block):
                qT, kT = recT[:, 0, i, :], recT[:, 1, i, :]
                cols = slice(i * P, (i + 1) * P)

                @block.tensor
                def _(pe):
                    for t in range(TILES):
                        lf = z[:, t, 512 + i * P:512 + (i + 1) * P]
                        T.matmul(ps[:, 2 * t, :], lf, spans[:, 0:512], start=True, stop=True)
                        if t == 0:
                            last = T.matmul(ps[:, 1, :], lf, spans[:, 512:1024], start=True, stop=True)
                        else:
                            T.matmul(ps[:, 3, 0:384], lf, spans[:, 512:896], start=True, stop=True)
                            last = T.matmul(ps[:, 3, 384:512], lf, last_span, start=True, stop=True)
                        last.then_inc(spanned, 1)
                    for t in range(TILES):
                        pe.wait_ge(spread_done, 2 * t + 2)
                        for l in range(LEVELS - 1):
                            T.matmul(ps[:, 4 + 2 * t + l // 4, (l % 4) * P:(l % 4 + 1) * P], spread[:, t, l, :],
                                     q_spread[:, t, l, :], start=True, stop=True)
                        tok = slice(t * P, (t + 1) * P)
                        T.matmul(ps[:, 5 + 2 * t, 3 * P:], kT[:, tok], qT[:, tok], start=True, stop=True)\
                            .then_inc(paired, 1)
                    T.matmul(ps[:, 0, 0:P], spread[:, 0, LEVELS - 1, :], q_spread[:, 1, LEVELS - 1, :],
                             start=True, stop=True).then_inc(paired, 1)
                    pe.wait_ge(masked, 3)
                    v = [z[:, t, 1024 + i * P:1024 + (i + 1) * P] for t in range(TILES)]
                    T.matmul(ps[:, 1, 0:P], attnT[:, 0, :], v[0], start=True, stop=True)
                    T.matmul(ps[:, 1, P:2 * P], attnT[:, 2, :], v[0], start=True, stop=False)
                    T.matmul(ps[:, 1, P:2 * P], attnT[:, 1, :], v[1], start=False, stop=True).then_inc(summed, 1)

                @block.scalar
                def _(act):
                    for t in range(TILES):
                        act.wait_ge(spanned, t + 1)
                        S.activation(spread[:, t, :, :].rearrange("p l x -> p (l x)"),
                                     ps[:, 2 * t:2 * t + 2, :].rearrange("p b n -> p (b n)"), ACT.Exp)\
                            .then_inc(grown, 1)
                    act.wait_ge(summed, 1)
                    S.activation(mixed[:, :, cols], ps[:, 1, 0:2 * P].rearrange("p (t v) -> p t v", t=TILES),
                                 ACT.Copy).then_inc(grown, 1)

                @block.vector
                def _(dve):
                    link = Chain(dve, chain)
                    for t in range(TILES):
                        tok = slice(t * P, (t + 1) * P)
                        dve.wait_ge(grown, t + 1)
                        V.tensor_tensor(q_spread[:, t], spread[:, t], bc(qT[:, tok], (P, LEVELS, P), 1), ALU.mult)\
                            .then_inc(spread_done, 1)
                        dve.wait_ge(spread_done, 2 * t + 1)
                        V.tensor_tensor(spread[:, t], spread[:, t], bc(kT[:, tok], (P, LEVELS, P), 1), ALU.mult)\
                            .then_inc(spread_done, 1)
                    for t in range(TILES):
                        dve.wait_ge(paired, t + 1)
                        picked = room[:, 0:LEVELS * P]
                        link(V.tensor_tensor(picked, ps[:, 4 + 2 * t:6 + 2 * t, :].rearrange("p b n -> p (b n)"),
                                             level_mask, ALU.mult))
                        V.tensor_reduce(attnT[:, t, :], picked.rearrange("p (l x) -> p x l", l=LEVELS), AX, ALU.add)\
                            .then_inc(masked, 1)
                        dve.wait_ge(masked, t + 1)
                    dve.wait_ge(paired, 3)
                    V.tensor_copy(attnT[:, 2, :], ps[:, 0, 0:P]).then_inc(masked, 1)

        rec = mixed[:, :, 0:512].rearrange("p t (h v) -> p t h v", v=REC_D)
        rec_gain = p2("rec_g").rearrange("p (h v) -> p h v", v=REC_D)
        with stage("gated") as ((gated,), block):
            @block.scalar
            def _(act):
                S.activation(z[:, :, 1536:2048], z[:, :, 1536:2048], ACT.Silu).then_inc(gated, 1)
        rms_stage([(rec[:, t], rec[:, t], 1e-6,
                    [rec_gain, z[:, t, 1536:2048].rearrange("p (h v) -> p h v", v=REC_D)]) for t in range(TILES)] +
                  [(z[:, t, o:o + 512].rearrange("p (h d) -> p h d", d=HD),
                    z[:, t, o:o + 512].rearrange("p (h d) -> p h d", d=HD), 1e-6, [bc(p2(g), (P, HEADS, HD), 1)])
                   for t in range(TILES) for o, g in ((2048, "q_g"), (2560, "k_g"))], region(z_n, 2048))

        bias_rows = region(z_n, HEADS, 2 * SEQ)
        buckets, rel = room[0:BUCKETS, 0:2 * SEQ], room[0:BUCKETS, 512:520]
        load_stage([(buckets, a["bucket"]), (rel, a["rel_bias_2"])])
        with stage("spread_rows", "copied_rows", "stored") as ((spread_rows, copied_rows, stored), block):
            @block.tensor
            def _(pe):
                for i in range(HEADS):
                    T.matmul(ps[:, i, :], rel[:, i:i + 1].broadcast_to((BUCKETS, P)), buckets,
                             start=True, stop=True).then_inc(spread_rows, 1)

            @block.scalar
            def _(act):
                for i in range(HEADS):
                    act.wait_ge(spread_rows, i + 1)
                    S.activation(bias_rows[:, i, :], ps[:, i, :], ACT.Copy).then_inc(copied_rows, 1)

            @block.sync
            def _(sp):
                sp.wait_ge(copied_rows, HEADS)
                flat = scratch["bias_rows"]
                sp.dma_start(flat[0:HEADS * P * 2 * SEQ].rearrange("(h p n) -> p h n", h=HEADS, p=P), bias_rows).then_inc(stored, 16)
                sp.wait_ge(stored, 16)
                for t in range(TILES):
                    for i in range(HEADS):
                        at = i * P * 2 * SEQ + SEQ - 1 - P * t
                        askew = flat[at:at + P * (2 * SEQ - 1)]\
                            .rearrange("(p n) -> p n", n=2 * SEQ - 1)[:, 0:SEQ]
                        sp.dma_start(z[:, t, i * SEQ:(i + 1) * SEQ], askew).then_inc(stored, 16)
                sp.wait_ge(stored, 16 * (1 + TILES * HEADS))

        work = room[:, 600:600 + TILES * SEQ].rearrange("p (t k) -> p t k", t=TILES)
        iqT, ikT = region(z_n + 4096, HEADS, SEQ), region(z_n + 6144, 1, SEQ)

        with stage("chain", "moment", "rooted") as ((chain, moment, rooted), block):
            @block.vector
            def _(dve):
                link = Chain(dve, chain)
                for t in range(TILES):
                    link(V.bn_stats(small[:, 8 * t:8 * t + 6], z[:, t, 4096:4160]))
                    link(V.bn_aggr(small[:, 16 + 2 * t:18 + 2 * t], small[:, 8 * t:8 * t + 6]))
                V.tensor_scalar(small[:, 20:22], small[:, 17:20:2], 1e-6, None, ALU.add).then_inc(moment, 1)
                dve.wait_ge(rooted, 1)
                link(V.reciprocal(small[:, 24:26], small[:, 22:24]))
                for t in range(TILES):
                    x = z[:, t, 4096:4160]
                    link(V.tensor_scalar(x, x, small[:, 16 + 2 * t:17 + 2 * t], small[:, 24 + t:25 + t],
                                         ALU.subtract, ALU.mult))
                    link(V.tensor_tensor(x, x, p2("idx_g"), ALU.mult))
                    link(V.tensor_tensor(x, x, p2("idx_b"), ALU.add))
                    link(V.tensor_scalar(z[:, t, 4160:4168], z[:, t, 4160:4168], HD ** -0.5 * HEADS ** -0.5, None,
                                         ALU.mult))

            @block.scalar
            def _(act):
                act.wait_ge(moment, 1)
                S.activation(small[:, 22:24], small[:, 20:22], ACT.Sqrt).then_inc(rooted, 1)
        turn_stage(lambda t, i: z[:, t, 3584 + HD * i:3584 + HD * (i + 1)], HEADS, HD, iqT)
        turn_stage(lambda t, i: z[:, t, 4096:4160], 1, HD, ikT)
        with stage("scored", "chain") as ((scored, chain), block):
            @block.tensor
            def _(pe):
                for t in range(TILES):
                    for i in range(HEADS):
                        last = T.matmul(ps[:, 4 * t + i // 2, (i % 2) * SEQ:(i % 2 + 1) * SEQ],
                                        iqT[0:HD, i, t * P:(t + 1) * P], ikT[0:HD, 0, :], start=True, stop=True)
                    last.then_inc(scored, 1)

            @block.vector
            def _(dve):
                link = Chain(dve, chain)
                weighed = region(z_n + 2048, HEADS, SEQ)
                best = small[:, 0:8]
                for t in range(TILES):
                    dve.wait_ge(scored, t + 1)
                    link(V.scalar_tensor_tensor(weighed, ps[:, 4 * t:4 * t + 4, :]
                                                .rearrange("p b (j k) -> p (b j) k", j=2), 0.0,
                                                bc(z[:, t, 4160:4168], (P, HEADS, SEQ), 2), ALU.max, ALU.mult))
                    link(V.tensor_reduce(work[:, t, :], weighed.rearrange("p h k -> p k h"), AX, ALU.add))
                    link(V.tensor_tensor(work[:, t, :], work[:, t, :], masks["chunk_mask"][:, t, :], ALU.add))
                    for _ in range(TOPK // 8):
                        link(V.max(best, work[:, t, :]))
                        link(V.match_replace(work[:, t, :], best, work[:, t, :], -3e38))
                    link(V.tensor_scalar(work[:, t, :], work[:, t, :], -2e38, NEG, ALU.is_gt, ALU.mult))
                    bias = z[:, t, 0:HEADS * SEQ].rearrange("p (h k) -> p h k", k=SEQ)
                    link(V.tensor_tensor(bias, bias, bc(work[:, t, :], (P, HEADS, SEQ), 1), ALU.add))
        qT, kT, prob = (region(z_n + 2048 * i, HEADS, SEQ) for i in range(3))
        probT = par[:, 0:2048].rearrange("p (j q) -> p j q", q=P)
        turn_stage(lambda t, i: z[:, t, 2048 + HD * i:2048 + HD * (i + 1)], HEADS, HD, qT)
        turn_stage(lambda t, i: z[:, t, 2560 + HD * i:2560 + HD * (i + 1)], HEADS, HD, kT)
        attend_stage(HEADS, HD, qT, kT, lambda j, i: z[:, j, 3072 + HD * i:3072 + HD * (i + 1)], HD ** -0.5,
                     lambda t, keys: z[:, t, 0:HEADS * SEQ].rearrange("p (h k) -> p h k", k=SEQ)[:, :, 0:keys],
                     lambda t: out8[:, t, 8:16, :], prob, probT)
        rms_stage([(out8[:, t, 8:16, :], out8[:, t, 8:16, :], 1e-6,
                    [p2("att_g").rearrange("p (h d) -> p h d", d=HD)]) for t in range(TILES)], region(z_n, 2048))
        if stop in ("mixed2",):
            vector_stage(lambda link: link(V.tensor_copy(h[:, :, :], mixed)))
            finish_here()
            return
        mix = output_stage(plan2["out"])

        def kept_mod(i):
            return every(scratch["mod"][i * D:(i + 1) * D], D)

        def add_gated(gate, rows):
            def program(link):
                for t in range(TILES):
                    link(V.tensor_tensor(rows[:, t, :], rows[:, t, :], gate, ALU.mult))
                    link(V.tensor_tensor(h[:, t, :], h[:, t, :], rows[:, t, :], ALU.add))
            vector_stage(program)

        rw = region(8 * D, DC, 20)
        load_stage([(room[:, 0:D], kept_mod(0)), (p2("norm_g"), every(a["norm2_g_2"][0], D)),
                    (p2("mod_a"), kept_mod(1)), (par[:, 2048:3072], kept_mod(2)),
                    (rw[:, :, 0:4], a["w_rg_2"][0].rearrange("(c p) e -> p c e", p=P)),
                    (rw[:, :, 4:20], a["w_re_2"][0].rearrange("(c p) e -> p c e", p=P))])
        add_gated(room[:, 0:D], mix)
        modulated_stage(p2("norm_g"), par[:, 2048:3072], p2("mod_a"), u_rows, region(4 * D, TILES * D))
        turn_stage(lambda t, c: u_rows[:, t, c * P:(c + 1) * P], DC, P, hT)
        router_stage(rw, 20)
        load_stage([(room[:, 0:D], kept_mod(3))])

        with stage("chain", "asked", "answered") as ((chain, asked, answered), block):
            base = 288

            @block.scalar
            def _(act):
                for t in range(TILES):
                    act.wait_ge(asked, 2 * t + 1)
                    S.activation(small[:, 24:28], small[:, 20:24], ACT.Exp).then_inc(answered, 1)
                    act.wait_ge(asked, 2 * t + 2)
                    S.activation(small[:, 29:30], small[:, 28:29], ACT.Exp).then_inc(answered, 1)

            @block.vector
            def _(dve):
                link = Chain(dve, chain)
                for t in range(TILES):
                    logit = small[:, 0:20]
                    link(V.tensor_tensor(logit, ps[:, t, 0:20], p2("route_b"), ALU.add))
                    group, vals = first_of_groups(link, logit[:, 0:4], small[:, 80:112])
                    V.tensor_scalar(small[:, 20:24], logit[:, 0:4], vals[:, 0:1], None, ALU.subtract)\
                        .then_inc(asked, 1)
                    keep_group(link, small[:, 112:128], logit[:, 4:20], group, small[:, 128:160])
                    vals, hot = top2(link, small[:, 112:128], small[:, 160:224])
                    V.tensor_tensor(small[:, 28:29], vals[:, 1:2], vals[:, 0:1], ALU.subtract).then_inc(asked, 1)
                    dve.wait_ge(answered, 2 * t + 2)
                    link(V.tensor_reduce(small[:, 30:31], small[:, 24:28], AX, ALU.add))
                    link(V.tensor_scalar(small[:, 31:32], small[:, 29:30], 1.0, None, ALU.add))
                    link(V.tensor_tensor(small[:, 32:33], small[:, 30:31], small[:, 31:32], ALU.mult))
                    link(V.reciprocal(small[:, 33:34], small[:, 32:33]))
                    link(V.tensor_tensor(small[:, 34:35], small[:, 33:34], small[:, 29:30], ALU.mult))
                    link(V.tensor_scalar(small[:, 36:52], hot[:, 0, :], small[:, 33:34], None, ALU.mult))
                    link(V.scalar_tensor_tensor(gates[:, t, :], hot[:, 1, :], small[:, 34:35], small[:, 36:52],
                                                ALU.mult, ALU.add))
        y = experts_stage(plan2["experts"])
        add_gated(room[:, 0:D], y)
        finish_here()


def kernel(**inputs):
    import numpy as _np
    import concourse.bacc as _bacc
    from concourse import mybir as _mybir
    from concourse.bass_utils import run_bass_kernel_spmd as _run

    nc = _bacc.Bacc("TRN2", target_bir_lowering=False, num_devices=1)
    arrays, aps = {}, {}
    given = dict(inputs)
    given["tab"] = tables()
    given["bucket"] = bucket_table()
    for name, value in given.items():
        value = _np.ascontiguousarray(value)
        arrays[f"in_{name}"] = value
        aps[name] = nc.dram_tensor(f"in_{name}", value.shape, _mybir.dt.from_np(value.dtype),
                                   kind="ExternalInput").ap()
    out = nc.dram_tensor("out_0", (SEQ, D), F32, kind="ExternalOutput").ap()
    scratch = {n: nc.dram_tensor(f"scratch_{n}", s, F32, kind="Internal").ap() for n, s in SCRATCH.items()}
    build(nc, aps, scratch, [out])
    r = _run(nc, [arrays], core_ids=[0])
    return r.results[0]["out_0"].reshape(1, SEQ, D)
```

```python
from contextlib import ExitStack, contextmanager
import math

import numpy as np

import concourse.bass as bass
from concourse import mybir

F32 = mybir.dt.float32
I32 = mybir.dt.int32
U32 = mybir.dt.uint32
ALU = mybir.AluOpType
ACT = mybir.ActivationFunctionType
AX = mybir.AxisListType.X

P = 128
SEQ = 256
TILES = SEQ // P
D = 1024
DC = D // P
DEPTH = 2
HEADS = 8
CHUNK = 64
NEG = -1e30

MLA_Q, MLA_KV, MLA_ROPE, MLA_NOPE = 384, 256, 32, 64
MLA_QK = MLA_NOPE + MLA_ROPE
DIFF_QK, DIFF_ROT, DIFF_HEADS = 32, 8, 4
FOX_HEADS = 4
HD = 64
IN1 = 2212
IN2 = 4168
THETA = 500000.0
ALPHA = (2 * DEPTH) ** 0.25

REC_HEADS, REC_D = 4, 128
TOPK = 64
BUCKETS = 32
LEVELS = 8

N_EXPERTS, N_GROUPS, D_EXPERT = 16, 4, 512
EC = D_EXPERT // P
PAIRS = N_EXPERTS // 2
PADDED = N_EXPERTS + 2
CAP = 64

SLOT = 4096
SLOTS = 6
BANKS, BANK = 8, 512

TAB = {}
_at = 0
for _name, _n in (("ident", P), ("upto", P), ("before", P), ("ones", P), ("chunk_mask", TILES * SEQ),
                  ("causal_mask", TILES * SEQ), ("spans", LEVELS * P), ("last_span", P),
                  ("level_mask", LEVELS * P), ("freq_mla", MLA_ROPE // 2), ("freq_diff", DIFF_ROT // 2),
                  ("iota", CAP)):
    TAB[_name] = (_at, _n)
    _at += _n
TAB_N = _at


def tables():
    tab = np.zeros((P, TAB_N), np.float32)

    def put(name, value):
        a, n = TAB[name]
        tab[:, a:a + n] = np.asarray(value, np.float32).reshape(P, n)

    p = np.arange(P)
    put("ident", np.eye(P))
    put("upto", p[:, None] <= p[None, :])
    put("before", p[:, None] < p[None, :])
    put("ones", np.ones((P, P)))
    k = np.arange(SEQ)
    q = p[:, None, None] + P * np.arange(TILES)[None, :, None]
    put("chunk_mask", np.where(k[None, None] // CHUNK <= q // CHUNK, 0.0, NEG))
    put("causal_mask", np.where(k[None, None] <= q, 0.0, NEG))
    u, x = p[:, None, None], p[None, None, :]
    size = (2 ** np.arange(LEVELS))[None, :, None]
    mid = (x // (2 * size)) * (2 * size) + size
    right = x >= mid
    put("spans", np.where(right, (mid <= u) & (u <= x), (x < u) & (u < mid)))
    put("last_span", p[:, None] <= p[None, :])
    s, t = p[:, None, None], p[None, None, :]
    size = (2 ** np.arange(LEVELS - 1))[None, :, None]
    pair = (s // (2 * size) == t // (2 * size)) & (s // size % 2 == 0) & (t // size % 2 == 1)
    put("level_mask", np.concatenate([pair, (s == t)], axis=1))
    f = lambda n: np.float32(THETA) ** (-np.arange(0, n, 2, dtype=np.float32) / np.float32(n))
    put("freq_mla", np.broadcast_to(f(MLA_ROPE), (P, MLA_ROPE // 2)))
    put("freq_diff", np.broadcast_to(f(DIFF_ROT), (P, DIFF_ROT // 2)))
    put("iota", np.broadcast_to(np.arange(CAP), (P, CAP)))
    return tab


SCRATCH = {"mod": (4 * D,), "bias_rows": (HEADS * P * 2 * SEQ + 2 * SEQ,)}


def bucket_table():
    rel = np.arange(-(SEQ - 1), SEQ)
    half, exact, far = BUCKETS // 2, BUCKETS // 4, 128
    n = np.abs(rel)
    nf = np.maximum(n, 1).astype(np.float32)
    large = exact + (np.log(nf / np.float32(exact)) / np.float32(np.log(far / exact))
                     * np.float32(half - exact)).astype(np.int32)
    b = np.where(rel > 0, half, 0) + np.where(n < exact, n, np.minimum(large, half - 1))
    out = np.zeros((BUCKETS, 2 * SEQ), np.float32)
    out[b, np.arange(rel.size)] = 1.0
    return out


class Ring:

    def __init__(self, tensor, landed, unit_used, sources):
        self.tensor, self.landed, self.unit_used, self.sources = tensor, landed, unit_used, sources
        self.sent = 0
        self.used = 0

    def view(self, n, c):
        w = self.sources[n].shape[2]
        return self.tensor[:, n % SLOTS, 0:c * w].rearrange("p (c w) -> p c w", c=c)

    def landings(self, n):
        return 16 * sum(s is not None for s in self.sources[n % SLOTS:n + 1:SLOTS])

    def after(self, n):
        n += 1
        while n < len(self.sources) and self.sources[n] is None:
            n += 1
        return n

    def feed(self, sp, consumed):
        while self.sent < min(len(self.sources), consumed + SLOTS):
            n = self.sent
            source = self.sources[n]
            if source is not None:
                if n >= SLOTS:
                    sp.wait_ge(self.unit_used, n - SLOTS + 1)
                sp.dma_start(self.view(n, source.shape[1]), source).then_inc(self.landed[n % SLOTS], 16)
            self.sent += 1


def build(nc, a, scratch, outs, stop=None):
    ctx = ExitStack()
    with ctx:
        def sb(name, shape, dt=F32):
            return ctx.enter_context(nc.sbuf_tensor(name, shape, dt))

        ring_mem = sb("ring", [P, SLOTS, SLOT])
        tab = sb("tab", [P, TAB_N])
        h = sb("h", [P, TILES, D])
        hT = sb("hT", [P, DC, SEQ])
        par = sb("par", [P, 5120])
        ARENA = 14900
        arena = sb("arena", [P, ARENA])
        trig = sb("trig", [P, TILES, 2, 20])
        positions_i = sb("positions_i", [P, TILES], I32)
        small = sb("small", [P, 512])
        index = sb("index", [P, 16], U32)
        crowded = sb("crowded", [P, 1], I32)
        ps = ctx.enter_context(nc.psum_tensor("ps", [P, BANKS, BANK], F32))

        def table(name):
            at, n = TAB[name]
            return tab[:, at:at + n]

        ident, upto, before, ones = (table(x) for x in ("ident", "upto", "before", "ones"))

        def region(at, *dims):
            n = int(np.prod(dims))
            assert at + n <= ARENA, (at, dims)
            v = arena[:, at:at + n]
            if len(dims) == 1:
                return v
            names = "abcd"[:len(dims)]
            return v.rearrange(f"p ({' '.join(names)}) -> p {' '.join(names)}",
                               **{x: d for x, d in zip(names, dims)})

        mixed = hT[:, :, :].rearrange("p c t -> p (c t)").rearrange("p (t n) -> p t n", t=TILES)

        sources = []

        def unit(w, chunks, lo, hi):
            sources.append(w.rearrange("(c p) n -> p c n", p=P)[:, :, lo:hi])
            return len(sources) - 1

        def cut(w, chunks, cols, width):
            return [unit(w, chunks, x, min(x + width, cols)) for x in range(0, cols, width)]

        def expert_units(gate, up, down):
            while len(sources) % SLOTS:
                sources.append(None)
            first = len(sources)
            for pair in range(PAIRS):
                for w in (gate, up, down):
                    for e in (2 * pair, 2 * pair + 1):
                        unit(w[e], DC if w is not down else EC, 0, w.shape[2])
            return first

        plan = []
        for l in range(DEPTH):
            plan.append({
                "in": cut(a["w_in"][l], DC, IN1, 512),
                "uq": cut(a["mla_w_uq"][l], 3, 768, 768),
                "ukv": cut(a["mla_w_ukv"][l], 2, 1024, 1024),
                "out": cut(a["w_out"][l], DC, D, 512),
                "experts": expert_units(a["exp_w_gate"][l], a["exp_w_up"][l], a["exp_w_down"][l]),
            })
        plan.append({
            "ada": cut(a["w_ada_2"][0], DC, 6 * D, 512),
            "in": cut(a["w_in_2"][0], DC, IN2, 512),
            "out": cut(a["w_out_2"][0], DC, D, 512),
            "experts": expert_units(a["w1_2"][0], a["w3_2"][0], a["w2_2"][0]),
        })
        landed = [ctx.enter_context(nc.semaphore(f"landed{i}")) for i in range(SLOTS)]
        unit_used = ctx.enter_context(nc.semaphore("unit_used"))
        ring = Ring(ring_mem, landed, unit_used, sources)

        @contextmanager
        def stage(*names):
            with ExitStack() as s:
                sems = [s.enter_context(nc.semaphore(x)) for x in names]
                with nc.Block(no_gpsimd_drain=True) as block:
                    yield sems, block
                for x in sems:
                    nc.sync.sem_clear(x)

        class Chain:

            def __init__(self, eng, sem):
                self.eng, self.sem, self.n = eng, sem, 0

            def __call__(self, ins):
                ins.then_inc(self.sem, 1)
                self.n += 1
                self.eng.wait_ge(self.sem, self.n)

        V, S, G, T = nc.vector, nc.scalar, nc.gpsimd, nc.tensor

        def bc(x, dims, at):
            return x.unsqueeze(at).broadcast_to(tuple(dims))


        def load_stage(pairs):
            with stage("loaded") as ((loaded,), block):
                @block.scalar
                def _(act):
                    with nc.allow_non_contiguous_dma("small vectors, once"):
                        for dst, src in pairs:
                            act.dma_start(dst, src).then_inc(loaded, 16)
                    act.wait_ge(loaded, 16 * len(pairs))

        def every(x, n):
            return x.rearrange("(o n) -> o n", o=1).broadcast_to((P, n))

        def turn_stage(src, n, rows, dst):
            banks = (n + 1) // 2
            with stage("turned", "act_copied", "dve_copied") as ((turned, act_copied, dve_copied), block):
                @block.tensor
                def _(pe):
                    for b in range(banks):
                        if b >= BANKS:
                            pe.wait_ge((act_copied, dve_copied)[b % 2], (b - BANKS) // 2 + 1)
                        for i in range(2 * b, min(2 * b + 2, n)):
                            for t in range(TILES):
                                at = (i % 2) * SEQ + t * P
                                last = T.transpose(ps[0:rows, b % BANKS, at:at + P], src(t, i), ident)
                        last.then_inc(turned, 1)

                def copy(eng, b, sem, op):
                    i, m = 2 * b, min(2, n - 2 * b)
                    eng.wait_ge(turned, b + 1)
                    op(dst[0:rows, i:i + m, :], ps[0:rows, b % BANKS, 0:m * SEQ]
                       .rearrange("p (i t) -> p i t", i=m)).then_inc(sem, 1)

                @block.scalar
                def _(act):
                    for b in range(0, banks, 2):
                        copy(act, b, act_copied, lambda o, i: S.activation(o, i, ACT.Copy))

                @block.vector
                def _(dve):
                    for b in range(1, banks, 2):
                        copy(dve, b, dve_copied, V.tensor_copy)

        def project_stage(xT, chunks, jobs):
            with stage("group_done", "act_copied", "dve_copied") as ((group_done, act_copied, dve_copied), block):
                copied = (act_copied, dve_copied)
                signals, n = {}, 0
                for i, (u, *_) in enumerate(jobs):
                    for t in range(TILES):
                        if t == TILES - 1 and (i + 1 == len(jobs) or jobs[i + 1][0] != u):
                            signals[i, t] = (ring.unit_used, ring.after(u), ring.after(u) - ring.used)
                            ring.used = ring.after(u)
                        else:
                            n += 1
                            signals[i, t] = (group_done, n, 1)

                @block.sync
                def _(sp):
                    ring.feed(sp, ring.used)

                @block.tensor
                def _(pe):
                    for i, (u, lo, width, _) in enumerate(jobs):
                        w = ring.view(u, chunks)
                        pe.wait_ge(ring.landed[u % SLOTS], ring.landings(u))
                        for t in range(TILES):
                            if i >= BANKS // 2:
                                pe.wait_ge(copied[t], i - BANKS // 2 + 1)
                            for c in range(chunks):
                                last = T.matmul(ps[:, (TILES * i + t) % BANKS, 0:width],
                                                xT[:, c, t * P:(t + 1) * P], w[:, c, lo:lo + width],
                                                start=c == 0, stop=c == chunks - 1)
                            sem, _, by = signals[i, t]
                            last.then_inc(sem, by)

                def copy(eng, t, op):
                    for i, (_, _, width, dst) in enumerate(jobs):
                        sem, value, _ = signals[i, t]
                        eng.wait_ge(sem, value)
                        op(dst(t), ps[:, (TILES * i + t) % BANKS, 0:width]).then_inc(copied[t], 1)

                @block.scalar
                def _(act):
                    copy(act, 0, lambda o, i: S.activation(o, i, ACT.Copy))

                @block.vector
                def _(dve):
                    copy(dve, 1, V.tensor_copy)

        def layer_norm_stage(eps, gain, bias, mix=None):
            with stage("chain", "rooted", "moment") as ((chain, rooted, moment), block):
                stats, mv = small[:, 0:24].rearrange("p (t s) -> p t s", t=TILES), small[:, 24:28]

                @block.vector
                def _(dve):
                    link = Chain(dve, chain)
                    for t in range(TILES):
                        if mix is not None:
                            link(V.scalar_tensor_tensor(h[:, t, :], h[:, t, :], ALPHA, mix[:, t, :],
                                                        ALU.mult, ALU.add))
                        for j in range(2):
                            link(V.bn_stats(stats[:, t, 6 * j:6 * j + 6], h[:, t, 512 * j:512 * j + 512]))
                        link(V.bn_aggr(mv[:, 2 * t:2 * t + 2], stats[:, t, :]))
                    V.tensor_scalar(small[:, 28:30], mv[:, 1:4:2], eps, None, ALU.add).then_inc(moment, 1)
                    dve.wait_ge(rooted, 1)
                    link(V.reciprocal(small[:, 32:34], small[:, 30:32]))
                    for t in range(TILES):
                        link(V.tensor_scalar(h[:, t, :], h[:, t, :], mv[:, 2 * t:2 * t + 1],
                                             small[:, 32 + t:33 + t], ALU.subtract, ALU.mult))
                        link(V.tensor_tensor(h[:, t, :], h[:, t, :], gain, ALU.mult))
                        link(V.tensor_tensor(h[:, t, :], h[:, t, :], bias, ALU.add))

                @block.scalar
                def _(act):
                    act.wait_ge(moment, 1)
                    S.activation(small[:, 30:32], small[:, 28:30], ACT.Sqrt).then_inc(rooted, 1)

        def rms_stage(jobs, squares):
            with stage("chain", "rooted", "moment") as ((chain, rooted, moment), block):
                @block.vector
                def _(dve):
                    link = Chain(dve, chain)
                    for i, (x, out, eps, factors) in enumerate(jobs):
                        g, w = x.shape[1], x.shape[2]
                        sq = squares[:, 0:g * w].rearrange("p (g w) -> p g w", g=g)
                        link(V.tensor_tensor(sq, x, x, ALU.mult))
                        link(V.tensor_reduce(small[:, 0:g], sq, AX, ALU.add))
                        V.tensor_scalar(small[:, 32:32 + g], small[:, 0:g], 1.0 / w, eps, ALU.mult, ALU.add)\
                            .then_inc(moment, 1)
                        dve.wait_ge(rooted, i + 1)
                        link(V.reciprocal(small[:, 96:96 + g], small[:, 64:64 + g]))
                        link(V.tensor_tensor(out, x, bc(small[:, 96:96 + g], (P, g, w), 2), ALU.mult))
                        for f in factors:
                            link(V.tensor_tensor(out, out, f, ALU.mult))

                @block.scalar
                def _(act):
                    for i, (x, *_) in enumerate(jobs):
                        g = x.shape[1]
                        act.wait_ge(moment, i + 1)
                        S.activation(small[:, 64:64 + g], small[:, 32:32 + g], ACT.Sqrt).then_inc(rooted, 1)

        def attend_stage(heads, dh, qT, kT, value, scale, bias, out, prob, probT, combine=None):
            mx, total = small[:, 0:heads], small[:, 8:8 + heads]
            names = ("scored", "chain", "ready", "weighed", "turned", "copied", "mixed_v", "written")
            with stage(*names) as ((scored, chain, ready, weighed, turned, copied, mixed_v, written), block):
                def scores(t):
                    return ps[:, 4 * t:4 * t + heads // 2, :].rearrange("p b (j k) -> p (b j) k", j=2)

                def turned_p(t):
                    return ps[:, 4 * t:4 * t + (t + 1) * heads // 4, :].rearrange(
                        "p b (h q) -> p (b h) q", q=P)

                def result(t):
                    return ps[:, 2 + t, 0:heads * HD].rearrange("p (h d) -> p h d", h=heads)

                @block.tensor
                def _(pe):
                    for t in range(TILES):
                        keys = (t + 1) * P
                        for i in range(heads):
                            last = T.matmul(scores(t)[:, i, 0:keys], qT[0:dh, i, t * P:(t + 1) * P],
                                            kT[0:dh, i, 0:keys], start=True, stop=True)
                        last.then_inc(scored, 1)
                    for t in range(TILES):
                        pe.wait_ge(weighed, t + 1)
                        for j in range(t + 1):
                            for i in range(heads):
                                last = T.transpose(turned_p(t)[:, j * heads + i, :],
                                                   prob[:, i, j * P:(j + 1) * P], ident)
                        last.then_inc(turned, 1)
                        pe.wait_ge(copied, t + 1)
                        for i in range(heads):
                            for j in range(t + 1):
                                last = T.matmul(result(t)[:, i, :], probT[:, j * heads + i, :], value(j, i),
                                                start=j == 0, stop=j == t)
                        last.then_inc(mixed_v, 1)

                @block.scalar
                def _(act):
                    for t in range(TILES):
                        keys = (t + 1) * P
                        act.wait_ge(ready, t + 1)
                        S.activation(prob[:, 0:heads, 0:keys], prob[:, 0:heads, 0:keys], ACT.Exp)\
                            .then_inc(weighed, 1)
                        act.wait_ge(turned, t + 1)
                        if t:
                            act.wait_ge(mixed_v, t)
                        n = (t + 1) * heads
                        S.activation(probT[:, 0:n, :], turned_p(t), ACT.Copy).then_inc(copied, 1)

                @block.vector
                def _(dve):
                    link = Chain(dve, chain)
                    for t in range(TILES):
                        keys = (t + 1) * P
                        s = prob[:, 0:heads, 0:keys]
                        dve.wait_ge(scored, t + 1)
                        if t:
                            dve.wait_ge(turned, t)
                        link(V.scalar_tensor_tensor(s, scores(t)[:, :, 0:keys], scale, bias(t, keys),
                                                    ALU.mult, ALU.add))
                        link(V.tensor_reduce(mx, s, AX, ALU.max))
                        V.tensor_tensor(s, s, bc(mx, (P, heads, keys), 2), ALU.subtract).then_inc(ready, 1)
                        dve.wait_ge(weighed, t + 1)
                        link(V.tensor_reduce(total, s, AX, ALU.add))
                        link(V.reciprocal(total, total))
                        dve.wait_ge(mixed_v, t + 1)
                        if combine is None:
                            link(V.tensor_tensor(out(t), result(t), bc(total, (P, heads, HD), 2), ALU.mult))
                        else:
                            combine(link, t, result(t), total)


        def vector_stage(program):
            with stage("chain") as ((chain,), block):
                @block.vector
                def _(dve):
                    program(Chain(dve, chain))

        ang = small[:, 16:96].rearrange("p (t c f) -> p t c f", t=TILES, c=2)

        def trig_program(link):
            pos = small[:, 0:TILES]
            link(V.tensor_copy(pos, positions_i[:, :]))
            turns = small[:, 96:176].rearrange("p (t c f) -> p t c f", t=TILES, c=2)
            a0, n0 = TAB["freq_mla"][0], (MLA_ROPE + DIFF_ROT) // 2
            for t in range(TILES):
                link(V.tensor_scalar(ang[:, t, 1, :], tab[:, a0:a0 + n0], pos[:, t:t + 1], None, ALU.mult))
            magic = 1.5 * 2.0 ** 23
            two_pi = 2 * math.pi
            c1 = 6.28125
            c2 = float(np.float32(np.floor((two_pi - c1) * 2 ** 22) / 2 ** 22))
            c3 = two_pi - c1 - c2
            for t in range(TILES):
                x, y = ang[:, t, 1, :], turns[:, t, 1, :]
                link(V.tensor_scalar(y, x, 1 / two_pi, None, ALU.mult))
                link(V.tensor_scalar(y, y, magic, None, ALU.add))
                link(V.tensor_scalar(y, y, -magic, None, ALU.add))
                for c in (c1, c2, c3):
                    link(V.scalar_tensor_tensor(x, y, -c, x, ALU.mult, ALU.add))
                z = ang[:, t, 0, :]
                link(V.tensor_scalar(z, x, math.pi / 2, None, ALU.add))
                link(V.tensor_scalar(y, z, math.pi, -two_pi, ALU.is_gt, ALU.mult))
                link(V.tensor_tensor(z, z, y, ALU.add))
                link(V.tensor_scalar(ang[:, t, :, :], ang[:, t, :, :], 3.1415925, -3.1415925, ALU.min, ALU.max))

        def rope(link, x, heads, width, t, first, n, tmp):
            cos = bc(trig[:, t, 0, first:first + n], (P, heads, n), 1)
            sin = bc(trig[:, t, 1, first:first + n], (P, heads, n), 1)
            x1, x2 = x[:, :, 0:n], x[:, :, n:2 * n]
            y = tmp[:, 0:4 * heads * n].rearrange("p (i h n) -> p i h n", i=4, h=heads)
            link(V.tensor_tensor(y[:, 0], x1, cos, ALU.mult))
            link(V.tensor_tensor(y[:, 1], x2, sin, ALU.mult))
            link(V.tensor_tensor(y[:, 2], x2, cos, ALU.mult))
            link(V.tensor_tensor(y[:, 3], x1, sin, ALU.mult))
            link(V.tensor_tensor(x1, y[:, 0], y[:, 1], ALU.subtract))
            link(V.tensor_tensor(x2, y[:, 2], y[:, 3], ALU.add))

        PAR1 = {"q_g": (0, 384), "kv_g": (384, 256), "sub_g": (640, 64), "ln1_g": (704, 1024),
                "ln1_b": (1728, 1024), "ln2_g": (2752, 1024), "ln2_b": (3776, 1024), "fox_b": (4800, 4),
                "lam": (4804, 128), "router_b": (4932, 16)}

        def par_at(names, name):
            at, n = names[name]
            return par[:, at:at + n]

        with stage("start") as ((start,), block):
            @block.sync
            def _(sp):
                sp.dma_start(h[:, :, :], a["x"][0].rearrange("(t p) n -> p t n", p=P)).then_inc(start, 16)
                ring.feed(sp, 0)
                sp.wait_ge(start, 48)

            @block.scalar
            def _(act):
                act.dma_start(tab[:, :], a["tab"]).then_inc(start, 16)
                with nc.allow_non_contiguous_dma("256 positions"):
                    act.dma_start(positions_i[:, :], a["positions"].rearrange("o (t p) -> p (o t)", p=P))\
                        .then_inc(start, 16)
        load_stage([(par[:, 0:D], every(a["ln_in_g"], D)), (par[:, D:2 * D], every(a["ln_in_b"], D))])
        layer_norm_stage(1e-5, par[:, 0:D], par[:, D:2 * D])
        vector_stage(trig_program)
        with stage("sines") as ((sines,), block):
            @block.scalar
            def _(act):
                S.activation(trig[:, :, :, :], ang, ACT.Sin).then_inc(sines, 1)

        def finish_here():
            with stage("store") as ((store,), block):
                @block.sync
                def _(sp):
                    sp.dma_start(outs[0].rearrange("(t p) n -> p t n", p=P), h[:, :, :]).then_inc(store, 16)
                    sp.wait_ge(store, 16)

        gates = small[:, 400:400 + TILES * PADDED].rearrange("p (t e) -> p t e", t=TILES)
        place = small[:, 440:440 + TILES * PADDED].rearrange("p (t e) -> p t e", t=TILES)

        def router_stage(w, n):
            with stage("done") as ((done,), block):
                @block.tensor
                def _(pe):
                    for t in range(TILES):
                        for c in range(DC):
                            last = T.matmul(ps[:, t, 0:n], hT[:, c, t * P:(t + 1) * P], w[:, c, :],
                                            start=c == 0, stop=c == DC - 1)
                    last.then_inc(done, 1)
                    pe.wait_ge(done, 1)

        def top2(link, x, t_room):
            vals, hot = t_room[:, 0:8], t_room[:, 8:40].rearrange("p (j e) -> p j e", j=2)
            link(V.max(vals, x))
            link(V.max_index(index[:, 0:8], vals, x))
            link(V.tensor_copy(t_room[:, 40:48], index[:, 0:8]))
            for j in range(2):
                link(V.tensor_scalar(hot[:, j, :], table("iota")[:, 0:N_EXPERTS], t_room[:, 40 + j:41 + j], None, ALU.is_equal))
            return vals, hot

        def first_of_groups(link, x4, room):
            pad, vals = room[:, 0:8], room[:, 8:16]
            link(V.memset(pad[:, 4:8], -3e38))
            link(V.tensor_copy(pad[:, 0:4], x4))
            link(V.max(vals, pad))
            link(V.max_index(index[:, 0:8], vals, pad))
            link(V.tensor_copy(room[:, 16:17], index[:, 0:1]))
            link(V.tensor_scalar(room[:, 20:24], table("iota")[:, 0:4], room[:, 16:17], None, ALU.is_equal))
            return room[:, 20:24], vals

        def keep_group(link, out, x, group, room):
            full = room[:, 0:16].rearrange("p (g e) -> p g e", g=4)
            off = room[:, 16:20]
            link(V.tensor_scalar(off, group, -NEG, NEG, ALU.mult, ALU.add))
            link(V.tensor_tensor(full, x.rearrange("p (g e) -> p g e", g=4), bc(group, (P, 4, 4), 2), ALU.mult))
            link(V.tensor_tensor(out.rearrange("p (g e) -> p g e", g=4), full, bc(off, (P, 4, 4), 2), ALU.add))

        def route1(link):
            router_b = par_at(PAR1, "router_b")
            for t in range(TILES):
                score, biased = small[:, 16 * t:16 * t + 16], small[:, 32:48]
                link(V.tensor_tensor(biased, score, router_b, ALU.add))
                b4 = biased.rearrange("p (g e) -> p g e", g=4)
                even, odd = b4[:, :, 0:4:2], b4[:, :, 1:4:2]
                hi = small[:, 48:56].rearrange("p (g e) -> p g e", g=4)
                lo = small[:, 56:64].rearrange("p (g e) -> p g e", g=4)
                link(V.tensor_tensor(hi, even, odd, ALU.max))
                link(V.tensor_tensor(lo, even, odd, ALU.min))
                link(V.tensor_reduce(small[:, 64:68], hi, AX, ALU.max))
                link(V.tensor_reduce(small[:, 68:72], hi, AX, ALU.min))
                link(V.tensor_reduce(small[:, 72:76], lo, AX, ALU.max))
                link(V.tensor_tensor(small[:, 68:72], small[:, 68:72], small[:, 72:76], ALU.max))
                link(V.tensor_tensor(small[:, 64:68], small[:, 64:68], small[:, 68:72], ALU.add))
                group, _ = first_of_groups(link, small[:, 64:68], small[:, 80:112])
                keep_group(link, small[:, 112:128], biased, group, small[:, 128:160])
                _, hot = top2(link, small[:, 112:128], small[:, 160:224])
                g = gates[:, t, 0:N_EXPERTS]
                link(V.tensor_tensor(place[:, t, 0:N_EXPERTS], hot[:, 0, :], hot[:, 1, :], ALU.add))
                link(V.tensor_tensor(small[:, 240:256], place[:, t, 0:N_EXPERTS], score, ALU.mult))
                link(V.tensor_reduce(small[:, 256:257], small[:, 240:256], AX, ALU.add))
                link(V.reciprocal(small[:, 257:258], small[:, 256:257]))
                link(V.tensor_scalar(g, small[:, 240:256], small[:, 257:258], None, ALU.mult))

        def place_stage():
            with stage("counted", "chain") as ((counted, chain), block):
                chosen = [place[:, t, 0:N_EXPERTS] for t in range(TILES)]

                @block.tensor
                def _(pe):
                    pe.wait_ge(chain, 2)
                    T.matmul(ps[:, 0, 0:16], before, chosen[0], start=True, stop=True)
                    T.matmul(ps[:, 1, 0:16], ones, chosen[0], start=True, stop=False)
                    T.matmul(ps[:, 1, 0:16], before, chosen[1], start=False, stop=True)
                    T.matmul(ps[:, 2, 0:16], ones, chosen[0], start=True, stop=False)
                    T.matmul(ps[:, 2, 0:16], ones, chosen[1], start=False, stop=True).then_inc(counted, 1)

                @block.vector
                def _(dve):
                    link = Chain(dve, chain)
                    link(V.memset(place[:, :, N_EXPERTS:], 0.0))
                    link(V.memset(gates[:, :, N_EXPERTS:], 0.0))
                    dve.wait_ge(counted, 1)
                    for t in range(TILES):
                        link(V.scalar_tensor_tensor(chosen[t], ps[:, t, 0:16], 1.0, chosen[t], ALU.add, ALU.mult))
                    link(V.tensor_scalar(place[:, :, :], place[:, :, :], -1.0, None, ALU.add))
                    link(V.tensor_reduce(small[:, 0:1], ps[:, 2, 0:16], AX, ALU.max))
                    link(V.tensor_scalar(crowded[:, :], small[:, 0:1], float(CAP), None, ALU.is_gt))

        def experts_stage(first, tokens):
            y = arena[:, 0:TILES * D].rearrange("p (t n) -> p t n", t=TILES)
            at = TILES * D
            sig, rows = region(at, 512), region(at + 512, 512)
            actT = region(at + 1024, EC, P)
            picked = region(at + 1536, DC, P)
            sel = region(at + 2560, TILES, 2, CAP)
            sel_gate = region(at + 2816, TILES, 2, CAP)
            selT = region(at + 3072, TILES * P)
            out_rows = region(at + 3328, D)
            zeros = region(at + 4352, P + 512)
            flat = lambda x: x.rearrange("p e s -> p (e s)")
            W = [ring_mem[:, j, :].rearrange("p (c w) -> p c w", c=DC if j < 4 else EC) for j in range(SLOTS)]
            here = [ring.landings(first + j) for j in range(SLOTS)]
            assert ring.used == first
            ring.used = first + 3 * N_EXPERTS
            mats = sources_of[first]
            names = ("cleared", "sel_done", "sel_gate_done", "gathered", "picked_lo", "picked_hi", "sig_done",
                     "rows_done", "turned", "actT_done", "selT_done", "down_lo", "out_lo", "out_hi", "scattered",
                     "gu_done", "d_sig", "d_rows", "d_turned", "d_actT", "d_down", "y_copied")
            with stage(*names) as (sems, block):
                (cleared, sel_done, sel_gate_done, gathered, picked_lo, picked_hi, sig_done, rows_done, turned,
                 actT_done, selT_done, down_lo, out_lo, out_hi, scattered,
                 gu_done, d_sig, d_rows, d_turned, d_actT, d_down, y_copied) = sems

                def is_crowded(eng):
                    return eng.value_load(crowded[0:1, 0:1], min_val=0, max_val=1) > 0

                @block.sync
                def _(sp):
                    ring.feed(sp, first)
                    assert ring.sent == first + SLOTS
                    with sp.Fori(1, PAIRS) as i:
                        for j in range(SLOTS):
                            w = mats[j // 2][bass.ds(2 * i + j % 2, 1)].rearrange("o (c p) n -> p (o c) n", p=P)
                            sp.wait_ge(unit_used, i * SLOTS + (first - SLOTS + 2 * (j // 2) + 2))
                            sp.dma_start(W[j], w).then_inc(landed[j], 16)
                    ring.sent = first + 3 * N_EXPERTS
                    ring.feed(sp, first + 3 * N_EXPERTS)

                @block.tensor
                def _(pe):
                    pe.wait_ge(cleared, 1)
                    for b in range(4):
                        T.matmul(ps[:, b, :], zeros[:, 0:P], zeros[:, P:], start=True, stop=True)

                    def gather(half):
                        for c in range(4 * half, 4 * half + 4):
                            for t in range(TILES):
                                last = T.matmul(ps[:, 4 + half, (c % 4) * P:(c % 4 + 1) * P],
                                                tokens[:, t, c * P:(c + 1) * P], flat(sel[:, t]),
                                                start=t == 0, stop=t == TILES - 1)
                        return last

                    with pe.If(is_crowded(pe)):
                        with pe.Fori(0, PAIRS) as i:
                            for e in range(2):
                                for t in range(TILES):
                                    n = 2 * e + t
                                    for m in range(2):
                                        if t == 0:
                                            pe.wait_ge(landed[2 * m + e], i * 16 + here[2 * m + e])
                                        if m == 0:
                                            pe.wait_ge(d_rows, i * 4 + n)
                                        for c in range(DC):
                                            last = T.matmul(ps[:, 4 + m, :], hT[:, c, t * P:(t + 1) * P],
                                                            W[2 * m + e][:, c, :], start=c == 0, stop=c == DC - 1)
                                        last.then_inc(gu_done, 1)
                                    pe.wait_ge(d_rows, i * 4 + (n + 1))
                                    for k in range(EC):
                                        last = T.transpose(ps[:, 6, k * P:(k + 1) * P],
                                                           rows[:, k * P:(k + 1) * P], ident)
                                    last.then_inc(d_turned, 1)
                                    if t == 0:
                                        pe.wait_ge(landed[4 + e], i * 16 + here[4 + e])
                                    pe.wait_ge(d_actT, i * 4 + (n + 1))
                                    for k in range(EC):
                                        for x in range(2):
                                            last = T.matmul(ps[:, 2 * t + x, :], actT[:, k, :],
                                                            W[4 + e][:, k, x * 512:(x + 1) * 512],
                                                            start=False, stop=True, skip_group_check=True)
                                    last.then_inc(d_down, 1)
                            pe.wait_ge(d_down, i * 4 + 4)
                            pe.sem_inc(unit_used, SLOTS)
                    with pe.Else():
                        pe.wait_ge(sel_done, 1)
                        gather(0).then_inc(gathered, 1)
                        gather(1).then_inc(gathered, 1)
                        with pe.Fori(0, PAIRS) as i:
                            pe.wait_ge(picked_lo, i + 1)
                            pe.wait_ge(picked_hi, i + 1)
                            for m in range(2):
                                for e in range(2):
                                    pe.wait_ge(landed[2 * m + e], i * 16 + here[2 * m + e])
                                for c in range(DC):
                                    for e in range(2):
                                        last = T.matmul(ps[CAP * e:CAP * e + CAP, 6 + m, :],
                                                        picked[:, c, CAP * e:CAP * e + CAP], W[2 * m + e][:, c, :],
                                                        start=c == 0, stop=c == DC - 1)
                                last.then_inc(unit_used, 2)
                            pe.wait_ge(sel_done, i + 2)
                            gather(0).then_inc(gathered, 1)
                            pe.wait_ge(rows_done, i + 1)
                            for k in range(EC):
                                T.transpose(ps[:, 6, k * P:(k + 1) * P], rows[:, k * P:(k + 1) * P], ident)
                            pe.wait_ge(sel_gate_done, i + 1)
                            for t in range(TILES):
                                last = T.transpose(ps[:, 7, t * P:(t + 1) * P], flat(sel_gate[:, t]), ident)
                            last.then_inc(turned, 1)
                            gather(1).then_inc(gathered, 1)
                            pe.wait_ge(actT_done, i + 1)
                            pe.wait_ge(selT_done, i + 1)
                            for e in range(2):
                                pe.wait_ge(landed[4 + e], i * 16 + here[4 + e])
                            for x in range(2):
                                for k in range(EC):
                                    for e in range(2):
                                        last = T.matmul(ps[CAP * e:CAP * e + CAP, 6 + x, :],
                                                        actT[:, k, CAP * e:CAP * e + CAP],
                                                        W[4 + e][:, k, x * 512:(x + 1) * 512],
                                                        start=k == 0, stop=k == EC - 1)
                                if x == 0:
                                    last.then_inc(down_lo, 1)
                                else:
                                    last.then_inc(unit_used, 2)
                            for x, sem in ((0, out_lo), (1, out_hi)):
                                pe.wait_ge(sem, i + 1)
                                for t in range(TILES):
                                    last = T.matmul(ps[:, 2 * t + x, :], selT[:, t * P:(t + 1) * P],
                                                    out_rows[:, x * 512:(x + 1) * 512],
                                                    start=False, stop=True, skip_group_check=True)
                            last.then_inc(scattered, 1)

                @block.scalar
                def _(act):
                    with act.If(is_crowded(act)):
                        with act.Fori(0, PAIRS) as i:
                            for n in range(4):
                                act.wait_ge(gu_done, i * 8 + (2 * n + 1))
                                act.wait_ge(d_rows, i * 4 + n)
                                S.activation(sig, ps[:, 4, :], ACT.Silu).then_inc(d_sig, 1)
                                act.wait_ge(d_turned, i * 4 + (n + 1))
                                act.wait_ge(d_down, i * 4 + n)
                                S.activation(actT.rearrange("p k t -> p (k t)"), ps[:, 6, :], ACT.Copy)\
                                    .then_inc(d_actT, 1)
                    with act.Else():
                        lo = picked[:, 0:4, :].rearrange("p c s -> p (c s)")
                        act.wait_ge(gathered, 1)
                        S.activation(lo, ps[:, 4, :], ACT.Copy).then_inc(picked_lo, 1)
                        with act.Fori(0, PAIRS) as i:
                            act.wait_ge(unit_used, i * SLOTS + (first + 2))
                            act.wait_ge(rows_done, i)
                            S.activation(sig, ps[:, 6, :], ACT.Silu).then_inc(sig_done, 1)
                            act.wait_ge(gathered, i * 2 + 3)
                            S.activation(lo, ps[:, 4, :], ACT.Copy).then_inc(picked_lo, 1)
                            act.wait_ge(turned, i + 1)
                            act.wait_ge(unit_used, i * SLOTS + first)
                            S.activation(actT.rearrange("p k t -> p (k t)"), ps[:, 6, :], ACT.Copy)\
                                .then_inc(actT_done, 1)
                            act.wait_ge(down_lo, i + 1)
                            act.wait_ge(scattered, i)
                            S.activation(out_rows[:, 0:512], ps[:, 6, :], ACT.Copy).then_inc(out_lo, 1)

                @block.vector
                def _(dve):
                    V.memset(zeros, 0.0).then_inc(cleared, 1)

                    def one_hots(pair):
                        return V.tensor_tensor(sel, bc(bc(table("iota"), (P, 2, CAP), 1), (P, TILES, 2, CAP), 1),
                                               bc(place[:, :, bass.ds(2 * pair, 2)], (P, TILES, 2, CAP), 3),
                                               ALU.is_equal)

                    def gated(pair):
                        return V.tensor_tensor(sel_gate, sel, bc(gates[:, :, bass.ds(2 * pair, 2)],
                                                                 (P, TILES, 2, CAP), 3), ALU.mult)

                    with dve.If(is_crowded(dve)):
                        with dve.Fori(0, PAIRS) as i:
                            for n in range(4):
                                e, t = n // 2, n % 2
                                dve.wait_ge(gu_done, i * 8 + (2 * n + 2))
                                dve.wait_ge(d_sig, i * 4 + (n + 1))
                                dve.wait_ge(d_turned, i * 4 + n)
                                V.scalar_tensor_tensor(rows, sig, gates[:, t, bass.ds(2 * i + e, 1)], ps[:, 5, :],
                                                       ALU.mult, ALU.mult).then_inc(d_rows, 1)
                        dve.wait_ge(d_down, 2 * N_EXPERTS)
                    with dve.Else():
                        hi = picked[:, 4:8, :].rearrange("p c s -> p (c s)")
                        one_hots(0).then_inc(sel_done, 1)
                        dve.wait_ge(sel_done, 1)
                        gated(0).then_inc(sel_gate_done, 1)
                        dve.wait_ge(gathered, 2)
                        V.tensor_copy(hi, ps[:, 5, :]).then_inc(picked_hi, 1)
                        with dve.Fori(0, PAIRS) as i:
                            dve.wait_ge(sel_gate_done, i + 1)
                            one_hots(i + 1).then_inc(sel_done, 1)
                            dve.wait_ge(unit_used, i * SLOTS + (first + 4))
                            dve.wait_ge(sig_done, i + 1)
                            V.tensor_tensor(rows, sig, ps[:, 7, :], ALU.mult).then_inc(rows_done, 1)
                            dve.wait_ge(turned, i + 1)
                            V.tensor_copy(selT, ps[:, 7, 0:SEQ]).then_inc(selT_done, 1)
                            dve.wait_ge(sel_done, i + 2)
                            gated(i + 1).then_inc(sel_gate_done, 1)
                            dve.wait_ge(gathered, i * 2 + 4)
                            V.tensor_copy(hi, ps[:, 5, :]).then_inc(picked_hi, 1)
                            dve.wait_ge(unit_used, i * SLOTS + (first + 6))
                            V.tensor_copy(out_rows[:, 512:], ps[:, 7, :]).then_inc(out_hi, 1)
                        dve.wait_ge(scattered, PAIRS)
                    V.tensor_copy(y, ps[:, 0:4, :].rearrange("p (t x) n -> p t (x n)", t=TILES)).then_inc(y_copied, 1)
            return y

        sources_of = {plan[l]["experts"]: (a["exp_w_gate"][l], a["exp_w_up"][l], a["exp_w_down"][l])
                      for l in range(DEPTH)}
        sources_of[plan[DEPTH]["experts"]] = (a["w1_2"][0], a["w3_2"][0], a["w2_2"][0])

        def turn_h():
            turn_stage(lambda t, c: h[:, t, c * P:(c + 1) * P], DC, P, hT)

        def output_stage(units):
            oT = region(TILES * D, DC, SEQ)
            turn_stage(lambda t, c: mixed[:, t, c * P:(c + 1) * P], DC, P, oT)
            mix = region(0, TILES, D)
            project_stage(oT, DC, [(u, 0, 512, lambda t, i=i: mix[:, t, i * 512:(i + 1) * 512])
                                   for i, u in enumerate(units)])
            return mix

        for l in range(DEPTH):
            lam_init = 0.8 - 0.6 * math.exp(-0.3 * l)
            p1 = lambda name: par_at(PAR1, name)
            load_stage([(p1("q_g"), every(a["mla_q_norm_g"][l], 384)), (p1("kv_g"), every(a["mla_kv_norm_g"][l], 256)),
                        (p1("sub_g"), every(a["diff_subln_g"][l], 64)), (p1("ln1_g"), every(a["ln1_g"][l], D)),
                        (p1("ln1_b"), every(a["ln1_b"][l], D)), (p1("ln2_g"), every(a["ln2_g"][l], D)),
                        (p1("ln2_b"), every(a["ln2_b"][l], D)), (p1("fox_b"), every(a["fox_f_bias"][l], 4)),
                        (p1("router_b"), every(a["router_bias"], 16))] +
                       [(p1("lam")[:, 32 * i:32 * i + 32], every(a["diff_lam_" + x][l], 32))
                        for i, x in enumerate(("q1", "k1", "q2", "k2"))])
            turn_h()
            z = region(0, TILES, IN1)
            project_stage(hT, DC, [(u, 0, min(512, IN1 - 512 * i),
                                    lambda t, i=i: z[:, t, 512 * i:min(512 * i + 512, IN1)])
                                   for i, u in enumerate(plan[l]["in"])])
            base = TILES * IN1
            kv = region(base, TILES, HEADS, 128)
            qT, kT = region(base + 2048, HEADS, SEQ), region(base + 4096, HEADS, SEQ)
            prob, probT = region(base + 6144, HEADS, SEQ), region(base + 8192, TILES * HEADS, P)
            rms_stage([(z[:, t, o:o + w].unsqueeze(1), z[:, t, o:o + w].unsqueeze(1), 1e-6,
                        [p1(g).unsqueeze(1)])
                       for t in range(TILES) for o, w, g in ((0, MLA_Q, "q_g"), (MLA_Q, MLA_KV, "kv_g"))],
                      region(base + 6144, 2048))
            cT = region(base + 2048, 5, SEQ)
            turn_stage(lambda t, c: z[:, t, c * P:(c + 1) * P], 5, P, cT)
            q96 = region(base + 6144, TILES, HEADS, MLA_QK)
            q_flat = q96.rearrange("p t h d -> p t (h d)")
            kv_flat = kv.rearrange("p t h d -> p t (h d)")
            uq, ukv = plan[l]["uq"][0], plan[l]["ukv"][0]
            project_stage(cT[:, 0:3, :], 3, [(uq, o, w, lambda t, o=o, w=w: q_flat[:, t, o:o + w])
                                             for o, w in ((0, 512), (512, 256))])
            project_stage(cT[:, 3:5, :], 2, [(ukv, o, 512, lambda t, o=o: kv_flat[:, t, o:o + 512])
                                             for o in (0, 512)])
            k96 = region(base + 8192, TILES, HEADS, MLA_QK)
            tmp = region(base + 2048, 2048)

            def rope_program(link):
                r0 = MLA_Q + MLA_KV
                for t in range(TILES):
                    rope(link, q96[:, t, :, MLA_NOPE:], HEADS, MLA_QK, t, 0, MLA_ROPE // 2, tmp)
                    rope(link, z[:, t, r0:r0 + MLA_ROPE].unsqueeze(1), 1, MLA_ROPE, t, 0, MLA_ROPE // 2, tmp)
                    link(V.tensor_copy(k96[:, t, :, 0:MLA_NOPE], kv[:, t, :, 0:MLA_NOPE]))
                    link(V.tensor_copy(k96[:, t, :, MLA_NOPE:],
                                       bc(z[:, t, r0:r0 + MLA_ROPE], (P, HEADS, MLA_ROPE), 1)))
                    d0 = r0 + MLA_ROPE
                    for o in (d0, d0 + 256):
                        rope(link, z[:, t, o:o + 256].rearrange("p (h d) -> p h d", h=8), 8, DIFF_QK, t,
                             MLA_ROPE // 2, DIFF_ROT // 2, tmp)

            vector_stage(rope_program)
            turn_stage(lambda t, i: q96[:, t, i, :], HEADS, MLA_QK, qT)
            turn_stage(lambda t, i: k96[:, t, i, :], HEADS, MLA_QK, kT)
            out8 = mixed.rearrange("p t (h d) -> p t h d", d=HD)
            masks = {n: table(n).rearrange("p (t k) -> p t k", t=TILES) for n in ("chunk_mask", "causal_mask")}

            def chunk_bias(t, keys):
                return bc(masks["chunk_mask"][:, t, 0:keys], (P, HEADS, keys), 1)

            attend_stage(HEADS, MLA_QK, qT, kT, lambda j, i: kv[:, j, i, MLA_NOPE:], MLA_QK ** -0.5, chunk_bias,
                         lambda t: out8[:, t, 0:8, :], prob, probT)
            d0 = MLA_Q + MLA_KV + MLA_ROPE
            turn_stage(lambda t, i: z[:, t, d0 + 32 * i:d0 + 32 * i + 32], HEADS, DIFF_QK, qT)
            turn_stage(lambda t, i: z[:, t, d0 + 256 + 32 * i:d0 + 256 + 32 * i + 32], HEADS, DIFF_QK, kT)
            lam = small[:, 500:501]

            with stage("chain", "asked", "answered") as ((chain, asked, answered), block):
                w = small[:, 128:192].rearrange("p (j d) -> p j d", j=2)
                lams = p1("lam").rearrange("p (j i d) -> p j i d", j=2, i=2)

                @block.vector
                def _(dve):
                    link = Chain(dve, chain)
                    link(V.tensor_tensor(w, lams[:, :, 0, :], lams[:, :, 1, :], ALU.mult))
                    V.tensor_reduce(small[:, 192:194], w, AX, ALU.add).then_inc(asked, 1)
                    dve.wait_ge(answered, 1)
                    link(V.tensor_tensor(small[:, 196:197], small[:, 194:195], small[:, 195:196], ALU.subtract))
                    link(V.tensor_scalar(lam, small[:, 196:197], lam_init, None, ALU.add))

                @block.scalar
                def _(act):
                    act.wait_ge(asked, 1)
                    S.activation(small[:, 194:196], small[:, 192:194], ACT.Exp).then_inc(answered, 1)

            def diff_combine(link, t, res, total):
                both = region(base, HEADS, HD)
                link(V.tensor_tensor(both, res, bc(total, (P, HEADS, HD), 2), ALU.mult))
                pair = both.rearrange("p (h j) d -> p h j d", j=2)
                odd = region(base + 512, DIFF_HEADS, HD)
                link(V.tensor_scalar(odd, pair[:, :, 1, :], lam, None, ALU.mult))
                link(V.tensor_tensor(out8[:, t, 8:12, :], pair[:, :, 0, :], odd, ALU.subtract))

            attend_stage(HEADS, DIFF_QK, qT, kT,
                         lambda j, i: z[:, j, d0 + 512 + (i // 2) * HD:d0 + 512 + (i // 2 + 1) * HD],
                         DIFF_QK ** -0.5, chunk_bias, None, prob, probT, diff_combine)
            rms_stage([(out8[:, t, 8:12, :], out8[:, t, 8:12, :], 1e-6, [bc(p1("sub_g"), (P, 4, HD), 1)])
                       for t in range(TILES)], region(base, 2048))
            f0 = d0 + 768
            turn_stage(lambda t, i: z[:, t, f0 + HD * i:f0 + HD * i + HD], FOX_HEADS, HD, qT)
            turn_stage(lambda t, i: z[:, t, f0 + 256 + HD * i:f0 + 256 + HD * i + HD], FOX_HEADS, HD, kT)
            log_f = small[:, 256:264].rearrange("p (t h) -> p t h", t=TILES)
            cum = small[:, 264:272].rearrange("p (t h) -> p t h", t=TILES)
            fox = region(base, TILES, FOX_HEADS, SEQ)

            with stage("chain", "asked", "answered") as ((chain, asked, answered), block):
                x, n, e, m = (small[:, 128 + 8 * i:136 + 8 * i] for i in range(4))

                @block.vector
                def _(dve):
                    link = Chain(dve, chain)
                    link(V.tensor_tensor(x.rearrange("p (t h) -> p t h", t=TILES), z[:, :, f0 + 768:f0 + 772],
                                         bc(p1("fox_b"), (P, TILES, 4), 1), ALU.add))
                    link(V.tensor_scalar(n, x, -1.0, None, ALU.mult))
                    V.tensor_tensor(n, n, x, ALU.min).then_inc(asked, 1)
                    link(V.tensor_scalar(m, x, 0.0, None, ALU.min))
                    for t in range(TILES):
                        link(V.tensor_scalar(out8[:, t, 8:12, :], out8[:, t, 8:12, :], 1.0 - lam_init, None,
                                             ALU.mult))
                    dve.wait_ge(answered, 2)
                    link(V.tensor_tensor(small[:, 256:264], m, e, ALU.subtract))

                @block.scalar
                def _(act):
                    act.wait_ge(asked, 1)
                    S.activation(e, n, ACT.Exp).then_inc(answered, 1)
                    act.wait_ge(answered, 1)
                    S.activation(e, e, ACT.Ln, bias=1.0).then_inc(answered, 1)

            with stage("summed", "chain") as ((summed, chain), block):
                @block.tensor
                def _(pe):
                    T.matmul(ps[:, 0, 0:4], upto, log_f[:, 0, :], start=True, stop=True)
                    T.matmul(ps[:, 1, 0:4], ones, log_f[:, 0, :], start=True, stop=False)
                    T.matmul(ps[:, 1, 0:4], upto, log_f[:, 1, :], start=False, stop=True).then_inc(summed, 1)
                    for i in range(FOX_HEADS):
                        f = [log_f[:, t, i:i + 1].broadcast_to((P, P)) for t in range(TILES)]
                        row = ps[:, 2 + i, :]
                        T.matmul(row[:, 0:P], f[0], upto, start=True, stop=True)
                        T.matmul(row[:, P:SEQ], f[0], ones, start=True, stop=False)
                        T.matmul(row[:, P:SEQ], f[1], upto, start=False, stop=True).then_inc(summed, 1)

                @block.vector
                def _(dve):
                    link = Chain(dve, chain)
                    dve.wait_ge(summed, 1)
                    link(V.tensor_copy(cum, ps[:, 0:2, 0:4]))
                    for i in range(FOX_HEADS):
                        dve.wait_ge(summed, i + 2)
                        for t in range(TILES):
                            link(V.tensor_scalar(fox[:, t, i, :], ps[:, 2 + i, 0:SEQ], -1.0, cum[:, t, i:i + 1],
                                                 ALU.mult, ALU.add))
                            link(V.tensor_tensor(fox[:, t, i, :], fox[:, t, i, :], masks["causal_mask"][:, t, :],
                                                 ALU.add))
            attend_stage(FOX_HEADS, HD, qT, kT, lambda j, i: z[:, j, f0 + 512 + HD * i:f0 + 512 + HD * (i + 1)],
                         HD ** -0.5, lambda t, keys: fox[:, t, :, 0:keys],
                         lambda t: out8[:, t, 12:16, :], prob, probT)
            mix = output_stage(plan[l]["out"])
            layer_norm_stage(1e-5, p1("ln1_g"), p1("ln1_b"), mix)
            if stop == f"ln1_{l}":
                finish_here()
                return
            turn_h()
            rw = region(0, DC, N_EXPERTS)
            load_stage([(rw, a["router_w"].rearrange("(c p) e -> p c e", p=P))])
            router_stage(rw, N_EXPERTS)
            with stage("scores") as ((scores,), block):
                @block.scalar
                def _(act):
                    S.activation(small[:, 0:32].rearrange("p (t e) -> p t e", t=TILES), ps[:, 0:2, 0:16],
                                 ACT.Sigmoid).then_inc(scores, 1)
            vector_stage(route1)
            place_stage()
            y = experts_stage(plan[l]["experts"], h)
            layer_norm_stage(1e-5, p1("ln2_g"), p1("ln2_b"), y)
            if stop == f"ln2_{l}":
                finish_here()
                return
        plan2 = plan[DEPTH]
        PAR2 = {"norm_g": (0, D), "mod_a": (1024, D), "rec_g": (2048, 512), "att_g": (2560, 512), "q_g": (3072, 64),
                "k_g": (3136, 64), "idx_g": (3200, 64), "idx_b": (3264, 64), "route_b": (3328, 20),
                "room": (3400, 1720)}
        p2 = lambda name: par_at(PAR2, name)
        room = p2("room")
        z_n = TILES * IN2
        mod = region(0, 6 * D)
        cond = small[:, 0:DC]
        load_stage([(p2("norm_g"), every(a["norm1_g_2"][0], D)), (p2("rec_g"), every(a["rec_out_g_2"][0], 512)),
                    (p2("att_g"), every(a["attn_out_g_2"][0], 512)), (p2("q_g"), every(a["q_norm_g_2"][0], 64)),
                    (p2("k_g"), every(a["k_norm_g_2"][0], 64)), (p2("idx_g"), every(a["idx_k_norm_g_2"][0], 64)),
                    (p2("idx_b"), every(a["idx_k_norm_b_2"][0], 64)),
                    (p2("route_b")[:, 0:4], every(a["b_rg_2"][0], 4)),
                    (p2("route_b")[:, 4:20], every(a["b_re_2"][0], 16)),
                    (cond, a["c_2"].rearrange("o (c p) -> p (o c)", p=P)),
                    (mod, every(a["b_ada_2"][0], 6 * D))])
        with stage("cond_done", "added") as ((cond_done, added), block):
            units = plan2["ada"]
            assert ring.used == units[0] and ring.after(units[-1]) == units[-1] + 1
            ring.used = units[-1] + 1

            @block.scalar
            def _(act):
                S.activation(small[:, 8:16], cond, ACT.Silu).then_inc(cond_done, 1)

            @block.sync
            def _(sp):
                ring.feed(sp, ring.after(units[-1]))

            @block.tensor
            def _(pe):
                pe.wait_ge(cond_done, 1)
                for i, u in enumerate(units):
                    w = ring.view(u, DC)
                    pe.wait_ge(landed[u % SLOTS], ring.landings(u))
                    if i >= BANKS:
                        pe.wait_ge(added, i - BANKS + 1)
                    for c in range(DC):
                        last = T.matmul(ps[:, i % BANKS, :], small[:, 8 + c:9 + c].broadcast_to((P, P)), w[:, c, :],
                                        start=c == 0, stop=c == DC - 1)
                    last.then_inc(unit_used, 1)

            @block.vector
            def _(dve):
                for i, u in enumerate(units):
                    dve.wait_ge(unit_used, u + 1)
                    part = mod[:, 512 * i:512 * i + 512]
                    V.tensor_tensor(part, part, ps[:, i % BANKS, :], ALU.add).then_inc(added, 1)

        def modulated_stage(gain, scale, shift, out, squares):
            rms_stage([(h[:, t, :].unsqueeze(1), out[:, t, :].unsqueeze(1), 1e-6, [gain.unsqueeze(1)])
                       for t in range(TILES)], squares)

            def modulate(link):
                for t in range(TILES):
                    link(V.scalar_tensor_tensor(squares[:, 0:D], scale, 1.0, out[:, t, :], ALU.add, ALU.mult))
                    link(V.tensor_tensor(out[:, t, :], squares[:, 0:D], shift, ALU.add))

            vector_stage(modulate)

        u_rows = region(6 * D, TILES, D)
        with stage("kept") as ((kept,), block):
            @block.sync
            def _(sp):
                sp.dma_start(scratch["mod"].rearrange("(o n) -> o n", o=1), mod[0:1, 2 * D:6 * D]).then_inc(kept, 16)
                sp.wait_ge(kept, 16)
        modulated_stage(p2("norm_g"), mod[:, D:2 * D], mod[:, 0:D], u_rows, region(8 * D, TILES * D))
        turn_stage(lambda t, c: u_rows[:, t, c * P:(c + 1) * P], DC, P, hT)
        z = region(0, TILES, IN2)
        project_stage(hT, DC, [(u, 0, min(512, IN2 - 512 * i), lambda t, i=i: z[:, t, 512 * i:min(512 * i + 512, IN2)])
                               for i, u in enumerate(plan2["in"])])

        k_rows = region(z_n, TILES, 512)
        recT = region(z_n + 2048, 2, REC_HEADS, SEQ)
        spread, q_spread = region(z_n, TILES, LEVELS, P), region(z_n + 4096, TILES, LEVELS, P)
        attnT = region(z_n + 6144, 3, P)
        logits = region(z_n + 4096, 2, 512)
        lb, rest = region(z_n + 5120, 512), region(z_n + 5632, 512)
        load_stage([(logits[:, i, :], every(a["lb_logits_2"][i], 512)) for i in range(2)])
        with stage("chain", "asked", "answered") as ((chain, asked, answered), block):
            @block.scalar
            def _(act):
                S.activation(k_rows, z[:, :, 512:1024], ACT.Sigmoid).then_inc(answered, 1)
                act.wait_ge(asked, 1)
                S.activation(logits, logits, ACT.Exp).then_inc(answered, 1)
                S.activation(z[:, :, 0:512], z[:, :, 0:512], ACT.Silu).then_inc(answered, 1)
                act.wait_ge(asked, 3)
                S.activation(z[:, :, 512:1024], z[:, :, 512:1024], ACT.Ln).then_inc(answered, 1)

            @block.vector
            def _(dve):
                link = Chain(dve, chain)
                link(V.tensor_tensor(lb, logits[:, 0, :], logits[:, 1, :], ALU.max))
                V.tensor_tensor(logits, logits, bc(lb, (P, 2, 512), 1), ALU.subtract).then_inc(asked, 1)
                dve.wait_ge(answered, 2)
                link(V.tensor_tensor(rest, logits[:, 0, :], logits[:, 1, :], ALU.add))
                link(V.reciprocal(rest, rest))
                link(V.tensor_tensor(lb, logits[:, 0, :], rest, ALU.mult))
                link(V.tensor_scalar(rest, lb, -1.0, 1.0, ALU.mult, ALU.add))
                link(V.tensor_tensor(k_rows, k_rows, bc(rest, (P, TILES, 512), 1), ALU.mult))
                V.tensor_tensor(z[:, :, 512:1024], k_rows, bc(lb, (P, TILES, 512), 1), ALU.add).then_inc(asked, 1)
                dve.wait_ge(asked, 2)
                V.tensor_scalar(k_rows, z[:, :, 512:1024], -1.0, 1.0, ALU.mult, ALU.add).then_inc(asked, 1)
        turn_stage(lambda t, i: z[:, t, i * P:(i + 1) * P], REC_HEADS, P, recT[:, 0])
        turn_stage(lambda t, i: k_rows[:, t, i * P:(i + 1) * P], REC_HEADS, P, recT[:, 1])
        spans, last_span, level_mask = (table(x) for x in ("spans", "last_span", "level_mask"))
        for i in range(REC_HEADS):
            names = ("spanned", "grown", "spread_done", "paired", "chain", "masked", "summed")
            with stage(*names) as ((spanned, grown, spread_done, paired, chain, masked, summed), block):
                qT, kT = recT[:, 0, i, :], recT[:, 1, i, :]
                cols = slice(i * P, (i + 1) * P)

                @block.tensor
                def _(pe):
                    for t in range(TILES):
                        lf = z[:, t, 512 + i * P:512 + (i + 1) * P]
                        T.matmul(ps[:, 2 * t, :], lf, spans[:, 0:512], start=True, stop=True)
                        if t == 0:
                            last = T.matmul(ps[:, 1, :], lf, spans[:, 512:1024], start=True, stop=True)
                        else:
                            T.matmul(ps[:, 3, 0:384], lf, spans[:, 512:896], start=True, stop=True)
                            last = T.matmul(ps[:, 3, 384:512], lf, last_span, start=True, stop=True)
                        last.then_inc(spanned, 1)
                    for t in range(TILES):
                        pe.wait_ge(spread_done, 2 * t + 2)
                        for l in range(LEVELS - 1):
                            T.matmul(ps[:, 4 + 2 * t + l // 4, (l % 4) * P:(l % 4 + 1) * P], spread[:, t, l, :],
                                     q_spread[:, t, l, :], start=True, stop=True)
                        tok = slice(t * P, (t + 1) * P)
                        T.matmul(ps[:, 5 + 2 * t, 3 * P:], kT[:, tok], qT[:, tok], start=True, stop=True)\
                            .then_inc(paired, 1)
                    T.matmul(ps[:, 0, 0:P], spread[:, 0, LEVELS - 1, :], q_spread[:, 1, LEVELS - 1, :],
                             start=True, stop=True).then_inc(paired, 1)
                    pe.wait_ge(masked, 3)
                    v = [z[:, t, 1024 + i * P:1024 + (i + 1) * P] for t in range(TILES)]
                    T.matmul(ps[:, 1, 0:P], attnT[:, 0, :], v[0], start=True, stop=True)
                    T.matmul(ps[:, 1, P:2 * P], attnT[:, 2, :], v[0], start=True, stop=False)
                    T.matmul(ps[:, 1, P:2 * P], attnT[:, 1, :], v[1], start=False, stop=True).then_inc(summed, 1)

                @block.scalar
                def _(act):
                    for t in range(TILES):
                        act.wait_ge(spanned, t + 1)
                        S.activation(spread[:, t, :, :].rearrange("p l x -> p (l x)"),
                                     ps[:, 2 * t:2 * t + 2, :].rearrange("p b n -> p (b n)"), ACT.Exp)\
                            .then_inc(grown, 1)
                    act.wait_ge(summed, 1)
                    S.activation(mixed[:, :, cols], ps[:, 1, 0:2 * P].rearrange("p (t v) -> p t v", t=TILES),
                                 ACT.Copy).then_inc(grown, 1)

                @block.vector
                def _(dve):
                    link = Chain(dve, chain)
                    for t in range(TILES):
                        tok = slice(t * P, (t + 1) * P)
                        dve.wait_ge(grown, t + 1)
                        V.tensor_tensor(q_spread[:, t], spread[:, t], bc(qT[:, tok], (P, LEVELS, P), 1), ALU.mult)\
                            .then_inc(spread_done, 1)
                        dve.wait_ge(spread_done, 2 * t + 1)
                        V.tensor_tensor(spread[:, t], spread[:, t], bc(kT[:, tok], (P, LEVELS, P), 1), ALU.mult)\
                            .then_inc(spread_done, 1)
                    for t in range(TILES):
                        dve.wait_ge(paired, t + 1)
                        picked = room[:, 0:LEVELS * P]
                        link(V.tensor_tensor(picked, ps[:, 4 + 2 * t:6 + 2 * t, :].rearrange("p b n -> p (b n)"),
                                             level_mask, ALU.mult))
                        V.tensor_reduce(attnT[:, t, :], picked.rearrange("p (l x) -> p x l", l=LEVELS), AX, ALU.add)\
                            .then_inc(masked, 1)
                        dve.wait_ge(masked, t + 1)
                    dve.wait_ge(paired, 3)
                    V.tensor_copy(attnT[:, 2, :], ps[:, 0, 0:P]).then_inc(masked, 1)

        rec = mixed[:, :, 0:512].rearrange("p t (h v) -> p t h v", v=REC_D)
        rec_gain = p2("rec_g").rearrange("p (h v) -> p h v", v=REC_D)
        with stage("gated") as ((gated,), block):
            @block.scalar
            def _(act):
                S.activation(z[:, :, 1536:2048], z[:, :, 1536:2048], ACT.Silu).then_inc(gated, 1)
        rms_stage([(rec[:, t], rec[:, t], 1e-6,
                    [rec_gain, z[:, t, 1536:2048].rearrange("p (h v) -> p h v", v=REC_D)]) for t in range(TILES)] +
                  [(z[:, t, o:o + 512].rearrange("p (h d) -> p h d", d=HD),
                    z[:, t, o:o + 512].rearrange("p (h d) -> p h d", d=HD), 1e-6, [bc(p2(g), (P, HEADS, HD), 1)])
                   for t in range(TILES) for o, g in ((2048, "q_g"), (2560, "k_g"))], region(z_n, 2048))

        bias_rows = region(z_n, HEADS, 2 * SEQ)
        buckets, rel = room[0:BUCKETS, 0:2 * SEQ], room[0:BUCKETS, 512:520]
        load_stage([(buckets, a["bucket"]), (rel, a["rel_bias_2"])])
        with stage("spread_rows", "copied_rows", "stored") as ((spread_rows, copied_rows, stored), block):
            @block.tensor
            def _(pe):
                for i in range(HEADS):
                    T.matmul(ps[:, i, :], rel[:, i:i + 1].broadcast_to((BUCKETS, P)), buckets,
                             start=True, stop=True).then_inc(spread_rows, 1)

            @block.scalar
            def _(act):
                for i in range(HEADS):
                    act.wait_ge(spread_rows, i + 1)
                    S.activation(bias_rows[:, i, :], ps[:, i, :], ACT.Copy).then_inc(copied_rows, 1)

            @block.sync
            def _(sp):
                sp.wait_ge(copied_rows, HEADS)
                flat = scratch["bias_rows"]
                sp.dma_start(flat[0:HEADS * P * 2 * SEQ].rearrange("(h p n) -> p h n", h=HEADS, p=P), bias_rows).then_inc(stored, 16)
                sp.wait_ge(stored, 16)
                for t in range(TILES):
                    for i in range(HEADS):
                        at = i * P * 2 * SEQ + SEQ - 1 - P * t
                        askew = flat[at:at + P * (2 * SEQ - 1)]\
                            .rearrange("(p n) -> p n", n=2 * SEQ - 1)[:, 0:SEQ]
                        sp.dma_start(z[:, t, i * SEQ:(i + 1) * SEQ], askew).then_inc(stored, 16)
                sp.wait_ge(stored, 16 * (1 + TILES * HEADS))

        work = room[:, 600:600 + TILES * SEQ].rearrange("p (t k) -> p t k", t=TILES)
        iqT, ikT = region(z_n + 4096, HEADS, SEQ), region(z_n + 6144, 1, SEQ)

        with stage("chain", "moment", "rooted") as ((chain, moment, rooted), block):
            @block.vector
            def _(dve):
                link = Chain(dve, chain)
                for t in range(TILES):
                    link(V.bn_stats(small[:, 8 * t:8 * t + 6], z[:, t, 4096:4160]))
                    link(V.bn_aggr(small[:, 16 + 2 * t:18 + 2 * t], small[:, 8 * t:8 * t + 6]))
                V.tensor_scalar(small[:, 20:22], small[:, 17:20:2], 1e-6, None, ALU.add).then_inc(moment, 1)
                dve.wait_ge(rooted, 1)
                link(V.reciprocal(small[:, 24:26], small[:, 22:24]))
                for t in range(TILES):
                    x = z[:, t, 4096:4160]
                    link(V.tensor_scalar(x, x, small[:, 16 + 2 * t:17 + 2 * t], small[:, 24 + t:25 + t],
                                         ALU.subtract, ALU.mult))
                    link(V.tensor_tensor(x, x, p2("idx_g"), ALU.mult))
                    link(V.tensor_tensor(x, x, p2("idx_b"), ALU.add))
                    link(V.tensor_scalar(z[:, t, 4160:4168], z[:, t, 4160:4168], HD ** -0.5 * HEADS ** -0.5, None,
                                         ALU.mult))

            @block.scalar
            def _(act):
                act.wait_ge(moment, 1)
                S.activation(small[:, 22:24], small[:, 20:22], ACT.Sqrt).then_inc(rooted, 1)
        turn_stage(lambda t, i: z[:, t, 3584 + HD * i:3584 + HD * (i + 1)], HEADS, HD, iqT)
        turn_stage(lambda t, i: z[:, t, 4096:4160], 1, HD, ikT)
        with stage("scored", "chain") as ((scored, chain), block):
            @block.tensor
            def _(pe):
                for t in range(TILES):
                    for i in range(HEADS):
                        last = T.matmul(ps[:, 4 * t + i // 2, (i % 2) * SEQ:(i % 2 + 1) * SEQ],
                                        iqT[0:HD, i, t * P:(t + 1) * P], ikT[0:HD, 0, :], start=True, stop=True)
                    last.then_inc(scored, 1)

            @block.vector
            def _(dve):
                link = Chain(dve, chain)
                weighed = region(z_n + 2048, HEADS, SEQ)
                best = small[:, 0:8]
                for t in range(TILES):
                    dve.wait_ge(scored, t + 1)
                    link(V.scalar_tensor_tensor(weighed, ps[:, 4 * t:4 * t + 4, :]
                                                .rearrange("p b (j k) -> p (b j) k", j=2), 0.0,
                                                bc(z[:, t, 4160:4168], (P, HEADS, SEQ), 2), ALU.max, ALU.mult))
                    link(V.tensor_reduce(work[:, t, :], weighed.rearrange("p h k -> p k h"), AX, ALU.add))
                    link(V.tensor_tensor(work[:, t, :], work[:, t, :], masks["chunk_mask"][:, t, :], ALU.add))
                    for _ in range(TOPK // 8):
                        link(V.max(best, work[:, t, :]))
                        link(V.match_replace(work[:, t, :], best, work[:, t, :], -3e38))
                    link(V.tensor_scalar(work[:, t, :], work[:, t, :], -2e38, NEG, ALU.is_gt, ALU.mult))
                    bias = z[:, t, 0:HEADS * SEQ].rearrange("p (h k) -> p h k", k=SEQ)
                    link(V.tensor_tensor(bias, bias, bc(work[:, t, :], (P, HEADS, SEQ), 1), ALU.add))
        qT, kT, prob = (region(z_n + 2048 * i, HEADS, SEQ) for i in range(3))
        probT = par[:, 0:2048].rearrange("p (j q) -> p j q", q=P)
        turn_stage(lambda t, i: z[:, t, 2048 + HD * i:2048 + HD * (i + 1)], HEADS, HD, qT)
        turn_stage(lambda t, i: z[:, t, 2560 + HD * i:2560 + HD * (i + 1)], HEADS, HD, kT)
        attend_stage(HEADS, HD, qT, kT, lambda j, i: z[:, j, 3072 + HD * i:3072 + HD * (i + 1)], HD ** -0.5,
                     lambda t, keys: z[:, t, 0:HEADS * SEQ].rearrange("p (h k) -> p h k", k=SEQ)[:, :, 0:keys],
                     lambda t: out8[:, t, 8:16, :], prob, probT)
        rms_stage([(out8[:, t, 8:16, :], out8[:, t, 8:16, :], 1e-6,
                    [p2("att_g").rearrange("p (h d) -> p h d", d=HD)]) for t in range(TILES)], region(z_n, 2048))
        if stop in ("mixed2",):
            vector_stage(lambda link: link(V.tensor_copy(h[:, :, :], mixed)))
            finish_here()
            return
        mix = output_stage(plan2["out"])

        def kept_mod(i):
            return every(scratch["mod"][i * D:(i + 1) * D], D)

        def add_gated(gate, rows):
            def program(link):
                for t in range(TILES):
                    link(V.tensor_tensor(rows[:, t, :], rows[:, t, :], gate, ALU.mult))
                    link(V.tensor_tensor(h[:, t, :], h[:, t, :], rows[:, t, :], ALU.add))
            vector_stage(program)

        rw = region(10 * D, DC, 20)
        moe_rows = region(8 * D, TILES, D)
        load_stage([(room[:, 0:D], kept_mod(0)), (p2("norm_g"), every(a["norm2_g_2"][0], D)),
                    (p2("mod_a"), kept_mod(1)), (par[:, 2048:3072], kept_mod(2)),
                    (rw[:, :, 0:4], a["w_rg_2"][0].rearrange("(c p) e -> p c e", p=P)),
                    (rw[:, :, 4:20], a["w_re_2"][0].rearrange("(c p) e -> p c e", p=P))])
        add_gated(room[:, 0:D], mix)
        modulated_stage(p2("norm_g"), par[:, 2048:3072], p2("mod_a"), moe_rows, region(4 * D, TILES * D))
        turn_stage(lambda t, c: moe_rows[:, t, c * P:(c + 1) * P], DC, P, hT)
        router_stage(rw, 20)
        load_stage([(room[:, 0:D], kept_mod(3))])

        with stage("chain", "asked", "answered") as ((chain, asked, answered), block):
            base = 288

            @block.scalar
            def _(act):
                for t in range(TILES):
                    act.wait_ge(asked, 2 * t + 1)
                    S.activation(small[:, 24:28], small[:, 20:24], ACT.Exp).then_inc(answered, 1)
                    act.wait_ge(asked, 2 * t + 2)
                    S.activation(small[:, 29:30], small[:, 28:29], ACT.Exp).then_inc(answered, 1)

            @block.vector
            def _(dve):
                link = Chain(dve, chain)
                for t in range(TILES):
                    logit = small[:, 0:20]
                    link(V.tensor_tensor(logit, ps[:, t, 0:20], p2("route_b"), ALU.add))
                    group, vals = first_of_groups(link, logit[:, 0:4], small[:, 80:112])
                    V.tensor_scalar(small[:, 20:24], logit[:, 0:4], vals[:, 0:1], None, ALU.subtract)\
                        .then_inc(asked, 1)
                    keep_group(link, small[:, 112:128], logit[:, 4:20], group, small[:, 128:160])
                    vals, hot = top2(link, small[:, 112:128], small[:, 160:224])
                    V.tensor_tensor(small[:, 28:29], vals[:, 1:2], vals[:, 0:1], ALU.subtract).then_inc(asked, 1)
                    dve.wait_ge(answered, 2 * t + 2)
                    link(V.tensor_reduce(small[:, 30:31], small[:, 24:28], AX, ALU.add))
                    link(V.tensor_scalar(small[:, 31:32], small[:, 29:30], 1.0, None, ALU.add))
                    link(V.tensor_tensor(small[:, 32:33], small[:, 30:31], small[:, 31:32], ALU.mult))
                    link(V.reciprocal(small[:, 33:34], small[:, 32:33]))
                    link(V.tensor_tensor(small[:, 34:35], small[:, 33:34], small[:, 29:30], ALU.mult))
                    link(V.tensor_scalar(small[:, 36:52], hot[:, 0, :], small[:, 33:34], None, ALU.mult))
                    link(V.tensor_tensor(place[:, t, 0:N_EXPERTS], hot[:, 0, :], hot[:, 1, :], ALU.add))
                    link(V.scalar_tensor_tensor(gates[:, t, 0:N_EXPERTS], hot[:, 1, :], small[:, 34:35], small[:, 36:52],
                                                ALU.mult, ALU.add))
        place_stage()
        y = experts_stage(plan2["experts"], moe_rows)
        add_gated(room[:, 0:D], y)
        finish_here()


def kernel(**inputs):
    import numpy as _np
    import concourse.bacc as _bacc
    from concourse import mybir as _mybir
    from concourse.bass_utils import run_bass_kernel_spmd as _run

    nc = _bacc.Bacc("TRN2", target_bir_lowering=False, num_devices=1)
    arrays, aps = {}, {}
    given = dict(inputs)
    given["tab"] = tables()
    given["bucket"] = bucket_table()
    for name, value in given.items():
        value = _np.ascontiguousarray(value)
        arrays[f"in_{name}"] = value
        aps[name] = nc.dram_tensor(f"in_{name}", value.shape, _mybir.dt.from_np(value.dtype),
                                   kind="ExternalInput").ap()
    out = nc.dram_tensor("out_0", (SEQ, D), F32, kind="ExternalOutput").ap()
    scratch = {n: nc.dram_tensor(f"scratch_{n}", s, F32, kind="Internal").ap() for n, s in SCRATCH.items()}
    build(nc, aps, scratch, [out])
    r = _run(nc, [arrays], core_ids=[0])
    return r.results[0]["out_0"].reshape(1, SEQ, D)
```

```python
from contextlib import ExitStack, contextmanager
import math

import numpy as np

import concourse.bass as bass
from concourse import mybir

F32 = mybir.dt.float32
I32 = mybir.dt.int32
U32 = mybir.dt.uint32
ALU = mybir.AluOpType
ACT = mybir.ActivationFunctionType
AX = mybir.AxisListType.X

P = 128
SEQ = 256
TILES = SEQ // P
D = 1024
DC = D // P
DEPTH = 2
HEADS = 8
CHUNK = 64
NEG = -1e30

MLA_Q, MLA_KV, MLA_ROPE, MLA_NOPE = 384, 256, 32, 64
MLA_QK = MLA_NOPE + MLA_ROPE
DIFF_QK, DIFF_ROT, DIFF_HEADS = 32, 8, 4
FOX_HEADS = 4
HD = 64
IN1 = 2212
IN2 = 4168
THETA = 500000.0
ALPHA = (2 * DEPTH) ** 0.25

REC_HEADS, REC_D = 4, 128
TOPK = 64
BUCKETS = 32
LEVELS = 8

N_EXPERTS, N_GROUPS, D_EXPERT = 16, 4, 512
EC = D_EXPERT // P
PAIRS = N_EXPERTS // 2
PADDED = N_EXPERTS + 2
CAP = 64

SLOT = 4096
SLOTS = 6
BANKS, BANK = 8, 512

TAB = {}
_at = 0
for _name, _n in (("freq_mla", MLA_ROPE // 2), ("freq_diff", DIFF_ROT // 2), ("ident", P), ("upto", P), ("before", P), ("ones", P), ("chunk_mask", TILES * SEQ),
                  ("causal_mask", TILES * SEQ), ("spans", LEVELS * P), ("last_span", P),
                  ("level_mask", LEVELS * P),
                  ("iota", CAP)):
    TAB[_name] = (_at, _n)
    _at += _n
TAB_N = _at
TAB_FIRST = TAB["upto"][0]


def tables():
    tab = np.zeros((P, TAB_N), np.float32)

    def put(name, value):
        a, n = TAB[name]
        tab[:, a:a + n] = np.asarray(value, np.float32).reshape(P, n)

    p = np.arange(P)
    put("ident", np.eye(P))
    put("upto", p[:, None] <= p[None, :])
    put("before", p[:, None] < p[None, :])
    put("ones", np.ones((P, P)))
    k = np.arange(SEQ)
    q = p[:, None, None] + P * np.arange(TILES)[None, :, None]
    put("chunk_mask", np.where(k[None, None] // CHUNK <= q // CHUNK, 0.0, NEG))
    put("causal_mask", np.where(k[None, None] <= q, 0.0, NEG))
    u, x = p[:, None, None], p[None, None, :]
    size = (2 ** np.arange(LEVELS))[None, :, None]
    mid = (x // (2 * size)) * (2 * size) + size
    right = x >= mid
    put("spans", np.where(right, (mid <= u) & (u <= x), (x < u) & (u < mid)))
    put("last_span", p[:, None] <= p[None, :])
    s, t = p[:, None, None], p[None, None, :]
    size = (2 ** np.arange(LEVELS - 1))[None, :, None]
    pair = (s // (2 * size) == t // (2 * size)) & (s // size % 2 == 0) & (t // size % 2 == 1)
    put("level_mask", np.concatenate([pair, (s == t)], axis=1))
    f = lambda n: np.float32(THETA) ** (-np.arange(0, n, 2, dtype=np.float32) / np.float32(n))
    put("freq_mla", np.broadcast_to(f(MLA_ROPE), (P, MLA_ROPE // 2)))
    put("freq_diff", np.broadcast_to(f(DIFF_ROT), (P, DIFF_ROT // 2)))
    put("iota", np.broadcast_to(np.arange(CAP), (P, CAP)))
    return tab


SCRATCH = {"mod": (6 * D,), "bias_rows": (HEADS * P * 2 * SEQ + 2 * SEQ,)}


def bucket_table():
    rel = np.arange(-(SEQ - 1), SEQ)
    half, exact, far = BUCKETS // 2, BUCKETS // 4, 128
    n = np.abs(rel)
    nf = np.maximum(n, 1).astype(np.float32)
    large = exact + (np.log(nf / np.float32(exact)) / np.float32(np.log(far / exact))
                     * np.float32(half - exact)).astype(np.int32)
    b = np.where(rel > 0, half, 0) + np.where(n < exact, n, np.minimum(large, half - 1))
    out = np.zeros((BUCKETS, 2 * SEQ), np.float32)
    out[b, np.arange(rel.size)] = 1.0
    return out


class Ring:

    def __init__(self, tensor, landed, unit_used, sources):
        self.tensor, self.landed, self.unit_used, self.sources = tensor, landed, unit_used, sources
        self.sent = 0
        self.used = 0

    def view(self, n, c):
        w = self.sources[n].shape[2]
        return self.tensor[:, n % SLOTS, 0:c * w].rearrange("p (c w) -> p c w", c=c)

    def landings(self, n):
        return 16 * sum(s is not None for s in self.sources[n % SLOTS:n + 1:SLOTS])

    def after(self, n):
        n += 1
        while n < len(self.sources) and self.sources[n] is None:
            n += 1
        return n

    def feed(self, sp, consumed):
        while self.sent < min(len(self.sources), consumed + SLOTS):
            n = self.sent
            source = self.sources[n]
            if source is not None:
                if n >= SLOTS:
                    sp.wait_ge(self.unit_used, n - SLOTS + 1)
                sp.dma_start(self.view(n, source.shape[1]), source).then_inc(self.landed[n % SLOTS], 16)
            self.sent += 1


class Small:

    def __init__(self, sem):
        self.sem, self.sent = sem, 0

    def send(self, eng, pairs):
        for dst, src in pairs:
            eng.dma_start(dst, src).then_inc(self.sem, 16)
        self.sent += len(pairs)

    def arrive(self, eng):
        eng.wait_ge(self.sem, 16 * self.sent)


def build(nc, a, scratch, outs):
    ctx = ExitStack()
    with ctx:
        def sb(name, shape, dt=F32):
            return ctx.enter_context(nc.sbuf_tensor(name, shape, dt))

        ring_mem = sb("ring", [P, SLOTS, SLOT])
        tab = sb("tab", [P, TAB_N])
        h = sb("h", [P, TILES, D])
        hT = sb("hT", [P, DC, SEQ])
        par = sb("par", [P, 5120])
        ARENA = 14900
        arena = sb("arena", [P, ARENA])
        trig = sb("trig", [P, TILES, 2, 20])
        positions_i = sb("positions_i", [P, TILES], I32)
        small = sb("small", [P, 512])
        index = sb("index", [P, 16], U32)
        crowded = sb("crowded", [P, 1], I32)
        ps = ctx.enter_context(nc.psum_tensor("ps", [P, BANKS, BANK], F32))

        def table(name):
            at, n = TAB[name]
            return tab[:, at:at + n]

        ident, upto, before, ones = (table(x) for x in ("ident", "upto", "before", "ones"))

        def region(at, *dims):
            n = int(np.prod(dims))
            assert at + n <= ARENA, (at, dims)
            v = arena[:, at:at + n]
            if len(dims) == 1:
                return v
            names = "abcd"[:len(dims)]
            return v.rearrange(f"p ({' '.join(names)}) -> p {' '.join(names)}",
                               **{x: d for x, d in zip(names, dims)})

        mixed = hT[:, :, :].rearrange("p c t -> p (c t)").rearrange("p (t n) -> p t n", t=TILES)

        sources = []

        def unit(w, chunks, lo, hi):
            sources.append(w.rearrange("(c p) n -> p c n", p=P)[:, :, lo:hi])
            return len(sources) - 1

        def cut(w, chunks, cols, width):
            return [unit(w, chunks, x, min(x + width, cols)) for x in range(0, cols, width)]

        def expert_units(gate, up, down):
            while len(sources) % SLOTS:
                sources.append(None)
            first = len(sources)
            for pair in range(PAIRS):
                for w in (gate, up, down):
                    for e in (2 * pair, 2 * pair + 1):
                        unit(w[e], DC if w is not down else EC, 0, w.shape[2])
            return first

        def in_and_ada(w, first, each):
            ins, ada = [], []
            for x in range(0, IN1, 512):
                for _ in range(each if x else 0):
                    at = (first + len(ada)) * 512
                    ada.append(unit(a["w_ada_2"][0], DC, at, at + 512))
                ins.append(unit(w, DC, x, min(x + 512, IN1)))
            return ins, ada

        plan, ada_first, ada_each = [], (0, 4), (1, 2)
        for l in range(DEPTH):
            in_units, ada_units = in_and_ada(a["w_in"][l], ada_first[l], ada_each[l])
            plan.append({
                "in": in_units, "ada": ada_units,
                "uq": cut(a["mla_w_uq"][l], 3, 768, 768),
                "ukv": cut(a["mla_w_ukv"][l], 2, 1024, 1024),
                "out": cut(a["w_out"][l], DC, D, 512),
                "experts": expert_units(a["exp_w_gate"][l], a["exp_w_up"][l], a["exp_w_down"][l]),
            })
        plan.append({
            "in": cut(a["w_in_2"][0], DC, IN2, 512),
            "out": cut(a["w_out_2"][0], DC, D, 512),
            "experts": expert_units(a["w1_2"][0], a["w3_2"][0], a["w2_2"][0]),
        })
        landed = [ctx.enter_context(nc.semaphore(f"landed{i}")) for i in range(SLOTS)]
        unit_used = ctx.enter_context(nc.semaphore("unit_used"))
        small_loads = Small(ctx.enter_context(nc.semaphore("small_loads")))
        pool_loads = Small(ctx.enter_context(nc.semaphore("pool_loads")))
        ring = Ring(ring_mem, landed, unit_used, sources)

        @contextmanager
        def stage(*names):
            with ExitStack() as s:
                sems = [s.enter_context(nc.semaphore(x)) for x in names]
                with nc.Block(no_gpsimd_drain=True) as block:
                    yield sems, block
                for x in sems:
                    nc.sync.sem_clear(x)

        class Chain:

            def __init__(self, eng, sem):
                self.eng, self.sem, self.n = eng, sem, 0

            def __call__(self, ins):
                ins.then_inc(self.sem, 1)
                self.n += 1
                self.eng.wait_ge(self.sem, self.n)

        class Alternate:

            def __init__(self, eng, sem):
                self.eng, self.sem, self.n = eng, sem, 0

            def __call__(self, step):
                for t in range(TILES):
                    if self.n >= TILES:
                        self.eng.wait_ge(self.sem, self.n - TILES + 1)
                    step(t).then_inc(self.sem, 1)
                    self.n += 1

            def for_other(self, step, sem):
                for t in range(TILES):
                    self.eng.wait_ge(self.sem, self.n - TILES + 1 + t)
                    step(t).then_inc(sem, 1)

            def settle(self):
                self.eng.wait_ge(self.sem, self.n)

        V, S, G, T = nc.vector, nc.scalar, nc.gpsimd, nc.tensor

        def bc(x, dims, at):
            return x.unsqueeze(at).broadcast_to(tuple(dims))


        def every(x, n):
            return x.rearrange("(o n) -> o n", o=1).broadcast_to((P, n))

        def turn_stage(src, n, rows, dst, sync=None):
            banks = (n + 1) // 2
            with stage("turned", "act_copied", "dve_copied") as ((turned, act_copied, dve_copied), block):
                if sync is not None:
                    block.sync(sync)

                @block.tensor
                def _(pe):
                    for b in range(banks):
                        if b >= BANKS:
                            pe.wait_ge((act_copied, dve_copied)[b % 2], (b - BANKS) // 2 + 1)
                        for i in range(2 * b, min(2 * b + 2, n)):
                            for t in range(TILES):
                                at = (i % 2) * SEQ + t * P
                                last = T.transpose(ps[0:rows, b % BANKS, at:at + P], src(t, i), ident)
                        last.then_inc(turned, 1)

                def copy(eng, b, sem, op):
                    i, m = 2 * b, min(2, n - 2 * b)
                    eng.wait_ge(turned, b + 1)
                    op(dst[0:rows, i:i + m, :], ps[0:rows, b % BANKS, 0:m * SEQ]
                       .rearrange("p (i t) -> p i t", i=m)).then_inc(sem, 1)

                @block.scalar
                def _(act):
                    for b in range(0, banks, 2):
                        copy(act, b, act_copied, lambda o, i: S.activation(o, i, ACT.Copy))

                @block.vector
                def _(dve):
                    for b in range(1, banks, 2):
                        copy(dve, b, dve_copied, V.tensor_copy)

        def project_stage(xT, chunks, jobs, sync=None, early=None, ada=(), sums=None,
                          take=None, prelude=None):
            if not callable(xT):
                xT, chunks = (lambda u, x=xT: x), (lambda u, n=chunks: n)
            names = ("group_done", "act_copied", "dve_copied", "chain", "asked", "answered")
            with stage(*names) as ((group_done, act_copied, dve_copied, chain, asked, answered), block):
                copied = (act_copied, dve_copied)
                signals, n = {}, 0
                for i, (u, *_) in enumerate(jobs):
                    for t in range(TILES):
                        if t == TILES - 1 and (i + 1 == len(jobs) or jobs[i + 1][0] != u):
                            signals[i, t] = (ring.unit_used, ring.after(u), ring.after(u) - u)
                            ring.used = ring.after(u)
                        else:
                            n += 1
                            signals[i, t] = (group_done, n, 1)

                @block.sync
                def _(sp):
                    if early is not None:
                        early(sp)
                    ring.feed(sp, ring.used)
                    if sync is not None:
                        sync(sp)

                @block.tensor
                def _(pe):
                    for i, (u, lo, width, _) in enumerate(jobs):
                        x, n = xT(u), chunks(u)
                        w = ring.view(u, n)
                        pe.wait_ge(ring.landed[u % SLOTS], ring.landings(u))
                        for t in range(TILES):
                            if i >= BANKS // 2:
                                pe.wait_ge(copied[t], i - BANKS // 2 + 1)
                            for c in range(n):
                                if (t, c) == (TILES - 1, n - 1) and u - 1 in ada:
                                    pe.wait_ge(ring.unit_used, u)
                                last = T.matmul(ps[:, (TILES * i + t) % BANKS, 0:width],
                                                x[:, c, t * P:(t + 1) * P], w[:, c, lo:lo + width],
                                                start=c == 0, stop=c == n - 1)
                            sem, _, by = signals[i, t]
                            last.then_inc(sem, by)

                def copy(eng, t, op, before=lambda i: None):
                    for i, (_, _, width, dst) in enumerate(jobs):
                        before(i)
                        sem, value, _ = signals[i, t]
                        eng.wait_ge(sem, value)
                        op(dst(t), ps[:, (TILES * i + t) % BANKS, 0:width]).then_inc(copied[t], 1)

                if take is None:
                    @block.scalar
                    def _(act):
                        if prelude is not None:
                            prelude(None, act, asked, answered)
                        copy(act, 0, lambda o, i: S.activation(o, i, ACT.Copy))

                @block.vector
                def _(dve):
                    link = Chain(dve, chain)
                    if prelude is not None:
                        prelude(link, None, asked, answered)
                    if take is not None:
                        assert TILES * len(jobs) <= BANKS
                        small_loads.arrive(dve)
                        for i, (_, _, width, _) in enumerate(jobs):
                            for t in range(TILES):
                                sem, value, _ = signals[i, t]
                                dve.wait_ge(sem, value)
                                take(link, t, i, ps[:, (TILES * i + t) % BANKS, 0:width])
                        return

                    def sum_ada(i):
                        u = jobs[i][0]
                        for j, x in enumerate(ada):
                            if i + 1 == len(jobs) or not u < x < jobs[i + 1][0]:
                                continue
                            w = ring.view(x, DC)
                            dve.wait_ge(ring.landed[x % SLOTS], ring.landings(x))
                            link(V.tensor_scalar(sums[:, j, :], w[:, 0, :], cond_silu[:, 0:1], None, ALU.mult))
                            for c in range(1, DC):
                                if c == DC - 1:
                                    dve.wait_ge(ring.unit_used, x)
                                ins = V.scalar_tensor_tensor(sums[:, j, :], w[:, c, :], cond_silu[:, c:c + 1],
                                                             sums[:, j, :], ALU.mult, ALU.add)
                                if c < DC - 1:
                                    link(ins)
                            ins.then_inc(ring.unit_used, 1)

                    copy(dve, 1, V.tensor_copy, sum_ada)

        stats = small[:, 0:24].rearrange("p (t s) -> p t s", t=TILES)

        def norm_stage(eps, gain, bias, scale=None, out=h, stats_here=True, turned_to=hT,
                       router=None, sync=None):
            names = ("chain", "summed", "moment", "rooted", "offset_done", "normed", "tile_done", "pool_chain", "turned",
                     "act_copied", "dve_copied", "logits_done")
            with stage(*names) as ((chain, summed, moment, rooted, offset_done, normed, tile_done, pool_chain, turned,
                                    act_copied, dve_copied, logits_done), block):
                centred = scale is None
                mv, moments, roots, scales = (small[:, 24 + a:24 + b] for a, b in ((0, 4), (4, 6), (6, 8), (8, 10)))
                offset, sums = small[:, 34:35], small[:, 36:38]
                factor = gain if centred else scale
                if sync is not None:
                    block.sync(sync)
                half = D // 2
                row_ends = slice(half, D)

                @block.vector
                def _(dve):
                    link = Chain(dve, chain)
                    if centred:
                        for t in range(TILES):
                            if not stats_here:
                                V.bn_stats(stats[:, t, 0:6], h[:, t, 0:half])
                                link(V.bn_stats(stats[:, t, 6:12], h[:, t, row_ends]))
                            link(V.bn_aggr(mv[:, 2 * t:2 * t + 2], stats[:, t, :]))
                        V.tensor_scalar(moments, mv[:, 1:4:2], eps, None, ALU.add).then_inc(moment, 1)
                    else:
                        link(V.scalar_tensor_tensor(scale, scale, 1.0, gain, ALU.add, ALU.mult))
                        dve.wait_ge(summed, TILES)
                        V.tensor_scalar(moments, sums, 1.0 / D, eps, ALU.mult, ALU.add).then_inc(moment, 1)

                    def times_factor(t, cols):
                        if centred:
                            link(V.scalar_tensor_tensor(out[:, t, cols], h[:, t, cols], mv[:, 2 * t:2 * t + 1],
                                                        factor[:, cols], ALU.subtract, ALU.mult))
                        else:
                            link(V.tensor_tensor(out[:, t, cols], h[:, t, cols], factor[:, cols], ALU.mult))

                    def scaled(t, cols):
                        V.scalar_tensor_tensor(out[:, t, cols], out[:, t, cols], scales[:, t:t + 1], bias[:, cols],
                                               ALU.mult, ALU.add).then_inc(tile_done, 1)

                    times_factor(0, slice(0, D))
                    dve.wait_ge(rooted, 1)
                    link(V.reciprocal(scales, roots))
                    if centred:
                        V.scalar_tensor_tensor(offset, mv[:, 2:3], -1.0, scales[:, 1:2], ALU.mult, ALU.mult)\
                            .then_inc(offset_done, 1)
                    else:
                        V.memset(offset, 0.0).then_inc(offset_done, 1)
                    scaled(0, slice(0, D))
                    times_factor(1, slice(0, half))
                    scaled(1, slice(0, half))
                    if turned_to is None:
                        dve.wait_ge(tile_done, 2)
                        return
                    dve.wait_ge(turned, 3)
                    V.tensor_copy(turned_to[:, 0:4, P:], ps[:, 2, :].rearrange("p (c t) -> p c t", c=4))\
                        .then_inc(dve_copied, 1)

                @block.scalar
                def _(act):
                    if not centred:
                        for t in range(TILES):
                            S.activation(out[:, t, :], h[:, t, :], ACT.Square, accum_out=sums[:, t:t + 1])\
                                .then_inc(summed, 1)
                    act.wait_ge(moment, 1)
                    S.activation(roots, moments, ACT.Sqrt).then_inc(rooted, 1)
                    act.wait_ge(offset_done, 1)
                    S.activation(out[:, 1, row_ends], h[:, 1, row_ends], ACT.Identity, bias=offset,
                                 scale=scales[:, 1:2]).then_inc(normed, 1)
                    if turned_to is None:
                        return
                    for b, (tok, cs) in ((0, (slice(0, P), slice(0, 4))), (1, (slice(0, P), slice(4, 8))),
                                         (3, (slice(P, SEQ), slice(4, 8)))):
                        act.wait_ge(turned, b + 1)
                        S.activation(turned_to[:, cs, tok], ps[:, b, :].rearrange("p (c t) -> p c t", c=4), ACT.Copy)\
                            .then_inc(act_copied, 1)

                @block.gpsimd
                def _(pool):
                    link = Chain(pool, pool_chain)
                    pool.wait_ge(normed, 1)
                    x = out[:, 1, row_ends]
                    link(G.tensor_tensor(x, x, factor[:, row_ends], ALU.mult))
                    link(G.tensor_tensor(x, x, bias[:, row_ends], ALU.add))

                if turned_to is not None:
                    @block.tensor
                    def _(pe):
                        def logits(t):
                            w, n = router
                            for c in range(DC):
                                last = T.matmul(ps[:, 4 + t, 0:n], turned_to[:, c, t * P:(t + 1) * P], w[:, c, :],
                                                start=c == 0, stop=c == DC - 1)
                            return last

                        for b in range(4):
                            if b == 3:
                                pe.wait_ge(pool_chain, 2)
                            else:
                                pe.wait_ge(tile_done, b // 2 + 1)
                            for c in range(4):
                                at = (b % 2 * 4 + c) * P
                                last = T.transpose(ps[:, b, c * P:(c + 1) * P], out[:, b // 2, at:at + P], ident)
                            last.then_inc(turned, 1)
                        if router is not None:
                            pe.wait_ge(act_copied, 2)
                            logits(0)
                            pe.wait_ge(act_copied, 3)
                            pe.wait_ge(dve_copied, 1)
                            logits(1).then_inc(logits_done, 1)
                            pe.wait_ge(logits_done, 1)

        def rms_stage(jobs, squares):
            names = ("squared", "chain", "rooted", "moment", "scaled", "pool_chain")
            with stage(*names) as ((squared, chain, rooted, moment, scaled, pool_chain), block):
                at, places, room_at, rooms = 0, [], 0, []
                for x, *_ in jobs:
                    n, w = x.shape[1], x.shape[2]
                    places.append(slice(at, at + n))
                    rooms.append(squares[:, room_at:room_at + n * w].rearrange("p (g w) -> p g w", g=n))
                    at, room_at = at + n, room_at + n * w
                total = at
                assert total <= 80 and room_at <= squares.shape[1]
                sums, means, roots, scales = (small[:, 80 * i:80 * i + total] for i in range(4))

                def scale_jobs(on, link):
                    for i, ((x, out, eps, factors), g) in enumerate(zip(jobs, places)):
                        if (i % (3 if len(jobs) > 4 else 2) == 1) != (on is G):
                            continue
                        link(on.tensor_tensor(out, x, bc(scales[:, g], x.shape, 2), ALU.mult))
                        for f in factors:
                            link(on.tensor_tensor(out, out, f, ALU.mult))

                @block.scalar
                def _(act):
                    for (x, *_), sq in zip(jobs, rooms):
                        S.activation(sq, x, ACT.Square).then_inc(squared, 1)
                    act.wait_ge(moment, len(jobs))
                    S.activation(roots, means, ACT.Sqrt).then_inc(rooted, 1)

                @block.vector
                def _(dve):
                    link = Chain(dve, chain)
                    for i, ((x, out, eps, factors), g) in enumerate(zip(jobs, places)):
                        dve.wait_ge(squared, i + 1)
                        link(V.tensor_reduce(sums[:, g], rooms[i], AX, ALU.add))
                        V.tensor_scalar(means[:, g], sums[:, g], 1.0 / x.shape[2], eps, ALU.mult, ALU.add)\
                            .then_inc(moment, 1)
                    dve.wait_ge(rooted, 1)
                    V.reciprocal(scales, roots).then_inc(scaled, 1)
                    dve.wait_ge(scaled, 1)
                    scale_jobs(V, link)

                @block.gpsimd
                def _(pool):
                    pool.wait_ge(scaled, 1)
                    scale_jobs(G, Chain(pool, pool_chain))

        def attend_stage(heads, dh, qT, kT, value, scale, bias, out, prob, probT, combine=None, sync=None):
            items = [(t, g) for t in reversed(range(TILES)) for g in range(heads // 4)]
            last_item = len(items)
            weights = [prob[:, 4 * i:4 * i + 4, :] for i in range(2)]
            weightsT = [probT[:, 8 * i:8 * i + 8, :] for i in range(2)]
            less_max = [small[:, 4 * i:4 * i + 4] for i in range(2)]
            total = [small[:, 8 + 4 * i:12 + 4 * i] for i in range(2)]
            names = ("scored", "chain", "ready", "weighed", "turned", "copied", "act_copied", "mixed_v", "written")
            with stage(*names) as ((scored, chain, ready, weighed, turned, copied, act_copied, mixed_v, written), block):
                if sync is not None:
                    block.sync(sync)

                def scores(k):
                    return ps[:, 2 * (k % 2):2 * (k % 2) + 2, :].rearrange("p b (j k) -> p (b j) k", j=2)

                turned_p = ps[:, 4:6, :].rearrange("p b (h q) -> p (b h) q", q=P)

                def result(k):
                    return ps[:, 6 + k % 2, 0:4 * HD].rearrange("p (h d) -> p h d", h=4)

                @block.tensor
                def _(pe):
                    def score(k):
                        t, g = items[k]
                        keys = (t + 1) * P
                        if k >= 2:
                            pe.wait_ge(ready, k - 1)
                        for i in range(4):
                            last = T.matmul(scores(k)[:, i, 0:keys], qT[0:dh, 4 * g + i, t * P:(t + 1) * P],
                                            kT[0:dh, 4 * g + i, 0:keys], start=True, stop=True)
                        last.then_inc(scored, 1)

                    score(0)
                    score(1)
                    for k, (t, g) in enumerate(items):
                        pe.wait_ge(weighed, 4 * k + 4)
                        for j in range(t + 1):
                            for i in range(4):
                                last = T.transpose(turned_p[:, 4 * j + i, :],
                                                   weights[k % 2][:, i, j * P:(j + 1) * P], ident)
                        last.then_inc(turned, 1)
                        if k + 2 < last_item:
                            score(k + 2)
                        pe.wait_ge(copied, k + 1)
                        if t:
                            pe.wait_ge(act_copied, sum(x for x, _ in items[:k + 1]))
                        if k >= 2:
                            pe.wait_ge(written, k - 1)
                        for i in range(4):
                            for j in range(t + 1):
                                last = T.matmul(result(k)[:, i, :], weightsT[k % 2][:, 4 * j + i, :],
                                                value(j, 4 * g + i), start=j == 0, stop=j == t)
                        last.then_inc(mixed_v, 1)

                @block.scalar
                def _(act):
                    def weigh(k):
                        t, _ = items[k]
                        act.wait_ge(ready, k + 1)
                        if k >= 2:
                            act.wait_ge(written, k - 1)
                        for i in range(4):
                            x = weights[k % 2][:, i, 0:(t + 1) * P]
                            S.activation(x, x, ACT.Exp, bias=less_max[k % 2][:, i:i + 1],
                                         accum_out=total[k % 2][:, i:i + 1]).then_inc(weighed, 1)

                    weigh(0)
                    for k, (t, _) in enumerate(items):
                        if k + 1 < last_item:
                            weigh(k + 1)
                        if t:
                            act.wait_ge(turned, k + 1)
                            if k >= 2:
                                act.wait_ge(mixed_v, k - 1)
                            S.activation(weightsT[k % 2][:, 4:8, :], turned_p[:, 4:8, :], ACT.Copy)\
                                .then_inc(act_copied, 1)

                @block.vector
                def _(dve):
                    link = Chain(dve, chain)

                    def prepare(k):
                        t, g = items[k]
                        keys = (t + 1) * P
                        s = weights[k % 2][:, :, 0:keys]
                        dve.wait_ge(scored, k + 1)
                        if k >= 2:
                            dve.wait_ge(turned, k - 1)
                        link(V.scalar_tensor_tensor(s, scores(k)[:, :, 0:keys], scale, bias(t, g, keys),
                                                    ALU.mult, ALU.add))
                        V.tensor_reduce(less_max[k % 2], s, AX, ALU.max, negate=True).then_inc(ready, 1)

                    prepare(0)
                    prepare(1)
                    for k, (t, g) in enumerate(items):
                        dve.wait_ge(turned, k + 1)
                        if k >= 2:
                            dve.wait_ge(mixed_v, k - 1)
                        V.tensor_copy(weightsT[k % 2][:, 0:4, :], turned_p[:, 0:4, :]).then_inc(copied, 1)
                        if k + 2 < last_item:
                            prepare(k + 2)
                        dve.wait_ge(weighed, 4 * k + 4)
                        link(V.reciprocal(total[k % 2], total[k % 2]))
                        dve.wait_ge(mixed_v, k + 1)
                        if combine is None:
                            last = V.tensor_tensor(out(t, g), result(k), bc(total[k % 2], (P, 4, HD), 2), ALU.mult)
                        else:
                            last = combine(link, t, g, result(k), total[k % 2])
                        last.then_inc(written, 1)


        ang = small[:, 16:96].rearrange("p (t c f) -> p t c f", t=TILES, c=2)

        def add_residual(link, t, i, products):
            x = h[:, t, 512 * i:512 * (i + 1)]
            link(V.scalar_tensor_tensor(x, x, ALPHA, products, ALU.mult, ALU.add))
            link(V.bn_stats(stats[:, t, 6 * i:6 * i + 6], x))

        def add_gated(link, t, i, products):
            cols = slice(512 * i, 512 * (i + 1))
            x, y = h[:, t, cols], arena[:, 512 * (2 * t + i):512 * (2 * t + i + 1)]
            link(V.tensor_tensor(y, products, p2("gate")[:, cols], ALU.mult))
            link(V.tensor_tensor(x, x, y, ALU.add))

        def trig_program(link, angles):
            pos = small[:, 0:TILES]
            link(V.tensor_copy(pos, positions_i[:, :]))
            turns = small[:, 96:176].rearrange("p (t c f) -> p t c f", t=TILES, c=2)
            a0, n0 = TAB["freq_mla"][0], (MLA_ROPE + DIFF_ROT) // 2
            for t in range(TILES):
                link(V.tensor_scalar(ang[:, t, 1, :], tab[:, a0:a0 + n0], pos[:, t:t + 1], None, ALU.mult))
            magic = 1.5 * 2.0 ** 23
            two_pi = 2 * math.pi
            c1 = 6.28125
            c2 = float(np.float32(np.floor((two_pi - c1) * 2 ** 22) / 2 ** 22))
            c3 = two_pi - c1 - c2
            for t in range(TILES):
                x, y = ang[:, t, 1, :], turns[:, t, 1, :]
                link(V.tensor_scalar(y, x, 1 / two_pi, None, ALU.mult))
                link(V.tensor_scalar(y, y, magic, None, ALU.add))
                link(V.tensor_scalar(y, y, -magic, None, ALU.add))
                for c in (c1, c2, c3):
                    link(V.scalar_tensor_tensor(x, y, -c, x, ALU.mult, ALU.add))
                z = ang[:, t, 0, :]
                link(V.tensor_scalar(z, x, math.pi / 2, None, ALU.add))
                link(V.tensor_scalar(y, z, math.pi, -two_pi, ALU.is_gt, ALU.mult))
                link(V.tensor_tensor(z, z, y, ALU.add))
                V.tensor_scalar(ang[:, t, :, :], ang[:, t, :, :], 3.1415925, -3.1415925, ALU.min, ALU.max)\
                    .then_inc(angles, 1)

        def rope(on, link, x, heads, t, first, n, tmp):
            cos = bc(trig[:, t, 0, first:first + n], (P, heads, n), 1)
            sin = bc(trig[:, t, 1, first:first + n], (P, heads, n), 1)
            x1, x2 = x[:, :, 0:n], x[:, :, n:2 * n]
            y = tmp[:, 0:4 * heads * n].rearrange("p (i h n) -> p i h n", i=4, h=heads)
            on.tensor_tensor(y[:, 0], x1, cos, ALU.mult)
            on.tensor_tensor(y[:, 1], x2, sin, ALU.mult)
            on.tensor_tensor(y[:, 2], x2, cos, ALU.mult)
            link(on.tensor_tensor(y[:, 3], x1, sin, ALU.mult))
            on.tensor_tensor(x1, y[:, 0], y[:, 1], ALU.subtract)
            link(on.tensor_tensor(x2, y[:, 2], y[:, 3], ALU.add))

        PAR1 = {"ln1_g": (0, D), "ln1_b": (D, D), "ln2_g": (2 * D, D), "ln2_b": (3 * D, D), "q_g": (4096, 384),
                "kv_g": (4480, 256), "sub_g": (4736, 64), "fox_b": (4800, 4), "lam": (4804, 128),
                "router_b": (4932, 16)}
        router_w = par[:, 4948:5076].rearrange("p (c e) -> p c e", c=DC)
        cond, cond_silu = par[:, 5076:5084], par[:, 5084:5092]

        def par_at(names, name):
            at, n = names[name]
            return par[:, at:at + n]

        def layer_pairs(l):
            p1 = lambda name: par_at(PAR1, name)
            return [(p1("q_g"), every(a["mla_q_norm_g"][l], 384)), (p1("kv_g"), every(a["mla_kv_norm_g"][l], 256)),
                    (p1("sub_g"), every(a["diff_subln_g"][l], 64)), (p1("fox_b"), every(a["fox_f_bias"][l], 4)),
                    (p1("router_b"), every(a["router_bias"], 16))] + \
                [(p1("lam")[:, 32 * i:32 * i + 32], every(a["diff_lam_" + x][l], 32))
                 for i, x in enumerate(("q1", "k1", "q2", "k2"))]

        def norm_pairs(names, g, b):
            return [(par_at(PAR1, names + "_g"), every(g, D)), (par_at(PAR1, names + "_b"), every(b, D))]

        with stage("x_here", "pos_here", "cond_here", "gains_here", "chain", "angles", "sines") as (
                (x_here, pos_here, cond_here, gains_here, chain, angles, sines), block):
            @block.sync
            def _(sp):
                sp.dma_start(tab[:, 0:TAB_FIRST], a["tab"][:, 0:TAB_FIRST]).then_inc(pos_here, 16)
                sp.dma_start(h[:, :, :], a["x"][0].rearrange("(t p) n -> p t n", p=P)).then_inc(x_here, 16)
                sp.wait_ge(x_here, 16)
                sp.wait_ge(gains_here, 32)

            @block.scalar
            def _(act):
                with nc.allow_non_contiguous_dma("256 positions, 1024 elements"):
                    act.dma_start(positions_i[:, :], a["positions"].rearrange("o (t p) -> p (o t)", p=P))\
                        .then_inc(pos_here, 16)
                    act.dma_start(cond, a["c_2"].rearrange("o (c p) -> p (o c)", p=P)).then_inc(cond_here, 16)
                for dst, src in norm_pairs("ln1", a["ln_in_g"], a["ln_in_b"]):
                    act.dma_start(dst, src).then_inc(gains_here, 16)
                act.wait_ge(cond_here, 16)
                S.activation(cond_silu, cond, ACT.Silu).then_inc(sines, 1)
                act.wait_ge(angles, TILES)
                S.activation(trig[:, :, :, :], ang, ACT.Sin).then_inc(sines, 1)

            @block.vector
            def _(dve):
                dve.wait_ge(pos_here, 32)
                trig_program(Chain(dve, chain), angles)

            @block.gpsimd
            def _(pool):
                pool.wait_ge(x_here, 16)
                with nc.allow_non_contiguous_dma("1024 elements"):
                    pool_loads.send(pool, layer_pairs(0) + [
                        (router_w, a["router_w"].rearrange("(c p) e -> p c e", p=P))])
        norm_stage(1e-5, par[:, 0:D], par[:, D:2 * D], stats_here=False, sync=lambda sp: (
            ring.feed(sp, 0), small_loads.send(sp, [(tab[:, TAB_FIRST:], a["tab"][:, TAB_FIRST:])])))

        def store_stage():
            with stage("store") as ((store,), block):
                @block.sync
                def _(sp):
                    sp.dma_start(outs[0].rearrange("(t p) n -> p t n", p=P), h[:, :, :]).then_inc(store, 16)
                    sp.wait_ge(store, 16)

        gates = small[:, 400:400 + TILES * PADDED].rearrange("p (t e) -> p t e", t=TILES)
        place = small[:, 440:440 + TILES * PADDED].rearrange("p (t e) -> p t e", t=TILES)

        def top2(both, x, t_room):
            vals = lambda t: t_room(t)[:, 0:8]
            hot = lambda t: t_room(t)[:, 8:40].rearrange("p (j e) -> p j e", j=2)
            both(lambda t: V.max(vals(t), x(t)))
            both(lambda t: V.max_index(index[:, 8 * t:8 * t + 8], vals(t), x(t)))
            both(lambda t: V.tensor_copy(t_room(t)[:, 40:48], index[:, 8 * t:8 * t + 8]))
            for j in range(2):
                both(lambda t: V.tensor_scalar(hot(t)[:, j, :], table("iota")[:, 0:N_EXPERTS],
                                               t_room(t)[:, 40 + j:41 + j], None, ALU.is_equal))
            return vals, hot

        def first_of_groups(both, x4, t_room):
            pad, vals = (lambda t: t_room(t)[:, 0:8]), (lambda t: t_room(t)[:, 8:16])
            both(lambda t: V.memset(pad(t)[:, 4:8], -3e38))
            both(lambda t: V.tensor_copy(pad(t)[:, 0:4], x4(t)))
            both(lambda t: V.max(vals(t), pad(t)))
            both(lambda t: V.max_index(index[:, 8 * t:8 * t + 8], vals(t), pad(t)))
            both(lambda t: V.tensor_copy(t_room(t)[:, 16:17], index[:, 8 * t:8 * t + 1]))
            both(lambda t: V.tensor_scalar(t_room(t)[:, 20:24], table("iota")[:, 0:4], t_room(t)[:, 16:17], None,
                                           ALU.is_equal))
            return (lambda t: t_room(t)[:, 20:24]), vals

        def keep_group(both, out, x, group, t_room):
            full = lambda t: t_room(t)[:, 0:16].rearrange("p (g e) -> p g e", g=4)
            off = lambda t: t_room(t)[:, 16:20]
            groups = lambda y: y.rearrange("p (g e) -> p g e", g=4)
            both(lambda t: V.tensor_scalar(off(t), group(t), -NEG, NEG, ALU.mult, ALU.add))
            both(lambda t: V.tensor_tensor(full(t), groups(x(t)), bc(group(t), (P, 4, 4), 2), ALU.mult))
            both(lambda t: V.tensor_tensor(groups(out(t)), full(t), bc(off(t), (P, 4, 4), 2), ALU.add))

        def routing(a, b):
            return lambda t: small[:, 32 + 172 * t + a:32 + 172 * t + b]

        def route1(both, asked, dve, answered):
            router_b = par_at(PAR1, "router_b")
            biased, tops, lows, work4, recip = (routing(*x) for x in ((0, 16), (16, 24), (24, 32), (32, 44), (44, 46)))
            score = lambda t: small[:, 16 * t:16 * t + 16]
            by_group = lambda x: x.rearrange("p (g e) -> p g e", g=4)
            dve.wait_ge(answered, 1)
            both(lambda t: V.tensor_tensor(biased(t), score(t), router_b, ALU.add))
            even, odd = (lambda t: by_group(biased(t))[:, :, 0:4:2]), (lambda t: by_group(biased(t))[:, :, 1:4:2])
            hi, lo = (lambda t: by_group(tops(t))), (lambda t: by_group(lows(t)))
            both(lambda t: V.tensor_tensor(hi(t), even(t), odd(t), ALU.max))
            both(lambda t: V.tensor_tensor(lo(t), even(t), odd(t), ALU.min))
            both(lambda t: V.tensor_reduce(work4(t)[:, 0:4], hi(t), AX, ALU.max))
            both(lambda t: V.tensor_reduce(work4(t)[:, 4:8], hi(t), AX, ALU.min))
            both(lambda t: V.tensor_reduce(work4(t)[:, 8:12], lo(t), AX, ALU.max))
            both(lambda t: V.tensor_tensor(work4(t)[:, 4:8], work4(t)[:, 4:8], work4(t)[:, 8:12], ALU.max))
            both(lambda t: V.tensor_tensor(work4(t)[:, 0:4], work4(t)[:, 0:4], work4(t)[:, 4:8], ALU.add))
            group, _ = first_of_groups(both, lambda t: work4(t)[:, 0:4], routing(48, 72))
            masked = routing(72, 88)
            keep_group(both, masked, biased, group, routing(88, 108))
            _, hot = top2(both, masked, routing(108, 172))
            picked = routing(16, 32)
            both(lambda t: V.tensor_tensor(place[:, t, 0:N_EXPERTS], hot(t)[:, 0, :], hot(t)[:, 1, :], ALU.add))
            both(lambda t: V.tensor_tensor(picked(t), place[:, t, 0:N_EXPERTS], score(t), ALU.mult))
            both(lambda t: V.tensor_reduce(recip(t)[:, 0:1], picked(t), AX, ALU.add))
            both(lambda t: V.reciprocal(recip(t)[:, 1:2], recip(t)[:, 0:1]))
            both(lambda t: V.tensor_scalar(gates[:, t, 0:N_EXPERTS], picked(t), recip(t)[:, 1:2], None, ALU.mult))

        def score1(act, asked, answered):
            S.activation(small[:, 0:32].rearrange("p (t e) -> p t e", t=TILES), ps[:, 4:6, 0:16],
                         ACT.Sigmoid).then_inc(answered, 1)

        def route2(both, asked, dve, answered):
            logit, less_max, grown, second = (routing(*x) for x in ((0, 20), (156, 160), (160, 164), (164, 166)))
            sums, weighed = routing(166, 171), routing(20, 36)
            both(lambda t: V.tensor_tensor(logit(t), ps[:, 4 + t, 0:20], p2("route_b"), ALU.add))
            group, vals = first_of_groups(both, lambda t: logit(t)[:, 0:4], routing(48, 72))
            both.for_other(lambda t: V.tensor_scalar(less_max(t), logit(t)[:, 0:4], vals(t)[:, 0:1], None, ALU.subtract),
                        asked)
            masked = routing(72, 88)
            keep_group(both, masked, lambda t: logit(t)[:, 4:20], group, routing(88, 108))
            vals, hot = top2(both, masked, routing(108, 156))
            both.for_other(lambda t: V.tensor_tensor(second(t)[:, 0:1], vals(t)[:, 1:2], vals(t)[:, 0:1], ALU.subtract),
                        asked)
            dve.wait_ge(answered, 2 * TILES)
            both(lambda t: V.tensor_reduce(sums(t)[:, 0:1], grown(t), AX, ALU.add))
            both(lambda t: V.tensor_scalar(sums(t)[:, 1:2], second(t)[:, 1:2], 1.0, None, ALU.add))
            both(lambda t: V.tensor_tensor(sums(t)[:, 2:3], sums(t)[:, 0:1], sums(t)[:, 1:2], ALU.mult))
            both(lambda t: V.reciprocal(sums(t)[:, 3:4], sums(t)[:, 2:3]))
            both(lambda t: V.tensor_tensor(sums(t)[:, 4:5], sums(t)[:, 3:4], second(t)[:, 1:2], ALU.mult))
            both(lambda t: V.tensor_scalar(weighed(t), hot(t)[:, 0, :], sums(t)[:, 3:4], None, ALU.mult))
            both(lambda t: V.tensor_tensor(place[:, t, 0:N_EXPERTS], hot(t)[:, 0, :], hot(t)[:, 1, :], ALU.add))
            both(lambda t: V.scalar_tensor_tensor(gates[:, t, 0:N_EXPERTS], hot(t)[:, 1, :], sums(t)[:, 4:5],
                                                  weighed(t), ALU.mult, ALU.add))

        def score2(act, asked, answered):
            less_max, grown, second = (routing(*x) for x in ((156, 160), (160, 164), (164, 166)))
            for t in range(TILES):
                act.wait_ge(asked, t + 1)
                S.activation(grown(t), less_max(t), ACT.Exp).then_inc(answered, 1)
            for t in range(TILES):
                act.wait_ge(asked, TILES + t + 1)
                S.activation(second(t)[:, 1:2], second(t)[:, 0:1], ACT.Exp).then_inc(answered, 1)

        zeros = region(TILES * D + 4352, P + 512)

        def route_stage(score, route):
            names = ("cleared", "chain", "asked", "answered", "chosen_done", "counted", "settled")
            with stage(*names) as ((cleared, chain, asked, answered, chosen_done, counted, settled), block):
                chosen = [place[:, t, 0:N_EXPERTS] for t in range(TILES)]

                @block.gpsimd
                def _(pool):
                    G.memset(zeros, 0.0).then_inc(cleared, 1)
                    pool.wait_ge(cleared, 1)

                @block.tensor
                def _(pe):
                    pe.wait_ge(cleared, 1)
                    for b in range(4):
                        T.matmul(ps[:, b, :], zeros[:, 0:P], zeros[:, P:], start=True, stop=True)
                    pe.wait_ge(chosen_done, 1)
                    T.matmul(ps[:, 6, 0:16], before, chosen[0], start=True, stop=True)
                    T.matmul(ps[:, 7, 0:16], ones, chosen[0], start=True, stop=False)
                    T.matmul(ps[:, 7, 0:16], before, chosen[1], start=False, stop=True)
                    T.matmul(ps[:, 4, 0:16], ones, chosen[0], start=True, stop=False)
                    T.matmul(ps[:, 4, 0:16], ones, chosen[1], start=False, stop=True).then_inc(counted, 1)

                @block.scalar
                def _(act):
                    score(act, asked, answered)

                @block.vector
                def _(dve):
                    both = Alternate(dve, chain)
                    both(lambda t: V.memset(place[:, t, N_EXPERTS:], 0.0))
                    both(lambda t: V.memset(gates[:, t, N_EXPERTS:], 0.0))
                    route(both, asked, dve, answered)
                    both.settle()
                    V.memset(small[:, 0:1], 0.0).then_inc(chosen_done, 1)
                    dve.wait_ge(counted, 1)
                    both(lambda t: V.scalar_tensor_tensor(chosen[t], ps[:, 6 + t, 0:16], 1.0, chosen[t],
                                                          ALU.add, ALU.mult))
                    both(lambda t: V.tensor_scalar(place[:, t, :], place[:, t, :], -1.0, None, ALU.add))
                    V.tensor_reduce(small[:, 1:2], ps[:, 4, 0:16], AX, ALU.max).then_inc(settled, 1)
                    dve.wait_ge(settled, 1)
                    V.tensor_scalar(crowded[:, :], small[:, 1:2], float(CAP), None, ALU.is_gt).then_inc(settled, 1)

        def experts_stage(first, tokens, pairs, take):
            at = TILES * D
            sig, rows = region(at, 512), region(at + 512, 512)
            actT = region(at + 1024, EC, P)
            picked = region(at + 1536, DC, P)
            sel = region(at + 2560, TILES, 2, CAP)
            sel_gate = region(at + 2816, TILES, 2, CAP)
            selT = region(at + 3072, TILES * P)
            out_rows = region(at + 3328, D)
            flat = lambda x: x.rearrange("p e s -> p (e s)")
            W = [ring_mem[:, j, :].rearrange("p (c w) -> p c w", c=DC if j < 4 else EC) for j in range(SLOTS)]
            here = [ring.landings(first + j) for j in range(SLOTS)]
            assert ring.used == first
            ring.used = first + 3 * N_EXPERTS
            mats = sources_of[first]
            names = ("sel_done", "sel_gate_done", "gathered", "picked_lo", "picked_hi", "sig_done",
                     "rows_done", "turned", "actT_done", "selT_done", "down_lo", "out_lo", "out_hi", "scattered",
                     "gu_done", "d_sig", "d_rows", "d_turned", "d_actT", "d_down", "chain")
            with stage(*names) as (sems, block):
                (sel_done, sel_gate_done, gathered, picked_lo, picked_hi, sig_done, rows_done, turned,
                 actT_done, selT_done, down_lo, out_lo, out_hi, scattered,
                 gu_done, d_sig, d_rows, d_turned, d_actT, d_down, chain) = sems

                def is_crowded(eng):
                    return eng.value_load(crowded[0:1, 0:1], min_val=0, max_val=1) > 0

                @block.gpsimd
                def _(pool):
                    pool_loads.send(pool, pairs)
                    pool_loads.arrive(pool)

                @block.sync
                def _(sp):
                    ring.feed(sp, first)
                    assert ring.sent == first + SLOTS
                    with sp.Fori(1, PAIRS) as i:
                        for j in range(SLOTS):
                            w = mats[j // 2][bass.ds(2 * i + j % 2, 1)].rearrange("o (c p) n -> p (o c) n", p=P)
                            sp.wait_ge(unit_used, i * SLOTS + (first - SLOTS + 2 * (j // 2) + 2))
                            sp.dma_start(W[j], w).then_inc(landed[j], 16)
                    ring.sent = first + 3 * N_EXPERTS
                    ring.feed(sp, first + 3 * N_EXPERTS)

                @block.tensor
                def _(pe):
                    def gather(half):
                        for c in range(4 * half, 4 * half + 4):
                            for t in range(TILES):
                                last = T.matmul(ps[:, 4 + half, (c % 4) * P:(c % 4 + 1) * P],
                                                tokens[:, t, c * P:(c + 1) * P], flat(sel[:, t]),
                                                start=t == 0, stop=t == TILES - 1)
                        return last

                    with pe.If(is_crowded(pe)):
                        with pe.Fori(0, PAIRS) as i:
                            for e in range(2):
                                for t in range(TILES):
                                    n = 2 * e + t
                                    for m in range(2):
                                        if t == 0:
                                            pe.wait_ge(landed[2 * m + e], i * 16 + here[2 * m + e])
                                        if m == 0:
                                            pe.wait_ge(d_rows, i * 4 + n)
                                        for c in range(DC):
                                            last = T.matmul(ps[:, 4 + m, :], hT[:, c, t * P:(t + 1) * P],
                                                            W[2 * m + e][:, c, :], start=c == 0, stop=c == DC - 1)
                                        last.then_inc(gu_done, 1)
                                    pe.wait_ge(d_rows, i * 4 + (n + 1))
                                    for k in range(EC):
                                        last = T.transpose(ps[:, 6, k * P:(k + 1) * P],
                                                           rows[:, k * P:(k + 1) * P], ident)
                                    last.then_inc(d_turned, 1)
                                    if t == 0:
                                        pe.wait_ge(landed[4 + e], i * 16 + here[4 + e])
                                    pe.wait_ge(d_actT, i * 4 + (n + 1))
                                    for k in range(EC):
                                        for x in range(2):
                                            last = T.matmul(ps[:, 2 * t + x, :], actT[:, k, :],
                                                            W[4 + e][:, k, x * 512:(x + 1) * 512],
                                                            start=False, stop=True, skip_group_check=True)
                                    last.then_inc(d_down, 1)
                            pe.wait_ge(d_down, i * 4 + 4)
                            pe.sem_inc(unit_used, SLOTS)
                    with pe.Else():
                        pe.wait_ge(sel_done, 1)
                        gather(0).then_inc(gathered, 1)
                        gather(1).then_inc(gathered, 1)
                        with pe.Fori(0, PAIRS) as i:
                            pe.wait_ge(picked_lo, i + 1)
                            pe.wait_ge(picked_hi, i + 1)
                            for m in range(2):
                                for e in range(2):
                                    pe.wait_ge(landed[2 * m + e], i * 16 + here[2 * m + e])
                                for c in range(DC):
                                    for e in range(2):
                                        last = T.matmul(ps[CAP * e:CAP * e + CAP, 6 + m, :],
                                                        picked[:, c, CAP * e:CAP * e + CAP], W[2 * m + e][:, c, :],
                                                        start=c == 0, stop=c == DC - 1)
                                last.then_inc(unit_used, 2)
                            pe.wait_ge(sel_done, i + 2)
                            gather(0).then_inc(gathered, 1)
                            pe.wait_ge(rows_done, i + 1)
                            for k in range(EC):
                                T.transpose(ps[:, 6, k * P:(k + 1) * P], rows[:, k * P:(k + 1) * P], ident)
                            pe.wait_ge(sel_gate_done, i + 1)
                            for t in range(TILES):
                                last = T.transpose(ps[:, 7, t * P:(t + 1) * P], flat(sel_gate[:, t]), ident)
                            last.then_inc(turned, 1)
                            gather(1).then_inc(gathered, 1)
                            pe.wait_ge(actT_done, i + 1)
                            pe.wait_ge(selT_done, i + 1)
                            for e in range(2):
                                pe.wait_ge(landed[4 + e], i * 16 + here[4 + e])
                            for x in range(2):
                                for k in range(EC):
                                    for e in range(2):
                                        last = T.matmul(ps[CAP * e:CAP * e + CAP, 6 + x, :],
                                                        actT[:, k, CAP * e:CAP * e + CAP],
                                                        W[4 + e][:, k, x * 512:(x + 1) * 512],
                                                        start=k == 0, stop=k == EC - 1)
                                if x == 0:
                                    last.then_inc(down_lo, 1)
                                else:
                                    last.then_inc(unit_used, 2)
                            for x, sem in ((0, out_lo), (1, out_hi)):
                                pe.wait_ge(sem, i + 1)
                                for t in range(TILES):
                                    last = T.matmul(ps[:, 2 * t + x, :], selT[:, t * P:(t + 1) * P],
                                                    out_rows[:, x * 512:(x + 1) * 512],
                                                    start=False, stop=True, skip_group_check=True)
                            last.then_inc(scattered, 1)

                @block.scalar
                def _(act):
                    with act.If(is_crowded(act)):
                        with act.Fori(0, PAIRS) as i:
                            for n in range(4):
                                act.wait_ge(gu_done, i * 8 + (2 * n + 1))
                                act.wait_ge(d_rows, i * 4 + n)
                                S.activation(sig, ps[:, 4, :], ACT.Silu).then_inc(d_sig, 1)
                                act.wait_ge(d_turned, i * 4 + (n + 1))
                                act.wait_ge(d_down, i * 4 + n)
                                S.activation(actT.rearrange("p k t -> p (k t)"), ps[:, 6, :], ACT.Copy)\
                                    .then_inc(d_actT, 1)
                    with act.Else():
                        lo = picked[:, 0:4, :].rearrange("p c s -> p (c s)")
                        act.wait_ge(gathered, 1)
                        S.activation(lo, ps[:, 4, :], ACT.Copy).then_inc(picked_lo, 1)
                        with act.Fori(0, PAIRS) as i:
                            act.wait_ge(unit_used, i * SLOTS + (first + 2))
                            act.wait_ge(rows_done, i)
                            S.activation(sig, ps[:, 6, :], ACT.Silu).then_inc(sig_done, 1)
                            act.wait_ge(gathered, i * 2 + 3)
                            S.activation(lo, ps[:, 4, :], ACT.Copy).then_inc(picked_lo, 1)
                            act.wait_ge(turned, i + 1)
                            act.wait_ge(unit_used, i * SLOTS + first)
                            S.activation(actT.rearrange("p k t -> p (k t)"), ps[:, 6, :], ACT.Copy)\
                                .then_inc(actT_done, 1)
                            act.wait_ge(down_lo, i + 1)
                            act.wait_ge(scattered, i)
                            S.activation(out_rows[:, 0:512], ps[:, 6, :], ACT.Copy).then_inc(out_lo, 1)

                @block.vector
                def _(dve):
                    def one_hots(pair):
                        return V.tensor_tensor(sel, bc(bc(table("iota"), (P, 2, CAP), 1), (P, TILES, 2, CAP), 1),
                                               bc(place[:, :, bass.ds(2 * pair, 2)], (P, TILES, 2, CAP), 3),
                                               ALU.is_equal)

                    def gated(pair):
                        return V.tensor_tensor(sel_gate, sel, bc(gates[:, :, bass.ds(2 * pair, 2)],
                                                                 (P, TILES, 2, CAP), 3), ALU.mult)

                    with dve.If(is_crowded(dve)):
                        with dve.Fori(0, PAIRS) as i:
                            for n in range(4):
                                e, t = n // 2, n % 2
                                dve.wait_ge(gu_done, i * 8 + (2 * n + 2))
                                dve.wait_ge(d_sig, i * 4 + (n + 1))
                                dve.wait_ge(d_turned, i * 4 + n)
                                V.scalar_tensor_tensor(rows, sig, gates[:, t, bass.ds(2 * i + e, 1)], ps[:, 5, :],
                                                       ALU.mult, ALU.mult).then_inc(d_rows, 1)
                        dve.wait_ge(d_down, 2 * N_EXPERTS)
                    with dve.Else():
                        hi = picked[:, 4:8, :].rearrange("p c s -> p (c s)")
                        one_hots(0).then_inc(sel_done, 1)
                        dve.wait_ge(sel_done, 1)
                        gated(0).then_inc(sel_gate_done, 1)
                        dve.wait_ge(gathered, 2)
                        V.tensor_copy(hi, ps[:, 5, :]).then_inc(picked_hi, 1)
                        with dve.Fori(0, PAIRS) as i:
                            dve.wait_ge(sel_gate_done, i + 1)
                            one_hots(i + 1).then_inc(sel_done, 1)
                            dve.wait_ge(unit_used, i * SLOTS + (first + 4))
                            dve.wait_ge(sig_done, i + 1)
                            V.tensor_tensor(rows, sig, ps[:, 7, :], ALU.mult).then_inc(rows_done, 1)
                            dve.wait_ge(turned, i + 1)
                            V.tensor_copy(selT, ps[:, 7, 0:SEQ]).then_inc(selT_done, 1)
                            dve.wait_ge(sel_done, i + 2)
                            gated(i + 1).then_inc(sel_gate_done, 1)
                            dve.wait_ge(gathered, i * 2 + 4)
                            V.tensor_copy(hi, ps[:, 5, :]).then_inc(picked_hi, 1)
                            dve.wait_ge(unit_used, i * SLOTS + (first + 6))
                            V.tensor_copy(out_rows[:, 512:], ps[:, 7, :]).then_inc(out_hi, 1)
                        dve.wait_ge(scattered, PAIRS)
                    link = Chain(dve, chain)
                    if take is add_gated:
                        pool_loads.arrive(dve)
                    for t in range(TILES):
                        for x in range(2):
                            take(link, t, x, ps[:, 2 * t + x, :])

        sources_of = {plan[l]["experts"]: (a["exp_w_gate"][l], a["exp_w_up"][l], a["exp_w_down"][l])
                      for l in range(DEPTH)}
        sources_of[plan[DEPTH]["experts"]] = (a["w1_2"][0], a["w3_2"][0], a["w2_2"][0])

        def output_stage(units, pairs, take):
            oT = region(TILES * D, DC, SEQ)
            turn_stage(lambda t, c: mixed[:, t, c * P:(c + 1) * P], DC, P, oT,
                       lambda sp: (small_loads.arrive(sp), small_loads.send(sp, pairs)))
            project_stage(oT, DC, [(u, 0, 512, None) for u in units], small_loads.arrive, take=take)

        def ada_pairs(n, first):
            return [(par[32 * (j % 4):32 * (j % 4) + 1, 512 * (j // 4):512 * (j // 4 + 1)],
                     a["b_ada_2"][0:1, 512 * (first + j):512 * (first + j + 1)]) for j in range(n)]

        def modulation_stage(sums, first):
            n = sums.shape[1]
            rows = par[:, 0:n // 4 * 512].rearrange("p (b n) -> p b n", b=n // 4)
            with stage("summed", "added") as ((summed, added), block):
                @block.tensor
                def _(pe):
                    for j in range(n):
                        g = j % 4
                        last = T.matmul(ps[32 * g:32 * g + 32, j // 4, :], ones[:, 0:32], sums[:, j, :],
                                        start=True, stop=True)
                    last.then_inc(summed, 1)

                @block.vector
                def _(dve):
                    dve.wait_ge(summed, 1)
                    V.tensor_tensor(rows, rows, ps[:, 0:n // 4, :], ALU.add).then_inc(added, 1)

                @block.sync
                def _(sp):
                    sp.wait_ge(added, 1)
                    small_loads.send(sp, [
                        (scratch["mod"][(first + 4 * b) * 512:(first + 4 * b + 4) * 512]
                         .rearrange("(g n) -> g n", g=4), rows[0:P:32, b, :]) for b in range(n // 4)])

        PAR2 = {"norm_g": (0, D), "rec_g": (1024, 512), "buckets": (1536, 512), "work": (0, TILES * SEQ),
                "gate": (1024, D), "room": (2048, 2048), "att_g": (4096, 512), "q_g": (4608, 64),
                "k_g": (4672, 64), "idx_g": (4736, 64), "idx_b": (4800, 64), "route_b": (4864, 20),
                "rel": (4884, HEADS)}
        p2 = lambda name: par_at(PAR2, name)
        mod_in = region(10 * D, 2, D)

        def kept_mod(i):
            return every(scratch["mod"][i * D:(i + 1) * D], D)

        logits = region(TILES * IN2 + 4096, 2, 512)

        def second_pairs():
            return [(logits[:, i, :], every(a["lb_logits_2"][i], 512)) for i in range(2)] + [
                    (p2("norm_g"), every(a["norm1_g_2"][0], D)), (p2("rec_g"), every(a["rec_out_g_2"][0], 512)),
                    (p2("att_g"), every(a["attn_out_g_2"][0], 512)), (p2("q_g"), every(a["q_norm_g_2"][0], 64)),
                    (p2("k_g"), every(a["k_norm_g_2"][0], 64)), (p2("idx_g"), every(a["idx_k_norm_g_2"][0], 64)),
                    (p2("idx_b"), every(a["idx_k_norm_b_2"][0], 64)),
                    (p2("route_b")[:, 0:4], every(a["b_rg_2"][0], 4)),
                    (p2("route_b")[:, 4:20], every(a["b_re_2"][0], 16)),
                    (p2("buckets")[0:BUCKETS], a["bucket"]), (p2("rel")[0:BUCKETS], a["rel_bias_2"]),
                    (mod_in[:, 0], kept_mod(0)), (mod_in[:, 1], kept_mod(1))]

        for l in range(DEPTH):
            lam_init = 0.8 - 0.6 * math.exp(-0.3 * l)
            p1 = lambda name: par_at(PAR1, name)
            z = region(0, TILES, IN1)
            base = TILES * IN1
            ada = plan[l]["ada"]
            ada_sums = region(base + 6144, len(ada), 512)
            project_stage(hT, DC, [(u, 0, min(512, IN1 - 512 * i),
                                    lambda t, i=i: z[:, t, 512 * i:min(512 * i + 512, IN1)])
                                   for i, u in enumerate(plan[l]["in"])],
                          lambda sp: (small_loads.arrive(sp), pool_loads.arrive(sp)),
                          lambda sp: small_loads.send(sp, ada_pairs(len(ada), ada_first[l])), ada, ada_sums)
            modulation_stage(ada_sums, ada_first[l])
            kv = region(base, TILES, HEADS, 128)
            qT, kT = region(base + 2048, HEADS, SEQ), region(base + 4096, HEADS, SEQ)
            prob, probT = region(base + 6144, HEADS, SEQ), region(base + 8192, TILES * HEADS, P)
            rms_stage([(z[:, t, o:o + w].unsqueeze(1), z[:, t, o:o + w].unsqueeze(1), 1e-6,
                        [p1(g).unsqueeze(1)])
                       for t in range(TILES) for o, w, g in ((0, MLA_Q, "q_g"), (MLA_Q, MLA_KV, "kv_g"))],
                      region(base + 6144, 2048))
            cT = region(base + 2048, 5, SEQ)
            turn_stage(lambda t, c: z[:, t, c * P:(c + 1) * P], 5, P, cT)
            q96 = region(base + 6144, TILES, HEADS, MLA_QK)
            q_flat = q96.rearrange("p t h d -> p t (h d)")
            kv_flat = kv.rearrange("p t h d -> p t (h d)")
            uq, ukv = plan[l]["uq"][0], plan[l]["ukv"][0]
            project_stage(lambda u: cT[:, 0:3, :] if u == uq else cT[:, 3:5, :], lambda u: 3 if u == uq else 2,
                          [(uq, o, w, lambda t, o=o, w=w: q_flat[:, t, o:o + w]) for o, w in ((0, 512), (512, 256))] +
                          [(ukv, o, 512, lambda t, o=o: kv_flat[:, t, o:o + 512]) for o in (0, 512)])
            k96 = region(base + 8192, TILES, HEADS, MLA_QK)
            tmp = region(base + 2048, 2048)

            r0 = MLA_Q + MLA_KV
            d0 = r0 + MLA_ROPE
            names = ("dve_chain", "pool_chain", "act_chain")
            with stage(*names) as ((dve_chain, pool_chain, act_chain), block):
                def rope_mla(on, link, t):
                    mine = tmp[:, 1024 * t:1024 * (t + 1)]
                    rope(on, link, z[:, t, r0:r0 + MLA_ROPE].unsqueeze(1), 1, t, 0, MLA_ROPE // 2, mine[:, 512:576])
                    rope(on, link, q96[:, t, :, MLA_NOPE:], HEADS, t, 0, MLA_ROPE // 2, mine[:, 0:512])

                def rope_diff(on, link, t):
                    rope(on, link, z[:, t, d0:d0 + 512].rearrange("p (h d) -> p h d", h=16), 16, t, MLA_ROPE // 2,
                         DIFF_ROT // 2, tmp[:, 1024 * t + 576:1024 * t + 832])

                @block.vector
                def _(dve):
                    link = Chain(dve, dve_chain)
                    rope_mla(V, link, 0)
                    rope_diff(V, link, 0)
                    rope_diff(V, link, 1)

                @block.gpsimd
                def _(pool):
                    rope_mla(G, Chain(pool, pool_chain), 1)

                @block.scalar
                def _(act):
                    for t in range(TILES):
                        S.activation(k96[:, t, :, 0:MLA_NOPE], kv[:, t, :, 0:MLA_NOPE], ACT.Copy).then_inc(act_chain, 1)
                    for t, sem in enumerate((dve_chain, pool_chain)):
                        act.wait_ge(sem, 2)
                        S.activation(k96[:, t, :, MLA_NOPE:], bc(z[:, t, r0:r0 + MLA_ROPE], (P, HEADS, MLA_ROPE), 1),
                                     ACT.Copy).then_inc(act_chain, 1)

            qkT = region(base + 2048, 2 * HEADS, SEQ)
            turn_stage(lambda t, i: (q96 if i < HEADS else k96)[:, t, i % HEADS, :], 2 * HEADS, MLA_QK, qkT)
            out8 = mixed.rearrange("p t (h d) -> p t h d", d=HD)
            masks = {n: table(n).rearrange("p (t k) -> p t k", t=TILES) for n in ("chunk_mask", "causal_mask")}

            def chunk_bias(t, g, keys):
                return bc(masks["chunk_mask"][:, t, 0:keys], (P, 4, keys), 1)

            attend_stage(HEADS, MLA_QK, qT, kT, lambda j, i: kv[:, j, i, MLA_NOPE:], MLA_QK ** -0.5, chunk_bias,
                         lambda t, g: out8[:, t, 4 * g:4 * g + 4, :], prob, probT, sync=small_loads.arrive)
            d0 = MLA_Q + MLA_KV + MLA_ROPE
            turn_stage(lambda t, i: z[:, t, d0 + 32 * i:d0 + 32 * i + 32], 2 * HEADS, DIFF_QK, qkT)
            lam = small[:, 500:501]

            f0 = d0 + 768
            log_f = small[:, 256:264].rearrange("p (t h) -> p t h", t=TILES)
            with stage("chain", "asked", "answered") as ((chain, asked, answered), block):
                w = small[:, 128:192].rearrange("p (j d) -> p j d", j=2)
                lams = p1("lam").rearrange("p (j i d) -> p j i d", j=2, i=2)
                x, n, e, m = (small[:, 200 + 8 * i:208 + 8 * i] for i in range(4))

                @block.vector
                def _(dve):
                    link = Chain(dve, chain)
                    link(V.tensor_tensor(w, lams[:, :, 0, :], lams[:, :, 1, :], ALU.mult))
                    V.tensor_reduce(small[:, 192:194], w, AX, ALU.add).then_inc(asked, 1)
                    link(V.tensor_tensor(x.rearrange("p (t h) -> p t h", t=TILES), z[:, :, f0 + 768:f0 + 772],
                                         bc(p1("fox_b"), (P, TILES, 4), 1), ALU.add))
                    link(V.tensor_scalar(n, x, -1.0, None, ALU.mult))
                    V.tensor_tensor(n, n, x, ALU.min).then_inc(asked, 1)
                    link(V.tensor_scalar(m, x, 0.0, None, ALU.min))
                    link(V.tensor_scalar(p1("sub_g"), p1("sub_g"), 1.0 - lam_init, None, ALU.mult))
                    dve.wait_ge(answered, 1)
                    link(V.tensor_tensor(small[:, 196:197], small[:, 194:195], small[:, 195:196], ALU.subtract))
                    link(V.tensor_scalar(lam, small[:, 196:197], lam_init, None, ALU.add))
                    dve.wait_ge(answered, 3)
                    link(V.tensor_tensor(small[:, 256:264], m, e, ALU.subtract))

                @block.scalar
                def _(act):
                    act.wait_ge(asked, 1)
                    S.activation(small[:, 194:196], small[:, 192:194], ACT.Exp).then_inc(answered, 1)
                    act.wait_ge(asked, 2)
                    S.activation(e, n, ACT.Exp).then_inc(answered, 1)
                    act.wait_ge(answered, 2)
                    S.activation(e, e, ACT.Ln, bias=1.0).then_inc(answered, 1)

            def diff_combine(link, t, g, res, total):
                both = region(base, 4, HD)
                link(V.tensor_tensor(both, res, bc(total, (P, 4, HD), 2), ALU.mult))
                pair = both.rearrange("p (h j) d -> p h j d", j=2)
                odd = region(base + 512, 2, HD)
                link(V.tensor_scalar(odd, pair[:, :, 1, :], lam, None, ALU.mult))
                return V.tensor_tensor(out8[:, t, 8 + 2 * g:10 + 2 * g, :], pair[:, :, 0, :], odd, ALU.subtract)

            attend_stage(HEADS, DIFF_QK, qT, kT,
                         lambda j, i: z[:, j, d0 + 512 + (i // 2) * HD:d0 + 512 + (i // 2 + 1) * HD],
                         DIFF_QK ** -0.5, chunk_bias, None, prob, probT, diff_combine, small_loads.arrive)
            rms_stage([(out8[:, t, 8:12, :], out8[:, t, 8:12, :], 1e-6, [bc(p1("sub_g"), (P, 4, HD), 1)])
                       for t in range(TILES)], region(base, 2048))
            turn_stage(lambda t, i: z[:, t, f0 + HD * i:f0 + HD * i + HD], 2 * FOX_HEADS, HD, qkT)
            fox_kT = qkT[:, FOX_HEADS:2 * FOX_HEADS, :]
            cum = small[:, 264:272].rearrange("p (t h) -> p t h", t=TILES)
            fox = region(base, TILES, FOX_HEADS, SEQ)

            with stage("summed", "cum_done", "lessened", "dve_masked", "pool_masked") as (
                    (summed, cum_done, lessened, dve_masked, pool_masked), block):
                @block.tensor
                def _(pe):
                    T.matmul(ps[:, 0, 0:4], upto, log_f[:, 0, :], start=True, stop=True)
                    T.matmul(ps[:, 1, 0:4], ones, log_f[:, 0, :], start=True, stop=False)
                    T.matmul(ps[:, 1, 0:4], upto, log_f[:, 1, :], start=False, stop=True).then_inc(summed, 1)
                    for i in range(FOX_HEADS):
                        f = [log_f[:, t, i:i + 1].broadcast_to((P, P)) for t in range(TILES)]
                        row = ps[:, 2 + i, :]
                        T.matmul(row[:, 0:P], f[0], upto, start=True, stop=True)
                        T.matmul(row[:, P:SEQ], f[0], ones, start=True, stop=False)
                        T.matmul(row[:, P:SEQ], f[1], upto, start=False, stop=True).then_inc(summed, 1)

                @block.scalar
                def _(act):
                    act.wait_ge(cum_done, 1)
                    for i in range(FOX_HEADS):
                        act.wait_ge(summed, i + 2)
                        for t in range(TILES):
                            keys = (t + 1) * P
                            S.activation(fox[:, t, i, 0:keys], ps[:, 2 + i, 0:keys], ACT.Identity,
                                         bias=cum[:, t, i:i + 1], scale=-1.0).then_inc(lessened, 1)

                def add_mask(on, eng, heads, masked):
                    for n, i in enumerate(heads):
                        eng.wait_ge(lessened, TILES * i + TILES)
                        for t in range(TILES):
                            x = fox[:, t, i, 0:(t + 1) * P]
                            on.tensor_tensor(x, x, masks["causal_mask"][:, t, 0:(t + 1) * P], ALU.add)\
                                .then_inc(masked, 1)
                    eng.wait_ge(masked, TILES * len(heads))

                @block.vector
                def _(dve):
                    dve.wait_ge(summed, 1)
                    V.tensor_copy(cum, ps[:, 0:2, 0:4]).then_inc(cum_done, 1)
                    add_mask(V, dve, range(0, FOX_HEADS, 2), dve_masked)

                @block.gpsimd
                def _(pool):
                    add_mask(G, pool, range(1, FOX_HEADS, 2), pool_masked)

            attend_stage(FOX_HEADS, HD, qT, fox_kT, lambda j, i: z[:, j, f0 + 512 + HD * i:f0 + 512 + HD * (i + 1)],
                         HD ** -0.5, lambda t, g, keys: fox[:, t, :, 0:keys],
                         lambda t, g: out8[:, t, 12:16, :], prob, probT, sync=small_loads.arrive)
            output_stage(plan[l]["out"], norm_pairs("ln1", a["ln1_g"][l], a["ln1_b"][l]), add_residual)
            norm_stage(1e-5, p1("ln1_g"), p1("ln1_b"), router=(router_w, N_EXPERTS))
            route_stage(score1, route1)
            experts_stage(plan[l]["experts"], h, norm_pairs("ln2", a["ln2_g"][l], a["ln2_b"][l]) +
                          (layer_pairs(l + 1) if l + 1 < DEPTH else second_pairs()), add_residual)
            norm_stage(1e-5, p1("ln2_g"), p1("ln2_b"), turned_to=hT if l + 1 < DEPTH else None)
        plan2 = plan[DEPTH]
        room = p2("room")
        z_n = TILES * IN2

        u_rows = region(6 * D, TILES, D)
        norm_stage(1e-6, p2("norm_g"), mod_in[:, 0], mod_in[:, 1], u_rows)
        z = region(0, TILES, IN2)
        lb, rest = region(z_n + 5120, 512), region(z_n + 5632, 512)
        bias_row = room[0:HEADS, 0:2 * SEQ]
        flat_bias = scratch["bias_rows"]
        with stage("row_made", "row_copied") as ((row_made, row_copied), block):
            @block.tensor
            def _(pe):
                T.matmul(ps[0:HEADS, 0, :], p2("rel")[0:BUCKETS], p2("buckets")[0:BUCKETS], start=True, stop=True)\
                    .then_inc(row_made, 1)

            @block.scalar
            def _(act):
                act.wait_ge(row_made, 1)
                S.activation(bias_row, ps[0:HEADS, 0, :], ACT.Copy).then_inc(row_copied, 1)

        def spread_rows(sp):
            small_loads.send(sp, [
                (flat_bias[0:HEADS * P * 2 * SEQ].rearrange("(h p n) -> h p n", h=HEADS, p=P),
                 bc(bias_row, (HEADS, P, 2 * SEQ), 1))])

        def lower_bound(link, act, asked, answered):
            if act is not None:
                act.wait_ge(asked, 1)
                S.activation(logits, logits, ACT.Exp).then_inc(answered, 1)
                return
            link(V.tensor_tensor(lb, logits[:, 0, :], logits[:, 1, :], ALU.max))
            V.tensor_tensor(logits, logits, bc(lb, (P, 2, 512), 1), ALU.subtract).then_inc(asked, 1)
            link.eng.wait_ge(answered, 1)
            link(V.tensor_tensor(rest, logits[:, 0, :], logits[:, 1, :], ALU.add))
            link(V.reciprocal(rest, rest))
            link(V.tensor_tensor(lb, logits[:, 0, :], rest, ALU.mult))
            link(V.tensor_scalar(rest, lb, -1.0, 1.0, ALU.mult, ALU.add))

        project_stage(hT, DC, [(u, 0, min(512, IN2 - 512 * i), lambda t, i=i: z[:, t, 512 * i:min(512 * i + 512, IN2)])
                               for i, u in enumerate(plan2["in"])], small_loads.arrive, spread_rows, prelude=lower_bound)

        k_rows = region(z_n, TILES, 512)
        recT = region(z_n + 2048, 2, REC_HEADS, SEQ)
        spread, q_spread = region(z_n, TILES, LEVELS, P), region(z_n + 4096, TILES, LEVELS, P)
        attnT = region(z_n + 6144, 3, P)
        names = ("dve_chain", "pool_chain", "asked", "answered", "pool_asked")
        with stage(*names) as ((dve_chain, pool_chain, asked, answered, pool_asked), block):
            @block.scalar
            def _(act):
                for t in range(TILES):
                    S.activation(k_rows[:, t], z[:, t, 512:1024], ACT.Sigmoid).then_inc(answered, 1)
                S.activation(z[:, :, 0:512], z[:, :, 0:512], ACT.Silu).then_inc(answered, 1)
                for t in range(TILES):
                    act.wait_ge((asked, pool_asked)[t], 2)
                    S.activation(z[:, t, 512:1024], z[:, t, 512:1024], ACT.Ln).then_inc(answered, 1)

            def forget_gates(on, eng, link, t, asked):
                eng.wait_ge(answered, t + 1)
                link(on.tensor_tensor(k_rows[:, t], k_rows[:, t], rest, ALU.mult))
                on.tensor_tensor(z[:, t, 512:1024], k_rows[:, t], lb, ALU.add).then_inc(asked, 1)
                eng.wait_ge(asked, 1)
                on.tensor_scalar(k_rows[:, t], z[:, t, 512:1024], -1.0, 1.0, ALU.mult, ALU.add).then_inc(asked, 1)
                eng.wait_ge(asked, 2)

            @block.vector
            def _(dve):
                forget_gates(V, dve, Chain(dve, dve_chain), 0, asked)

            @block.gpsimd
            def _(pool):
                forget_gates(G, pool, Chain(pool, pool_chain), 1, pool_asked)

        turn_stage(lambda t, i: (z if i < REC_HEADS else k_rows)[:, t, i % REC_HEADS * P:(i % REC_HEADS + 1) * P],
                   2 * REC_HEADS, P, region(z_n + 2048, 2 * REC_HEADS, SEQ))
        spans, last_span, level_mask = (table(x) for x in ("spans", "last_span", "level_mask"))
        names = ("spanned", "grown", "spread_done", "paired", "crossed", "masked", "chain", "summed", "copied_out")
        with stage(*names) as ((spanned, grown, spread_done, paired, crossed, masked, chain, summed, copied_out), block):
            @block.tensor
            def _(pe):
                def exponents(i, t):
                    if (i, t) != (0, 0):
                        pe.wait_ge(grown, TILES * i + t)
                    lf = z[:, t, 512 + i * P:512 + (i + 1) * P]
                    T.matmul(ps[:, 0, :], lf, spans[:, 0:512], start=True, stop=True)
                    if t == 0:
                        last = T.matmul(ps[:, 1, :], lf, spans[:, 512:1024], start=True, stop=True)
                    else:
                        T.matmul(ps[:, 1, 0:384], lf, spans[:, 512:896], start=True, stop=True)
                        last = T.matmul(ps[:, 1, 384:512], lf, last_span, start=True, stop=True)
                    last.then_inc(spanned, 1)

                def pairs(i, t):
                    pe.wait_ge(spread_done, 4 * i + 2 * t + 2)
                    if i:
                        pe.wait_ge(masked, 3 * i - (2, 0)[t])
                    for l in range(LEVELS - 1):
                        T.matmul(ps[:, 4 + 2 * t + l // 4, (l % 4) * P:(l % 4 + 1) * P], spread[:, t, l, :],
                                 q_spread[:, t, l, :], start=True, stop=True)
                    tok = slice(t * P, (t + 1) * P)
                    T.matmul(ps[:, 5 + 2 * t, 3 * P:], recT[:, 1, i, tok], recT[:, 0, i, tok], start=True, stop=True)\
                        .then_inc(paired, 1)

                def result(i):
                    pe.wait_ge(masked, 3 * i + 3)
                    if i:
                        pe.wait_ge(copied_out, i)
                    v = [z[:, t, 1024 + i * P:1024 + (i + 1) * P] for t in range(TILES)]
                    T.matmul(ps[:, 3, 0:P], attnT[:, 0, :], v[0], start=True, stop=True)
                    T.matmul(ps[:, 3, P:2 * P], attnT[:, 2, :], v[0], start=True, stop=False)
                    T.matmul(ps[:, 3, P:2 * P], attnT[:, 1, :], v[1], start=False, stop=True).then_inc(summed, 1)

                exponents(0, 0)
                exponents(0, 1)
                for i in range(REC_HEADS):
                    if i + 1 < REC_HEADS:
                        exponents(i + 1, 0)
                    pairs(i, 0)
                    if i:
                        result(i - 1)
                    pe.wait_ge(spread_done, 4 * i + 4)
                    T.matmul(ps[:, 2, 0:P], spread[:, 0, LEVELS - 1, :], q_spread[:, 1, LEVELS - 1, :],
                             start=True, stop=True).then_inc(crossed, 1)
                    pairs(i, 1)
                    if i + 1 < REC_HEADS:
                        exponents(i + 1, 1)
                result(REC_HEADS - 1)

            @block.scalar
            def _(act):
                def grow(i, t):
                    act.wait_ge(spanned, TILES * i + t + 1)
                    if i:
                        act.wait_ge((crossed, paired)[t], (i, TILES * i)[t])
                    S.activation(spread[:, t, :, :].rearrange("p l x -> p (l x)"),
                                 ps[:, 0:2, :].rearrange("p b n -> p (b n)"), ACT.Exp).then_inc(grown, 1)

                def copy_out(i):
                    act.wait_ge(summed, i + 1)
                    S.activation(mixed[:, :, i * P:(i + 1) * P], ps[:, 3, 0:2 * P]
                                 .rearrange("p (t v) -> p t v", t=TILES), ACT.Copy).then_inc(copied_out, 1)

                grow(0, 0)
                grow(0, 1)
                for i in range(REC_HEADS):
                    if i:
                        copy_out(i - 1)
                    if i + 1 < REC_HEADS:
                        grow(i + 1, 0)
                        grow(i + 1, 1)
                S.activation(z[:, :, 1536:2048], z[:, :, 1536:2048], ACT.Silu)
                copy_out(REC_HEADS - 1)

            @block.vector
            def _(dve):
                link = Chain(dve, chain)

                def spread_out(i, t):
                    tok = slice(t * P, (t + 1) * P)
                    dve.wait_ge(grown, TILES * i + t + 1)
                    V.tensor_tensor(q_spread[:, t], spread[:, t], bc(recT[:, 0, i, tok], (P, LEVELS, P), 1), ALU.mult)\
                        .then_inc(spread_done, 1)
                    dve.wait_ge(spread_done, 4 * i + 2 * t + 1)
                    V.tensor_tensor(spread[:, t], spread[:, t], bc(recT[:, 1, i, tok], (P, LEVELS, P), 1), ALU.mult)\
                        .then_inc(spread_done, 1)

                def pick(i, t):
                    dve.wait_ge(paired, TILES * i + t + 1)
                    picked = room[:, 0:LEVELS * P]
                    link(V.tensor_tensor(picked, ps[:, 4 + 2 * t:6 + 2 * t, :].rearrange("p b n -> p (b n)"),
                                         level_mask, ALU.mult))
                    if i and t == 0:
                        dve.wait_ge(summed, i)
                    V.tensor_reduce(attnT[:, t, :], picked.rearrange("p (l x) -> p x l", l=LEVELS), AX, ALU.add)\
                        .then_inc(masked, 1)
                    dve.wait_ge(masked, 3 * i + 2 * t + 1)

                spread_out(0, 0)
                for i in range(REC_HEADS):
                    spread_out(i, 1)
                    pick(i, 0)
                    dve.wait_ge(crossed, i + 1)
                    V.tensor_copy(attnT[:, 2, :], ps[:, 2, 0:P]).then_inc(masked, 1)
                    if i + 1 < REC_HEADS:
                        spread_out(i + 1, 0)
                    pick(i, 1)

        rec = mixed[:, :, 0:512].rearrange("p t (h v) -> p t h v", v=REC_D)
        rec_gain = p2("rec_g").rearrange("p (h v) -> p h v", v=REC_D)
        rms_stage([(rec[:, t], rec[:, t], 1e-6,
                    [rec_gain, z[:, t, 1536:2048].rearrange("p (h v) -> p h v", v=REC_D)]) for t in range(TILES)] +
                  [(z[:, t, o:o + 512].rearrange("p (h d) -> p h d", d=HD),
                    z[:, t, o:o + 512].rearrange("p (h d) -> p h d", d=HD), 1e-6, [bc(p2(g), (P, HEADS, HD), 1)])
                   for t in range(TILES) for o, g in ((2048, "q_g"), (2560, "k_g"))], region(z_n, 3072))

        work = p2("work").rearrange("p (t k) -> p t k", t=TILES)
        iqT, ikT = region(z_n + 4096, HEADS, SEQ), region(z_n + 6144, 1, SEQ)
        askew = []
        for t in range(TILES):
            for i in range(HEADS):
                at = i * P * 2 * SEQ + SEQ - 1 - P * t
                askew.append((z[:, t, i * SEQ:(i + 1) * SEQ],
                              flat_bias[at:at + P * (2 * SEQ - 1)].rearrange("(p n) -> p n", n=2 * SEQ - 1)[:, 0:SEQ]))

        with stage("chain", "moment", "rooted") as ((chain, moment, rooted), block):
            @block.sync
            def _(sp):
                small_loads.send(sp, askew)

            @block.vector
            def _(dve):
                both = Alternate(dve, chain)
                x = lambda t: z[:, t, 4096:4160]
                both(lambda t: V.bn_stats(small[:, 8 * t:8 * t + 6], x(t)))
                both(lambda t: V.bn_aggr(small[:, 16 + 2 * t:18 + 2 * t], small[:, 8 * t:8 * t + 6]))
                both.settle()
                V.tensor_scalar(small[:, 20:22], small[:, 17:20:2], 1e-6, None, ALU.add).then_inc(moment, 1)
                both(lambda t: V.tensor_scalar(z[:, t, 4160:4168], z[:, t, 4160:4168], HD ** -0.5 * HEADS ** -0.5,
                                               None, ALU.mult))
                dve.wait_ge(rooted, 1)
                both(lambda t: V.reciprocal(small[:, 24 + t:25 + t], small[:, 22 + t:23 + t]))
                both(lambda t: V.tensor_scalar(x(t), x(t), small[:, 16 + 2 * t:17 + 2 * t], small[:, 24 + t:25 + t],
                                               ALU.subtract, ALU.mult))
                both(lambda t: V.tensor_tensor(x(t), x(t), p2("idx_g"), ALU.mult))
                both(lambda t: V.tensor_tensor(x(t), x(t), p2("idx_b"), ALU.add))

            @block.scalar
            def _(act):
                act.wait_ge(moment, 1)
                S.activation(small[:, 22:24], small[:, 20:22], ACT.Sqrt).then_inc(rooted, 1)
        turn_stage(lambda t, i: z[:, t, 3584 + HD * i:3584 + HD * (i + 1)], HEADS + 1, HD,
                   region(z_n + 4096, HEADS + 1, SEQ))
        qT, kT, prob = (region(z_n + 2048 * i, HEADS, SEQ) for i in range(3))
        probT = room.rearrange("p (j q) -> p j q", q=P)
        with stage("scored", "chain", "turned", "turn_copied") as ((scored, chain, turned, turn_copied), block):
            @block.tensor
            def _(pe):
                for t in range(TILES):
                    keys = (t + 1) * P
                    for i in range(HEADS):
                        at = (i % 2) * SEQ
                        last = T.matmul(ps[:, 4 * t + i // 2, at:at + keys], iqT[0:HD, i, t * P:(t + 1) * P],
                                        ikT[0:HD, 0, 0:keys], start=True, stop=True)
                    last.then_inc(scored, 1)
                pe.wait_ge(chain, 1)
                for b in range(HEADS):
                    if b >= 4:
                        pe.wait_ge(turn_copied, b - 3)
                    for i in range(2 * b, 2 * b + 2):
                        for t in range(TILES):
                            at = (i % 2) * SEQ + t * P
                            last = T.transpose(ps[0:HD, b % 4, at:at + P],
                                               z[:, t, 2048 + HD * i:2048 + HD * (i + 1)], ident)
                    last.then_inc(turned, 1)

            @block.scalar
            def _(act):
                for b in range(HEADS):
                    act.wait_ge(turned, b + 1)
                    S.activation((qT, kT)[b // 4][0:HD, 2 * (b % 4):2 * (b % 4) + 2, :], ps[0:HD, b % 4, :]
                                 .rearrange("p (i t) -> p i t", i=2), ACT.Copy).then_inc(turn_copied, 1)

            @block.vector
            def _(dve):
                link = Chain(dve, chain)
                best = small[:, 0:8]
                for t in range(TILES):
                    keys = (t + 1) * P
                    weighed = room.rearrange("p (h k) -> p h k", k=SEQ)[:, :, 0:keys]
                    index_score = work[:, t, 0:keys]
                    dve.wait_ge(scored, t + 1)
                    link(V.scalar_tensor_tensor(weighed, ps[:, 4 * t:4 * t + 4, :]
                                                .rearrange("p b (j k) -> p (b j) k", j=2)[:, :, 0:keys], 0.0,
                                                bc(z[:, t, 4160:4168], (P, HEADS, keys), 2), ALU.max, ALU.mult))
                    link(V.tensor_reduce(index_score, weighed.rearrange("p h k -> p k h"), AX, ALU.add))
                    link(V.tensor_tensor(index_score, index_score, masks["chunk_mask"][:, t, 0:keys], ALU.add))
                    for _ in range(TOPK // 8):
                        link(V.max(best, index_score))
                        link(V.match_replace(index_score, best, index_score, -3e38))
                    link(V.tensor_scalar(index_score, index_score, -2e38, NEG, ALU.is_gt, ALU.mult))
                    small_loads.arrive(dve)
                    bias = z[:, t, 0:HEADS * SEQ].rearrange("p (h k) -> p h k", k=SEQ)[:, :, 0:keys]
                    link(V.tensor_tensor(bias, bias, bc(index_score, (P, HEADS, keys), 1), ALU.add))
        attend_stage(HEADS, HD, qT, kT, lambda j, i: z[:, j, 3072 + HD * i:3072 + HD * (i + 1)], HD ** -0.5,
                     lambda t, g, keys: z[:, t, 0:HEADS * SEQ].rearrange("p (h k) -> p h k", k=SEQ)
                     [:, 4 * g:4 * g + 4, 0:keys],
                     lambda t, g: out8[:, t, 8 + 4 * g:12 + 4 * g, :], prob, probT)
        rms_stage([(out8[:, t, 8:16, :], out8[:, t, 8:16, :], 1e-6,
                    [p2("att_g").rearrange("p (h d) -> p h d", d=HD)]) for t in range(TILES)], region(z_n, 2048))
        norm_g, shift, scale = (region((4 + i) * D, D) for i in range(3))
        rw = region(10 * D, DC, 20)
        output_stage(plan2["out"], [
            (p2("gate"), kept_mod(2)), (norm_g, every(a["norm2_g_2"][0], D)), (shift, kept_mod(3)),
            (scale, kept_mod(4)), (rw[:, :, 0:4], a["w_rg_2"][0].rearrange("(c p) e -> p c e", p=P)),
            (rw[:, :, 4:20], a["w_re_2"][0].rearrange("(c p) e -> p c e", p=P))], add_gated)

        moe_rows = region(8 * D, TILES, D)
        norm_stage(1e-6, norm_g, shift, scale, moe_rows, router=(rw, 20))
        route_stage(score2, route2)
        experts_stage(plan2["experts"], moe_rows, [(p2("gate"), kept_mod(5))], add_gated)
        store_stage()


def kernel(**inputs):
    import numpy as _np
    import concourse.bacc as _bacc
    from concourse import mybir as _mybir
    from concourse.bass_utils import run_bass_kernel_spmd as _run

    nc = _bacc.Bacc("TRN2", target_bir_lowering=False, num_devices=1)
    arrays, aps = {}, {}
    given = dict(inputs)
    given["tab"] = tables()
    given["bucket"] = bucket_table()
    for name, value in given.items():
        value = _np.ascontiguousarray(value)
        arrays[f"in_{name}"] = value
        aps[name] = nc.dram_tensor(f"in_{name}", value.shape, _mybir.dt.from_np(value.dtype),
                                   kind="ExternalInput").ap()
    out = nc.dram_tensor("out_0", (SEQ, D), F32, kind="ExternalOutput").ap()
    scratch = {n: nc.dram_tensor(f"scratch_{n}", s, F32, kind="Internal").ap() for n, s in SCRATCH.items()}
    build(nc, aps, scratch, [out])
    r = _run(nc, [arrays], core_ids=[0])
    return r.results[0]["out_0"].reshape(1, SEQ, D)
```
